# Optimizing a Trainium2 kernel written in Bass

```python
import math
import jax, jax.numpy as jnp
from jax import lax
import numpy as np
import jax
import jax.numpy as jnp

D_MODEL = 1024
BATCH = 1
SEQ = 512
DEPTH = 2

GRID_W = 64
CTX_LEN = 256
N_MIXERS = 2
NORM_EPS = 1e-6

MLA_HEADS = 8
QK_NOPE = 128
QK_ROPE = 64
V_DIM = 128
Q_LORA = 256
KV_LORA = 128
MLA_WIDTH = MLA_HEADS * V_DIM
MLA_IN_WIDTH = Q_LORA + KV_LORA + QK_ROPE + MLA_WIDTH
ROPE_AXIS_DIM = QK_ROPE // 2
ROPE_THETA = 10000.0
Q_BLOCK = 128

FOURIER_WIDTH = D_MODEL
FOURIER_GROUPS = 8
FOURIER_GROUP_DIM = FOURIER_WIDTH // FOURIER_GROUPS

N_MLA_LAYERS = (DEPTH + 1) // 2
N_FOURIER_LAYERS = DEPTH // 2
ADA_STD = 0.5 * D_MODEL ** -0.5


def rms_norm(x, g):
    xf = x.astype(jnp.float32)
    y = xf * lax.rsqrt(jnp.mean(xf * xf, axis=-1, keepdims=True) + NORM_EPS)
    return (y * g.astype(jnp.float32)).astype(x.dtype)

def axial_rope_tables(row, col):
    inv_freq = 1.0 / (ROPE_THETA ** (jnp.arange(0, ROPE_AXIS_DIM, 2, dtype=jnp.float32) / ROPE_AXIS_DIM))
    ang_r = row.astype(jnp.float32)[:, None] * inv_freq[None, :]
    ang_c = col.astype(jnp.float32)[:, None] * inv_freq[None, :]
    return jnp.cos(ang_r), jnp.sin(ang_r), jnp.cos(ang_c), jnp.sin(ang_c)

def _rotate(t, cos, sin):
    t1, t2 = jnp.split(t, 2, axis=-1)
    return jnp.concatenate([t1 * cos - t2 * sin, t2 * cos + t1 * sin], axis=-1)

def apply_axial_rope(t, tables):
    cos_r, sin_r, cos_c, sin_c = [a.astype(t.dtype)[None, :, None, :] for a in tables]
    t_r, t_c = jnp.split(t, 2, axis=-1)
    return jnp.concatenate([_rotate(t_r, cos_r, sin_r), _rotate(t_c, cos_c, sin_c)], axis=-1)

def mla_query(c_q, g_qa, w_qup):
    b, t, _ = c_q.shape
    q = (rms_norm(c_q, g_qa) @ w_qup).reshape(b, t, MLA_HEADS, QK_NOPE + QK_ROPE)
    return q[..., :QK_NOPE], q[..., QK_NOPE:]

def mla_keyvalue(c_kv, g_kva, w_kvup):
    b, t, _ = c_kv.shape
    kv = (rms_norm(c_kv, g_kva) @ w_kvup).reshape(b, t, MLA_HEADS, QK_NOPE + V_DIM)
    return kv[..., :QK_NOPE], kv[..., QK_NOPE:]

def assemble_keys(k_nope, k_pe):
    return jnp.concatenate([k_nope, jnp.broadcast_to(k_pe, k_nope.shape[:-1] + (QK_ROPE,))], axis=-1)

def dense_attention(q, k, v):
    scale = 1.0 / math.sqrt(QK_NOPE + QK_ROPE)
    s = jnp.einsum('bqhd,bkhd->bhqk', q, k).astype(jnp.float32) * scale
    p = jax.nn.softmax(s, axis=-1).astype(v.dtype)
    return jnp.einsum('bhqk,bkhd->bqhd', p, v)

def latent_attention(q, k_lat, v_lat, k_ctx, v_ctx):
    b, t, h, dk = q.shape
    k_all = jnp.concatenate([k_ctx, k_lat], axis=1)
    v_all = jnp.concatenate([v_ctx, v_lat], axis=1)
    nb = t // Q_BLOCK
    qb = q.reshape(b, nb, Q_BLOCK, h, dk).transpose(1, 0, 2, 3, 4)
    o = lax.map(lambda qblk: dense_attention(qblk, k_all, v_all), qb)
    return o.transpose(1, 0, 2, 3, 4).reshape(b, t, h * V_DIM)

def fourier_mix(u, w_in, w_out):
    proj = u @ w_in
    z, gate = proj[..., :FOURIER_WIDTH], proj[..., FOURIER_WIDTH:]
    b, t, _ = z.shape
    zg = z.reshape(b, t, FOURIER_GROUPS, FOURIER_GROUP_DIM).astype(jnp.float32)
    y = jnp.fft.fftn(zg, axes=(1, 3), norm="ortho").real.astype(u.dtype).reshape(b, t, FOURIER_WIDTH)
    return (y * jax.nn.silu(gate)) @ w_out

def ada_params(cond_act, w, b):
    mod = cond_act @ w + b
    return jnp.split(mod, 3, axis=-1)

def first_inputs(seed: int = 0) -> dict:
    key = jax.random.key(seed)
    ks = jax.random.split(key, 16)
    n = jax.random.normal
    f32 = jnp.float32
    return {
        "x": n(ks[0], (BATCH, SEQ, D_MODEL), f32),
        "c": n(ks[1], (BATCH, D_MODEL), f32),
        "ctx": n(ks[2], (BATCH, CTX_LEN, D_MODEL), f32),
        "c_ctx": n(ks[3], (D_MODEL,), f32),
        "norm_g": 1.0 + 0.02 * n(ks[4], (DEPTH, D_MODEL), f32),
        "w_ada": ADA_STD * n(ks[5], (DEPTH, D_MODEL, 3 * D_MODEL), f32),
        "b_ada": 0.02 * n(ks[6], (DEPTH, 3 * D_MODEL), f32),
        "mla_w_in": D_MODEL ** -0.5 * n(ks[7], (N_MLA_LAYERS, D_MODEL, MLA_IN_WIDTH), f32),
        "mla_g_qa": 1.0 + 0.02 * n(ks[8], (N_MLA_LAYERS, Q_LORA), f32),
        "mla_w_qup": Q_LORA ** -0.5 * n(ks[9], (N_MLA_LAYERS, Q_LORA, MLA_HEADS * (QK_NOPE + QK_ROPE)), f32),
        "mla_g_kva": 1.0 + 0.02 * n(ks[10], (N_MLA_LAYERS, KV_LORA), f32),
        "mla_w_kvup": KV_LORA ** -0.5 * n(ks[11], (N_MLA_LAYERS, KV_LORA, MLA_HEADS * (QK_NOPE + V_DIM)), f32),
        "mla_w_out": MLA_WIDTH ** -0.5 * n(ks[12], (N_MLA_LAYERS, MLA_WIDTH, D_MODEL), f32),
        "fno_w_in": D_MODEL ** -0.5 * n(ks[13], (N_FOURIER_LAYERS, D_MODEL, 2 * FOURIER_WIDTH), f32),
        "fno_w_out": FOURIER_WIDTH ** -0.5 * n(ks[14], (N_FOURIER_LAYERS, FOURIER_WIDTH, D_MODEL), f32),
        "final_g": 1.0 + 0.02 * n(ks[15], (D_MODEL,), f32),
    }

def first_block(x, c, ctx, c_ctx, norm_g, w_ada, b_ada, mla_w_in, mla_g_qa, mla_w_qup, mla_g_kva,
              mla_w_kvup, mla_w_out, fno_w_in, fno_w_out, final_g):
    n_tok = x.shape[1]
    rows = n_tok // GRID_W
    row = jnp.repeat(jnp.arange(rows, dtype=jnp.int32), GRID_W)
    col = jnp.tile(jnp.arange(GRID_W, dtype=jnp.int32), rows)
    rope = axial_rope_tables(row, col)

    act_lat = jax.nn.silu(c)
    act_ctx = jax.nn.silu(c_ctx)
    h_lat, h_ctx = x, ctx
    kv_lo, kv_hi = Q_LORA, Q_LORA + KV_LORA
    pe_hi = kv_hi + QK_ROPE

    for i in range(DEPTH):
        mixer = i % N_MIXERS
        idx = i // N_MIXERS
        ctx_later = any(j % N_MIXERS == 0 for j in range(i + 1, DEPTH))

        sh_l, sc_l, gt_l = ada_params(act_lat, w_ada[i], b_ada[i])
        u_lat = rms_norm(h_lat, norm_g[i]) * (1.0 + sc_l[:, None, :]) + sh_l[:, None, :]
        sh_c, sc_c, gt_c = ada_params(act_ctx, w_ada[i], b_ada[i])

        if mixer == 0:
            w_in = mla_w_in[idx]
            u_ctx = rms_norm(h_ctx, norm_g[i]) * (1.0 + sc_c) + sh_c
            p_lat = u_lat @ w_in
            qn_l, qp_l = mla_query(p_lat[..., :kv_lo], mla_g_qa[idx], mla_w_qup[idx])
            kn_l, v_l = mla_keyvalue(p_lat[..., kv_lo:kv_hi], mla_g_kva[idx], mla_w_kvup[idx])
            kp_l = apply_axial_rope(p_lat[..., None, kv_hi:pe_hi], rope)
            q_l = jnp.concatenate([qn_l, apply_axial_rope(qp_l, rope)], axis=-1)
            k_l = assemble_keys(kn_l, kp_l)
            if ctx_later:
                p_ctx = u_ctx @ w_in
            else:
                p_ctx = u_ctx @ w_in[:, kv_lo:pe_hi]
                p_ctx = jnp.concatenate([jnp.zeros(p_ctx.shape[:-1] + (kv_lo,), p_ctx.dtype), p_ctx], axis=-1) if False else p_ctx
            off = 0 if not ctx_later else kv_lo
            kn_c, v_c = mla_keyvalue(p_ctx[..., off:off + KV_LORA], mla_g_kva[idx], mla_w_kvup[idx])
            k_c = assemble_keys(kn_c, p_ctx[..., None, off + KV_LORA:off + KV_LORA + QK_ROPE])

            o_lat = latent_attention(q_l, k_l, v_l, k_c, v_c)
            y_lat = (o_lat * jax.nn.silu(p_lat[..., pe_hi:])) @ mla_w_out[idx]
            if ctx_later:
                qn_c, qp_c = mla_query(p_ctx[..., :kv_lo], mla_g_qa[idx], mla_w_qup[idx])
                q_c = jnp.concatenate([qn_c, qp_c], axis=-1)
                b_, t_c = h_ctx.shape[0], h_ctx.shape[1]
                o_ctx = dense_attention(q_c, k_c, v_c).reshape(b_, t_c, MLA_WIDTH)
                y_ctx = (o_ctx * jax.nn.silu(p_ctx[..., pe_hi:])) @ mla_w_out[idx]
                h_ctx = h_ctx + gt_c * y_ctx
            h_lat = h_lat + gt_l[:, None, :] * y_lat
        else:
            y_lat = fourier_mix(u_lat, fno_w_in[idx], fno_w_out[idx])
            if ctx_later:
                u_ctx = rms_norm(h_ctx, norm_g[i]) * (1.0 + sc_c) + sh_c
                h_ctx = h_ctx + gt_c * fourier_mix(u_ctx, fno_w_in[idx], fno_w_out[idx])
            h_lat = h_lat + gt_l[:, None, :] * y_lat

    return rms_norm(h_lat, final_g)


DEPTH_2 = 1

MOBA_HEADS = 8
MOBA_HEAD_DIM = 64
MOBA_BLOCK = 256
MOBA_TOPK = 3
MOBA_Q_CHUNK = 32
GLA_HEADS = 4
GLA_DK = D_MODEL // 2 // GLA_HEADS
GLA_DV = D_MODEL // GLA_HEADS
GLA_GATE_RANK = 16
GLA_GATE_TAU = 16.0
GLA_CHUNK = 64
T5_BUCKETS = 32
T5_MAX_DIST = 128
D_FF = 4 * D_MODEL
EPS = 1e-6

MOBA_WIDTH = MOBA_HEADS * MOBA_HEAD_DIM
GLA_K_WIDTH = GLA_HEADS * GLA_DK
GLA_V_WIDTH = GLA_HEADS * GLA_DV
IN_SPLIT_SIZES = (MOBA_WIDTH, MOBA_WIDTH, MOBA_WIDTH,
                  GLA_K_WIDTH, GLA_K_WIDTH, GLA_V_WIDTH, GLA_GATE_RANK, GLA_V_WIDTH,
                  D_MODEL, D_MODEL)
IN_SPLIT_POINTS = tuple(sum(IN_SPLIT_SIZES[:i + 1]) for i in range(len(IN_SPLIT_SIZES) - 1))
D_IN = sum(IN_SPLIT_SIZES)


def rms_norm_2(x, gain):
    xf = x.astype(jnp.float32)
    y = xf * lax.rsqrt(jnp.mean(xf * xf, axis=-1, keepdims=True) + EPS) * gain.astype(jnp.float32)
    return y.astype(x.dtype)

def t5_bucket(dist):
    max_exact = T5_BUCKETS // 2
    d = jnp.maximum(dist, 0)
    large = max_exact + (jnp.log(jnp.maximum(d, 1).astype(jnp.float32) / max_exact)
                         / math.log(T5_MAX_DIST / max_exact)
                         * (T5_BUCKETS - max_exact)).astype(jnp.int32)
    large = jnp.minimum(large, T5_BUCKETS - 1)
    return jnp.where(d < max_exact, d, large)

def moba_attention(q, k, v, t5_bias):
    B, S, H, Dh = q.shape
    q = q.transpose(0, 2, 1, 3)
    k = k.transpose(0, 2, 1, 3)
    v = v.transpose(0, 2, 1, 3)
    nb = -(-S // MOBA_BLOCK)
    s_pad = nb * MOBA_BLOCK
    pad = ((0, 0), (0, 0), (0, s_pad - S), (0, 0))
    kb = jnp.pad(k, pad).reshape(B, H, nb, MOBA_BLOCK, Dh)
    vb = jnp.pad(v, pad).reshape(B, H, nb, MOBA_BLOCK, Dh)
    scale = Dh ** -0.5
    q_block = jnp.arange(S) // MOBA_BLOCK
    n_sel = min(MOBA_TOPK, nb - 1)
    if n_sel > 0:
        k_mean = kb.astype(jnp.float32).mean(axis=3)
        gate = jnp.einsum("bhsd,bhnd->bhsn", q.astype(jnp.float32), k_mean)
        fully_past = jnp.arange(nb)[None, :] < q_block[:, None]
        gate = jnp.where(fully_past, gate, -jnp.inf)
        _, sel_idx = lax.top_k(gate, n_sel)
    else:
        sel_idx = jnp.zeros((B, H, S, 0), jnp.int32)
    n_chunks = S // MOBA_Q_CHUNK
    q_c = q.reshape(B, H, n_chunks, MOBA_Q_CHUNK, Dh).transpose(2, 0, 1, 3, 4)
    idx_c = sel_idx.reshape(B, H, n_chunks, MOBA_Q_CHUNK, n_sel).transpose(2, 0, 1, 3, 4)
    bias_hb = t5_bias.T
    b_ix = jnp.arange(B)[:, None, None, None]
    h_ix = jnp.arange(H)[None, :, None, None]
    h_ix5 = jnp.arange(H)[None, :, None, None, None]
    blk = jnp.arange(MOBA_BLOCK)

    def chunk_fn(args):
        ci, qc, ic = args
        c0 = ci * MOBA_Q_CHUNK
        t = c0 + jnp.arange(MOBA_Q_CHUNK)
        ob = c0 // MOBA_BLOCK
        k_own = lax.dynamic_index_in_dim(kb, ob, axis=2, keepdims=False)
        v_own = lax.dynamic_index_in_dim(vb, ob, axis=2, keepdims=False)
        d_own = t[:, None] - (ob * MOBA_BLOCK + blk)[None, :]
        l_own = jnp.einsum("bhqd,bhkd->bhqk", qc, k_own).astype(jnp.float32) * scale
        l_own = l_own + bias_hb[:, t5_bucket(d_own)].astype(jnp.float32)
        l_own = jnp.where(d_own >= 0, l_own, -jnp.inf)
        k_sel = kb[b_ix, h_ix, ic]
        v_sel = vb[b_ix, h_ix, ic]
        l_sel = jnp.einsum("bhqd,bhqjkd->bhqjk", qc, k_sel).astype(jnp.float32) * scale
        d_sel = t[None, None, :, None, None] - (ic[..., None] * MOBA_BLOCK + blk)
        l_sel = l_sel + bias_hb[h_ix5, t5_bucket(d_sel)].astype(jnp.float32)
        l_sel = jnp.where((ic < ob)[..., None], l_sel, -jnp.inf)
        l_sel = l_sel.reshape(B, H, MOBA_Q_CHUNK, n_sel * MOBA_BLOCK)
        p = jax.nn.softmax(jnp.concatenate([l_sel, l_own], axis=-1), axis=-1)
        p_sel = p[..., :n_sel * MOBA_BLOCK].astype(v.dtype)
        p_own = p[..., n_sel * MOBA_BLOCK:].astype(v.dtype)
        o = (jnp.einsum("bhqj,bhqjd->bhqd", p_sel,
                        v_sel.reshape(B, H, MOBA_Q_CHUNK, n_sel * MOBA_BLOCK, Dh))
             + jnp.einsum("bhqk,bhkd->bhqd", p_own, v_own))
        return o.astype(q.dtype)

    out = lax.map(chunk_fn, (jnp.arange(n_chunks, dtype=jnp.int32), q_c, idx_c))
    return out.transpose(1, 0, 3, 2, 4).reshape(B, S, H * Dh)

def gla_attention(q, k, v, log_a):
    B, S, H, dk = q.shape
    C = GLA_CHUNK
    nc = S // C

    def chunks(t):
        return t.astype(jnp.float32).reshape(B, nc, C, H, -1).transpose(1, 0, 3, 2, 4)

    qc = chunks(q) * dk ** -0.5
    kc = chunks(k)
    vc = chunks(v)
    b = jnp.cumsum(chunks(log_a), axis=3)
    b_last = b[..., -1:, :]
    q_dec = qc * jnp.exp(b)
    k_inv = kc * jnp.exp(-b)
    k_dec = kc * jnp.exp(b_last - b)
    causal = jnp.tril(jnp.ones((C, C), dtype=bool))
    attn = jnp.where(causal, jnp.einsum("nbhcd,nbhed->nbhce", q_dec, k_inv), 0.0)
    o_intra = jnp.einsum("nbhce,nbhev->nbhcv", attn, vc)

    def step(state, xs):
        qd, kd, vv, bl = xs
        o_inter = jnp.einsum("bhcd,bhdv->bhcv", qd, state)
        state = jnp.exp(bl)[:, :, 0, :, None] * state + jnp.einsum("bhcd,bhcv->bhdv", kd, vv)
        return state, o_inter

    state0 = jnp.zeros((B, H, dk, v.shape[-1]), jnp.float32)
    _, o_inter = lax.scan(step, state0, (q_dec, k_dec, vc, b_last))
    o = o_intra + o_inter
    return o.transpose(1, 0, 3, 2, 4).reshape(B, S, H, v.shape[-1])

def second_inputs(seed: int = 0) -> dict:
    key = jax.random.key(seed)
    ks = jax.random.split(key, 16)

    def nrm(k, shape, scale):
        return jax.random.normal(k, shape, jnp.float32) * scale

    return {
        "x": nrm(ks[0], (BATCH, SEQ, D_MODEL), 1.0),
        "norm1_g": 1.0 + nrm(ks[1], (DEPTH_2, D_MODEL), 0.05),
        "w_in": nrm(ks[2], (DEPTH_2, D_MODEL, D_IN), D_MODEL ** -0.5),
        "moba_q_norm_g": 1.0 + nrm(ks[3], (DEPTH_2, MOBA_HEAD_DIM), 0.05),
        "moba_k_norm_g": 1.0 + nrm(ks[4], (DEPTH_2, MOBA_HEAD_DIM), 0.05),
        "t5_bias": nrm(ks[5], (T5_BUCKETS, MOBA_HEADS), 0.5),
        "gla_gate_up": nrm(ks[6], (DEPTH_2, GLA_GATE_RANK, GLA_K_WIDTH), GLA_GATE_RANK ** -0.5),
        "gla_gate_bias": nrm(ks[7], (DEPTH_2, GLA_K_WIDTH), 0.1),
        "gla_out_norm_g": 1.0 + nrm(ks[8], (DEPTH_2, GLA_DV), 0.05),
        "w_branch_moba": nrm(ks[9], (DEPTH_2, MOBA_WIDTH, D_MODEL), MOBA_WIDTH ** -0.5),
        "w_branch_gla": nrm(ks[10], (DEPTH_2, GLA_V_WIDTH, D_MODEL), GLA_V_WIDTH ** -0.5),
        "w_out": nrm(ks[11], (DEPTH_2, D_MODEL, D_MODEL), D_MODEL ** -0.5),
        "norm2_g": 1.0 + nrm(ks[12], (DEPTH_2, D_MODEL), 0.05),
        "w_up": nrm(ks[13], (DEPTH_2, D_MODEL, D_FF), D_MODEL ** -0.5),
        "w_down": nrm(ks[14], (DEPTH_2, D_FF, D_MODEL), D_FF ** -0.5),
    }

def second_block(x, norm1_g, w_in, moba_q_norm_g, moba_k_norm_g, t5_bias, gla_gate_up,
              gla_gate_bias, gla_out_norm_g, w_branch_moba, w_branch_gla, w_out,
              norm2_g, w_up, w_down):
    B, S, _ = x.shape
    h = x
    for layer in range(DEPTH_2):
        n = rms_norm_2(h, norm1_g[layer])
        proj = n @ w_in[layer]
        (mq, mk, mv, gq, gk, gv, g_low, g_out, gate_moba, gate_gla) = jnp.split(
            proj, IN_SPLIT_POINTS, axis=-1)
        mq = rms_norm_2(mq.reshape(B, S, MOBA_HEADS, MOBA_HEAD_DIM), moba_q_norm_g[layer])
        mk = rms_norm_2(mk.reshape(B, S, MOBA_HEADS, MOBA_HEAD_DIM), moba_k_norm_g[layer])
        mv = mv.reshape(B, S, MOBA_HEADS, MOBA_HEAD_DIM)
        y_moba = moba_attention(mq, mk, mv, t5_bias)
        log_a = jax.nn.log_sigmoid(
            (g_low @ gla_gate_up[layer] + gla_gate_bias[layer]).astype(jnp.float32)) / GLA_GATE_TAU
        y_gla = gla_attention(gq.reshape(B, S, GLA_HEADS, GLA_DK),
                              gk.reshape(B, S, GLA_HEADS, GLA_DK),
                              gv.reshape(B, S, GLA_HEADS, GLA_DV),
                              log_a.reshape(B, S, GLA_HEADS, GLA_DK))
        y_gla = rms_norm_2(y_gla, gla_out_norm_g[layer]).astype(x.dtype)
        y_gla = (y_gla * jax.nn.silu(g_out.reshape(B, S, GLA_HEADS, GLA_DV))).reshape(B, S, GLA_V_WIDTH)
        mixed = (jax.nn.sigmoid(gate_moba) * (y_moba @ w_branch_moba[layer])
                 + jax.nn.sigmoid(gate_gla) * (y_gla @ w_branch_gla[layer]))
        h = h + mixed @ w_out[layer]
        n2 = rms_norm_2(h, norm2_g[layer])
        h = h + jnp.square(jax.nn.relu(n2 @ w_up[layer])) @ w_down[layer]
    return h


def setup_inputs(seed=0):
    out = dict(first_inputs(seed))
    for name, value in second_inputs(seed + 1).items():
        if name != "x":
            out[name + "_2"] = value
    return out


def reference(
    x, c, ctx, c_ctx, norm_g, w_ada, b_ada, mla_w_in, mla_g_qa, mla_w_qup, mla_g_kva,
    mla_w_kvup, mla_w_out, fno_w_in, fno_w_out, final_g, norm1_g_2, w_in_2, moba_q_norm_g_2,
    moba_k_norm_g_2, t5_bias_2, gla_gate_up_2, gla_gate_bias_2, gla_out_norm_g_2,
    w_branch_moba_2, w_branch_gla_2, w_out_2, norm2_g_2, w_up_2, w_down_2,
):
    x = first_block(
        x, c, ctx, c_ctx, norm_g, w_ada, b_ada, mla_w_in, mla_g_qa, mla_w_qup, mla_g_kva,
        mla_w_kvup, mla_w_out, fno_w_in, fno_w_out, final_g,
    )
    return second_block(
        x, norm1_g_2, w_in_2, moba_q_norm_g_2, moba_k_norm_g_2, t5_bias_2, gla_gate_up_2,
        gla_gate_bias_2, gla_out_norm_g_2, w_branch_moba_2, w_branch_gla_2, w_out_2, norm2_g_2,
        w_up_2, w_down_2,
    )


_drawn_inputs = setup_inputs


def setup_inputs(seed=0):
    import zlib

    import numpy as np

    out = dict(_drawn_inputs(seed))
    spreads = {}
    factors = {'ctx': 7.263,
     'norm_g': 8.0,
     'b_ada': 3.451,
     'mla_g_qa': 8.0,
     'mla_g_kva': 8.0,
     'moba_q_norm_g_2': 8.0,
     'moba_k_norm_g_2': 8.0,
     'gla_gate_bias_2': 4.037,
     'gla_out_norm_g_2': 3.493,
     't5_bias_2': 3.232}
    for name, (base, spread) in spreads.items():
        noise = np.random.default_rng([zlib.crc32(name.encode()), seed]).standard_normal(out[name].shape)
        drawn = base * np.exp(spread * noise) if base else spread * noise
        out[name] = jnp.asarray(drawn.astype(out[name].dtype))
    for name, factor in factors.items():
        out[name] = (out[name] * factor).astype(out[name].dtype)
    return out
```

```python
import math
from contextlib import ExitStack

import numpy as np

import concourse.bass as bass
from concourse import mybir

P = 128
T = 512
TC = 256
TK = T + TC
D = 1024
KC = D // P
TT = T // P
EPS = 1e-6
NEG = -1e30

HEADS = 8
NOPE = 128
ROPE = 64
QL = 256
KVL = 128
MLA_SCALE = 1.0 / math.sqrt(NOPE + ROPE)
GRID_W = 64
GROUP = 128
HALF = T // 2
MH = 8
MD = 64
BUCKETS = 32
MAX_DIST = 128
TOEP = T + P
GH = 4
DK = 128
DV = 256
RANK = 16
TAU = 16.0
CH = 64
NCH = T // CH

A0, G1, HD, MO, FG, FZ, FO, MV, MQ, GM, BM, GK, GO, GG, BG, WO, FF = (
    0, 4, 12, 20, 28, 36, 44, 52, 56, 64, 72, 76, 92, 100, 108, 116, 124)

VECS = [("c", 8), ("c_ctx", 8), ("norm_g", 16), ("b_ada", 48), ("final_g", 8), ("norm1", 8), ("norm2", 8),
        ("g_qa", 2), ("g_kva", 1), ("gate_bias", 4), ("out_norm", 2), ("q_norm", 1), ("k_norm", 1)]
ROW = {}
for _n, _r in VECS:
    ROW[_n] = sum(r for _, r in VECS[:len(ROW)])
NROWS = sum(r for _, r in VECS)


def shape_constants():
    out = {}
    out["identity"] = np.eye(P, dtype=np.float32)
    out["head_ones"] = np.kron(np.eye(2), np.ones((MD, MD))).astype(np.float32)
    e, c = np.meshgrid(np.arange(P), np.arange(P), indexing="ij")
    out["chunk_causal"] = ((e // CH == c // CH) & (e <= c)).astype(np.int32)
    axis_dim = ROPE // 2
    inv = (1.0 / (np.float32(10000.0) ** (np.arange(0, axis_dim, 2, dtype=np.float32) / np.float32(axis_dim)))).astype(np.float32)
    row = np.repeat(np.arange(T // GRID_W), GRID_W).astype(np.float32)
    col = np.tile(np.arange(GRID_W), T // GRID_W).astype(np.float32)
    cos, sin = [], []
    for pos in (row, col):
        ang = (pos[None, :] * inv[:, None]).astype(np.float32).astype(np.float64)
        cos += [np.cos(ang), np.cos(ang)]
        sin += [-np.sin(ang), np.sin(ang)]
    out["rope_cos"] = np.concatenate(cos).astype(np.float32)
    out["rope_sin"] = np.concatenate(sin).astype(np.float32)
    k = np.arange(GROUP)
    ang = 2 * np.pi * ((k[:, None] * k[None, :]) % GROUP) / GROUP
    norm = 1.0 / math.sqrt(T * GROUP)
    out["dft_dim"] = np.concatenate([np.cos(ang), -np.sin(ang)], 1).astype(np.float32) * np.float32(norm)
    t, s = np.arange(HALF)[:, None], np.arange(HALF)[None, :]
    mats = []
    for odd in (0, 1):
        ang = 2 * np.pi * ((t * (2 * s + odd)) % T) / T
        mats += [np.cos(ang), np.sin(ang)]
    out["dft_tok"] = np.stack(mats).astype(np.float32)
    d = T - 1 - np.arange(TOEP)
    exact = BUCKETS // 2
    large = exact + (np.log(np.maximum(d, 1).astype(np.float32) / np.float32(exact))
                     / np.float32(math.log(MAX_DIST / exact)) * np.float32(BUCKETS - exact)).astype(np.int32)
    bucket = np.where(d < exact, np.maximum(d, 0), np.minimum(large, BUCKETS - 1))
    out["bucket_hot"] = ((np.arange(BUCKETS)[:, None] == bucket[None, :]) & (d >= 0)).astype(np.float32)
    out["mask_row"] = np.tile(np.where(d >= 0, 0.0, NEG).astype(np.float32), (MH, 1))
    return out


class Steps:

    def __init__(self, sem):
        self.sem, self.base, self.k = sem, 0, 0
        self.i = None

    def loop(self, i, per):
        self.base, self.i, self.per, self.k = self.base + self.k, i, per, 0

    def leave(self, rounds):
        assert self.k == self.per, (self.k, self.per)
        self.base, self.i, self.k = self.base + rounds * self.per, None, 0

    def now(self):
        here = self.base + self.k
        return here if self.i is None else self.i * self.per + here


def build(nc, d):
    f32, f32r, i32 = mybir.dt.float32, mybir.dt.float32r, mybir.dt.int32
    ACT = mybir.ActivationFunctionType
    ALU = mybir.AluOpType
    AX = mybir.AxisListType.X

    ctx = ExitStack()
    with ctx:
        KB = 1024
        BASE = 16512

        def at(name, kb, shape, dt=f32):
            return nc.alloc_sbuf_tensor_at(name, shape, dt, offset=BASE + int(kb * KB))

        def sem(name):
            return ctx.enter_context(nc.semaphore(name))

        HT = at("residual", 0, [P, KC, T])
        UH = at("u_hi", 16, [P, KC, T], f32r)
        UL = at("u_lo", 32, [P, KC, T], f32r)
        RAW = at("w_raw", 48, [P, 2, KC * P])
        WH = at("w_hi", 56, [P, 4, KC * P], f32r)
        WL = at("w_lo", 72, [P, 4, KC * P], f32r)
        YH = at("y_hi", 88, [P, KC, T], f32r)
        YL = at("y_lo", 104, [P, KC, T], f32r)
        SG = at("gated", 120, [P, KC, T])
        MX = at("mixed", 136, [P, KC, T])
        IDENT = at("ident", 152, [P, P])
        HONES = at("head_ones_sb", 152.5, [P, P])
        ONES = at("ones", 153, [P, P])
        COLS = at("cols", 153.5, [P, P])
        ADAL = [at(f"ada_lat{n}", 154 + 0.125 * n, [P, 24]) for n in range(2)]
        ADAC = at("ada_ctx", 154.25, [P, 16])
        MULL = [at(f"mul_lat{n}", 154.375 + 0.0625 * n, [P, KC]) for n in range(2)]
        MULC = at("mul_ctx", 154.5, [P, KC])
        CACT = at("c_act", 154.5625, [P, KC, 2])
        RSC = at("row_rstd", 154.6875, [P, 8])
        NMAX = at("neg_max", 154.75, [P, 4])
        PSUM_ = at("prob_sum", 154.8125, [P, 4])
        EPST = at("eps", 154.875, [P, 1])
        QGAIN = at("q_gain", 154.90625, [P, 1])
        DUMMY = at("dummy", 154.9375, [P, 2])
        CMASK = at("causal_mask", 155, [P, P], i32)
        RS = at("rstd", 156, [P, T])
        ACC = at("sq_sum", 158, [P, T])
        SQ = at("squares", 160, [P, 2, T])
        E = at("stage", 164, [P, 2, T])

        UCH = at("uc_hi", 88, [P, KC, TC], f32r)
        UCL = at("uc_lo", 96, [P, KC, TC], f32r)
        AROW = at("ada_rows", 88, [2, 4, T])
        XTOK = at("x_tok", 104, [P, TT, D])
        AD = [at("ada_w0", 120, [P, KC, T]), at("ada_w1", 136, [P, KC, T])]
        AB = [at("ada_back0", 104, [P, KC, T]), at("ada_back1", 88, [P, KC, T])]
        VROWS = at("vec_rows", 168, [NROWS, P])
        JUNK = at("junk", 170, [P, D])
        CTOK = at("ctx_tok", 174, [P, TC // P, D])
        HOT = at("bucket_hot_sb", 184, [BUCKETS, TOEP])
        MROW = at("mask_row_sb", 187, [MH, TOEP])
        BROW = at("bias_row", 190, [MH, TOEP])
        T5 = at("t5", 193, [BUCKETS, MH])
        CQ = at("cq", 136, [P, 2, T])
        CK = at("ckv", 140, [P, TK])
        KP = at("kp", 143, [ROPE, TK])
        RQ = at("cq_rstd", 146, [P, T])
        RKV = at("ckv_rstd", 148, [P, TK])
        CQH, CQL = at("cq_hi", 168, [P, 2, T], f32r), at("cq_lo", 172, [P, 2, T], f32r)
        CKH, CKL = at("ckv_hi", 176, [P, TK], f32r), at("ckv_lo", 179, [P, TK], f32r)
        KPH, KPL = at("kp_hi", 182, [ROPE, TK], f32r), at("kp_lo", 185, [ROPE, TK], f32r)
        KNH = [at("kn_hi0", 188, [P, TK], f32r), at("kn_hi1", 204, [P, TK], f32r)]
        KNL = [at("kn_lo0", 191, [P, TK], f32r), at("kn_lo1", 162, [P, TK], f32r)]
        VAH, VAL = at("va_hi", 194, [P, TK // P, P], f32r), at("va_lo", 197, [P, TK // P, P], f32r)
        COS, SIN = at("cos", 200, [ROPE, T]), at("sin", 202, [ROPE, T])
        QPF = at("qp", 118, [ROPE, T])
        QNH, QNL = at("qn_hi", 136, [P, 2, T], f32r), at("qn_lo", 140, [P, 2, T], f32r)
        QPH, QPL = at("qp_hi", 144, [ROPE, 2, T], f32r), at("qp_lo", 148, [ROPE, 2, T], f32r)
        PTH, PTL = at("pt_hi", 88, [P, TK // P, T], f32r), at("pt_lo", 100, [P, TK // P, T], f32r)
        PA = at("probs", 112, [P, 2, TK])
        DFH, DFL = at("dft_tok_hi", 168, [P, 8, HALF], f32r), at("dft_tok_lo", 176, [P, 8, HALF], f32r)
        CDH, CDL = at("dft_dim_hi", 184, [P, 2 * GROUP], f32r), at("dft_dim_lo", 185, [P, 2 * GROUP], f32r)
        ZH, ZL = at("z_hi", 186, [P, 2, T], f32r), at("z_lo", 190, [P, 2, T], f32r)
        ZF = at("z_fold", 194, [P, 2, T])
        ZR = at("z_raw", 198, [P, 2, T])
        CDR = at("dft_dim_raw", 202, [P, 2 * GROUP])
        DFR = at("dft_tok_raw", 136, [P, 8, HALF])
        AH, AL = at("dim_dft_hi", 136, [P, 2, 4 * 2 * GROUP], f32r), at("dim_dft_lo", 144, [P, 2, 4 * 2 * GROUP], f32r)

        BIAS = at("toeplitz_bias", 120, [P, MH, T])
        VH, VL = at("mv_hi", 168, [P, TT, T], f32r), at("mv_lo", 176, [P, TT, T], f32r)
        QKH, QKL = at("mqk_hi", 184, [P, 4, T], f32r), at("mqk_lo", 192, [P, 4, T], f32r)
        MP = at("m_probs", 200, [P, 2, T])
        VSH, VSL = at("mv_pair_hi", 136, [P, 2, TT, P], f32r), at("mv_pair_lo", 140, [P, 2, TT, P], f32r)
        MTH, MTL = at("m_turned_hi", 96, [P, TT, T], f32r), at("m_turned_lo", 112, [P, TT, T], f32r)
        RQS = at("mqk_rstd", 156, [P, 2, T])
        LWR = at("low_raw", 176, [P, KC, P])
        LWH, LWL = at("low_hi", 180, [P, KC, P], f32r), at("low_lo", 184, [P, KC, P], f32r)
        GLO = at("g_low", 188, [RANK, T])
        GUP = at("gate_up", 190, [RANK, T])
        MN = at("log_decay", 192, [P, GH, T])
        RST = at("chunk_starts", 202, [P, T])
        BT = at("decay_sum", 96, [P, GH, T])
        GQK = at("gqk", 168, [P, 4, T])
        SALL = at("states", 176, [P, NCH - 1, DV])
        SH, SL = at("states_hi", 183, [P, NCH - 1, DV], f32r), at("states_lo", 190, [P, NCH - 1, DV], f32r)
        KDH, KDL = at("kdec_hi", 197, [P, TT, DK], f32r), at("kdec_lo", 199, [P, TT, DK], f32r)
        AMH, AML = at("attn_hi", 201, [P, T], f32r), at("attn_lo", 203, [P, T], f32r)
        AMF = at("attn", 205, [P, T])
        EB, EN = at("exp_decay", 156, [P, T]), at("exp_growth", 158, [P, T])
        GVH, GVL = at("gv_hi", 88, [P, TT, T], f32r), at("gv_lo", 104, [P, TT, T], f32r)
        QDH, QDL = at("qdec_hi", 112, [P, T], f32r), at("qdec_lo", 114, [P, T], f32r)
        KIH, KIL = at("kinv_hi", 116, [P, T], f32r), at("kinv_lo", 118, [P, T], f32r)

        PB = ctx.enter_context(nc.psum_tensor("psum", [P, 8 * T], f32))

        def bank(b, n=T, o=0):
            return PB[:, b * T + o:b * T + o + n]

        def kv_bank(c):
            return bank(4 + 2 * (c % 2) + c // 4, DV, (c // 2) % 2 * DV)

        def f(ap):
            return ap.bitcast(f32)

        raw_full = [sem(f"raw_full{s}") for s in range(2)]
        hi_done = sem("w_hi_done")
        lo_done = sem("w_lo_done")
        tile_done = sem("tile_done")
        s_vec = sem("vec_loaded")
        s_x = sem("x_loaded")
        s_ctx = sem("ctx_loaded")
        s_const = sem("const_loaded")
        s_rope = sem("rope_loaded")
        s_t5 = sem("t5_loaded")
        s_adaw = [sem("ada_loaded0"), sem("ada_loaded1")]
        ones_set = sem("ones_set")
        cols_t = sem("cols_transposed")
        cols_done = sem("cols_done")
        cact_done = sem("c_act_done")
        ada_mm = sem("ada_multiplied")
        ada_row, ada_t, ada_used = sem("ada_rows_copied"), sem("ada_turned"), sem("ada_used")
        x_t = sem("x_transposed")
        x_copied = sem("x_copied")
        row_ss = sem("row_sums")
        row_rstd = sem("row_rstd_done")
        x_scaled = sem("x_scaled")
        xn_t = sem("xn_transposed")
        u0_e, u0_hi, u0_lo = sem("u0_e"), sem("u0_hi"), sem("u0_lo")
        bias_mm = sem("bias_mm")
        bias_row = sem("bias_row_done")
        bias_out = sem("bias_stored")
        link_s = sem("vector_steps")
        a_raw = sem("a0_copied")
        a_sq = sem("a0_squares")
        a_ss = sem("a0_sums")
        a_sqrt = sem("a0_sqrt")
        a_n = sem("a0_normed")
        a_hi, a_lo = sem("a0_hi"), sem("a0_lo")
        sg1 = sem("gate1_done")
        kv_raw = sem("kv_up_loaded")
        un_mm, un_e, un_hi, un_lo = sem("unit_mm"), sem("unit_rope"), sem("unit_hi"), sem("unit_lo")
        s_mm, s_max, s_exp, s_scaled = sem("scores_mm"), sem("scores_max"), sem("scores_exp"), sem("probs_scaled")
        t_mm, t_hi, t_lo = sem("probs_turned"), sem("turned_hi"), sem("turned_lo")
        o_mm, o_e, o_hi, o_lo = sem("pv_mm"), sem("o_gated"), sem("o_hi"), sem("o_lo")

        norm = {k: sem(f"norm_{k}") for k in ("h", "sq", "acc", "ss", "sqrt", "rstd", "e", "hi", "lo")}

        def so_far(n, k):
            return {"h": KC, "sq": KC, "acc": KC + 2, "ss": 1, "sqrt": 1, "rstd": 1}[k] * n if k not in ("e", "hi", "lo") else KC * max(n - 1, 0)

        out_t = sem("out_transposed")
        out_c = sem("out_copied")
        out_s = sem("out_stored")
        s_dft = sem("dft_loaded")
        df_hi, df_lo = sem("dft_hi"), sem("dft_lo")
        z_raw, z_fold, z_hi, z_lo = sem("z_copied"), sem("z_folded"), sem("z_hi_done"), sem("z_lo_done")
        d_mm, d_hi, d_lo = sem("dim_dft_mm"), sem("dim_dft_hi_done"), sem("dim_dft_lo_done")
        f_mm, f_e, f_hi, f_lo = sem("tok_dft_mm"), sem("y_gated"), sem("y_hi_done"), sem("y_lo_done")

        s_bias = sem("bias_loaded")
        s_mask = sem("mask_loaded")
        v_hi, v_lo, vs_done = sem("mv_hi_done"), sem("mv_lo_done"), sem("mv_pair_done")
        q_sq, q_ss, q_rt = sem("mqk_squares"), sem("mqk_sums"), sem("mqk_sqrt")
        q_e, q_hi, q_lo = sem("mqk_normed"), sem("mqk_hi_done"), sem("mqk_lo_done")
        M0 = TT * HEADS
        gm_s, bm_e = sem("gate_moba"), sem("branch_moba")
        s_low = sem("low_loaded")
        l_hi, l_lo, l_mm, l_cp, l_up = sem("low_hi_done"), sem("low_lo_done"), sem("low_mm"), sem("low_copied"), sem("gate_up_mm")
        l_abs, l_min, l_ln, b_done = sem("gate_abs"), sem("gate_min"), sem("gate_log"), sem("decay_done")
        g_raw, gv_hi, gv_lo = sem("gqk_copied"), sem("gv_hi_done"), sem("gv_lo_done")
        g_ex, g_e, g_hi, g_lo = sem("exp_done"), sem("qk_decayed"), sem("qk_hi_done"), sem("qk_lo_done")
        kd_d, kd_x, kd_e, kd_t = sem("kdec_exponent"), sem("kdec_exp"), sem("kdec_done"), sem("kdec_turned")
        kd_hi, kd_lo = sem("kdec_hi_done"), sem("kdec_lo_done")
        at_mm, am_f, am_hi, am_lo = sem("attn_mm"), sem("attn_masked"), sem("attn_hi_done"), sem("attn_lo_done")
        kv_mm, st_f, st_hi, st_lo = sem("kv_mm"), sem("states_done"), sem("states_hi_done"), sem("states_lo_done")
        go_mm, go_sq, go_ss, go_rt, on_done = sem("gla_o_mm"), sem("gla_o_sq"), sem("gla_o_sums"), sem("gla_o_sqrt"), sem("gla_o_normed")
        y_s, y_e, y_hi, y_lo = sem("g_out_silu"), sem("g_out_gated"), sem("gy_hi_done"), sem("gy_lo_done")
        gg_s = sem("gate_gla")
        x_e, x_hi, x_lo = sem("mixed_e"), sem("mixed_hi"), sem("mixed_lo")
        f_r, f_sq, f_ylo, f_h = sem("relu_done"), sem("relu_sq_hi"), sem("relu_sq_lo"), sem("ff_added")

        toep = nc.dram_tensor("bias_scratch", (MH, P, TOEP), f32)
        OUT = at("out_rows", 16, [P, TT, D])

        block = ctx.enter_context(nc.Block())

        def raw_count(t0, i, j, per=4):
            return 16 * (t0 // 2 + j // 2 + 1) + (0 if i is None else 8 * per * i)

        def tile_no(t0, i, j, per=4):
            return t0 + j if i is None else per * i + (t0 + j)

        units = [(0, u) for u in range(4)]
        for j in range(4):
            units += [(j + 1, 0), (j, 4), (j, 5), (j + 1, 1), (j + 1, 2), (j + 1, 3)] if j < 3 else [(j, 4), (j, 5)]
        UPR = len(units)

        def unit_no(j, u):
            return units.index((j, u)) + 1

        def unit_mm_no(j, u):
            return sum(1 for x in units[:unit_no(j, u)] if x[1] < 5)

        @block.sync
        def _(sp):
            sp.dma_start(IDENT[:], d["identity"]).then_inc(s_const, 16)
            sp.dma_start(XTOK[:], d["x"].rearrange("(m p) n -> p m n", p=P)).then_inc(s_x, 16)
            sp.dma_start(HONES[:], d["head_ones"]).then_inc(s_const, 16)
            sp.dma_start(CMASK[:], d["chunk_causal"]).then_inc(s_mask, 16)
            for name, rows in VECS:
                src = d[name]
                if name in ("q_norm", "k_norm"):
                    for n in range(2):
                        sp.dma_start(VROWS[ROW[name]:ROW[name] + 1, n * MD:(n + 1) * MD], src).then_inc(s_vec, 16)
                else:
                    sp.dma_start(VROWS[ROW[name]:ROW[name] + rows, :], src).then_inc(s_vec, 16)
            sp.dma_start(CTOK[:], d["ctx"].rearrange("(m p) n -> p m n", p=P)).then_inc(s_ctx, 16)
            sp.dma_start(COS[:], d["rope_cos"]).then_inc(s_rope, 16)
            sp.dma_start(SIN[:], d["rope_sin"]).then_inc(s_rope, 16)
            sp.dma_start(T5[:], d["t5_bias_2"]).then_inc(s_t5, 16)
            sp.dma_start(HOT[:], d["bucket_hot"]).then_inc(s_t5, 16)
            sp.dma_start(MROW[:], d["mask_row"]).then_inc(s_t5, 16)

            def load_tile(t0, i, j, src, k, per=4):
                if t0 or j >= 2:
                    sp.wait_ge(lo_done, tile_no(t0 - 1, i, j, per))
                sp.dma_start(RAW[:, j % 2, :].rearrange("p (k n) -> p k n", k=k), src.rearrange("(k p) n -> p k n", p=P))\
                    .then_inc(raw_full[j % 2], 16)

            def load(t0, n, w, c0):
                if n == 1:
                    for j in range(4):
                        load_tile(t0, None, j, w[:, c0 + j * P:c0 + (j + 1) * P], KC)
                else:
                    with sp.Fori(0, n) as i:
                        for j in range(4):
                            load_tile(t0, i, j, w[:, bass.ds(4 * P * i + (c0 + j * P), P)], KC)

            def ada_weights(q):
                return d["w_ada"][q // 6, :, (q % 6) * T:(q % 6 + 1) * T].rearrange("(k p) n -> p k n", p=P)

            for q in range(4):
                if q >= 2:
                    sp.wait_ge(ada_mm, q - 1)
                sp.dma_start(AD[q % 2][:], ada_weights(q)).then_inc(s_adaw[q % 2], 16)
            load(A0, 1, d["mla_w_in"], 0)
            sp.wait_ge(bias_row, 1)
            sp.dma_start(toep.ap(), BROW[:].unsqueeze(1).to_broadcast([MH, P, TOEP])).then_inc(bias_out, 16)
            sp.wait_ge(xn_t, KC)
            def gate_tile(r):
                c0 = QL + KVL + ROPE + r * P
                load_tile(G1 + r - r % 4, None, r % 4, d["mla_w_in"][:, c0:c0 + P], KC)

            gate_tile(0)
            gate_tile(1)
            for r in range(8):
                if r == 1:
                    sp.wait_ge(tile_done, 4)
                if r >= 2:
                    sp.wait_ge(ada_used, r - 1)
                sp.dma_start(AB[r % 2][:], ada_weights(4 + r)).then_inc(s_adaw[r % 2], 16)
                if r == 0:
                    gate_tile(2)
                    gate_tile(3)
                elif 2 <= r < 6:
                    gate_tile(r + 2)

            def head_weights(i):
                for j in range(4):
                    sp.wait_ge(lo_done, tile_no(HD - 1, i, j))
                    h = 4 * i + j
                    sp.dma_start(RAW[:, j % 2, 2 * 192:2 * 192 + 256], d["mla_w_kvup"][:, bass.ds(256 * i * 4 + 256 * j, 256)])\
                        .then_inc(kv_raw, 16)
                    sp.wait_ge(kv_raw, 16 * h + 16)
                    sp.dma_start(RAW[:, j % 2, 0:2 * 192].rearrange("p (k n) -> p k n", k=2),
                                 d["mla_w_qup"][:, bass.ds(192 * i * 4 + 192 * j, 192)].rearrange("(k p) n -> p k n", p=P))\
                        .then_inc(raw_full[j % 2], 16)

            with sp.Fori(0, 2) as i:
                head_weights(i)
            load(MO, 2, d["mla_w_out"], 0)
            sp.wait_ge(o_lo, HEADS)
            sp.dma_start(CDR[:], d["dft_dim"]).then_inc(s_dft, 16)
            for m in range(4):
                sp.dma_start(DFR[:, 2 * m:2 * m + 2, :], d["dft_tok"][m].rearrange("(k p) n -> p k n", p=P)).then_inc(s_dft, 16)
            load(FG, 2, d["fno_w_in"], D)
            load(FZ, 2, d["fno_w_in"], 0)
            load(FO, 2, d["fno_w_out"], 0)
            w = d["w_in_2"]
            mw, kw, vw = MH * MD, GH * DK, GH * DV
            sp.wait_ge(f_lo, KC)
            sp.wait_ge(bias_out, 16)
            sp.dma_start(BIAS[:], bass.AP(toep, P - 1, [[TOEP - 1, P], [P * TOEP, MH], [1, T]])).then_inc(s_bias, 16)
            load(MV, 1, w, 2 * mw)
            with sp.Fori(0, 2) as i:
                for j in range(4):
                    load_tile(MQ, i, j, w[:, bass.ds(2 * P * i + (mw * (j // 2) + P * (j % 2)), P)], KC)
            load(GM, 2, w, 3 * mw + 2 * kw + vw + RANK + vw)
            for j in range(4):
                load_tile(BM, None, j, d["w_branch_moba_2"][:, 2 * P * j:2 * P * (j + 1)], 4)
            sp.wait_ge(o_lo, HEADS + MH)
            low = 3 * mw + 2 * kw + vw
            sp.dma_start(LWR[:], w[:, low:low + P].rearrange("(k p) n -> p k n", p=P)).then_inc(s_low, 16)
            sp.dma_start(GUP[:], d["gla_gate_up_2"]).then_inc(s_low, 16)
            with sp.Fori(0, 2) as i:
                for j in range(4):
                    load_tile(GK, i, j, w[:, bass.ds(2 * P * i + (3 * mw + kw * (j // 2) + P * (j % 2)), P)], KC, 8)
                for j in range(4):
                    load_tile(GK + 4, i, j, w[:, bass.ds(2 * DV * i + (3 * mw + 2 * kw + P * j), P)], KC, 8)
            load(GO, 2, w, low + RANK)
            load(GG, 2, w, low + RANK + vw + D)
            load(BG, 2, d["w_branch_gla_2"], 0)
            load(WO, 2, d["w_out_2"], 0)

            def quarter(i):
                for b in range(8):
                    c = slice(D * 3 + P * b, D * 3 + P * (b + 1)) if i is None else bass.ds(D * i + P * b, P)
                    load_tile(FF + 48 * (i is None) + (b // 4) * 4, i, b % 4, d["w_up_2"][:, c], KC, 16)
                for b in range(8):
                    r = slice(D * 3, D * 4) if i is None else bass.ds(D * i, D)
                    load_tile(FF + 48 * (i is None) + 8 + (b // 4) * 4, i, b % 4, d["w_down_2"][r, P * b:P * (b + 1)], KC, 16)

            with sp.Fori(0, 3) as i:
                quarter(i)
            quarter(None)
            sp.wait_ge(bias_out, 16)
            sp.wait_ge(out_c, 8)
            for m in range(TT):
                sp.dma_start(d["out"][m * P:(m + 1) * P, :], OUT[:, m, :]).then_inc(out_s, 16)
            sp.wait_ge(out_s, 16 * TT)

        @block.gpsimd
        def _(pool):
            def split_lo(t0, i, j, per=4):
                pool.wait_ge(hi_done, tile_no(t0 + 1, i, j, per))
                pool.tensor_tensor(WL[:, j, :], RAW[:, j % 2, :], f(WH[:, j, :]), ALU.subtract).then_inc(lo_done, 1)

            def clear_sum(n):
                pool.memset(ACC[:, 0:T // 2], 0.0).then_inc(norm["acc"], 1)
                pool.memset(ACC[:, T // 2:T], 0.0).then_inc(norm["acc"], 1)
                pool.wait_ge(norm["acc"], so_far(n, "acc") + 2)

            def add_square(n, c, slot):
                pool.wait_ge(norm["sq"], so_far(n, "sq") + c + 1)
                pool.wait_ge(norm["acc"], so_far(n, "acc") + c + 2)
                pool.tensor_tensor(ACC[:], ACC[:], SQ[:, slot, :], ALU.add).then_inc(norm["acc"], 1)

            for j in range(4):
                split_lo(A0, None, j)
            for j in range(4):
                pool.wait_ge(a_raw, j + 1)
                split_lo(G1, None, j)
            with pool.Fori(0, 2) as i:
                for j in range(4):
                    split_lo(G1 + 4, i, j)
            with pool.Fori(0, 2) as i:
                for j in range(4):
                    split_lo(HD + 4, i, j)
            clear_sum(0)
            with pool.Fori(0, 2) as i:
                for j in range(4):
                    c = 4 * i + j
                    add_square(0, c, j % 2)
                    pool.wait_ge(norm["h"], so_far(0, "h") + c + 1)
                    split_lo(MO + 4, i, j)
            with pool.Fori(0, 2) as i:
                for j in range(4):
                    split_lo(FG + 4, i, j)
            with pool.Fori(0, 2) as i:
                for j in range(4):
                    split_lo(FZ + 4, i, j)
            pool.wait_ge(norm["rstd"], so_far(0, "rstd") + 1)
            clear_sum(1)
            with pool.Fori(0, 2) as i:
                for j in range(4):
                    c = 4 * i + j
                    add_square(1, c, j % 2)
                    pool.wait_ge(norm["h"], so_far(1, "h") + c + 1)
                    split_lo(FO + 4, i, j)
            pool.wait_ge(norm["rstd"], so_far(1, "rstd") + 1)
            clear_sum(2)
            for c in range(KC):
                add_square(2, c, c % 2)
            for j in range(4):
                pool.wait_ge(v_lo, j + 1)
                split_lo(MQ, None, j)
            with pool.Fori(0, 2) as i:
                pool.wait_ge(v_lo, 4)
                for n in range(2):
                    for dst, src in ((VSH, VH), (VSL, VL)):
                        pool.tensor_copy(dst[:, n, :, :], f(src[:, :, bass.ds(2 * P * i + n * P, P)])).then_inc(vs_done, 1)
                for j in range(4):
                    pool.wait_ge(o_lo, 4 * i + (HEADS + j + 1))
                    split_lo(MQ + 4, i, j)
            with pool.Fori(0, 2) as i:
                for j in range(4):
                    split_lo(GM + 4, i, j)
            for j in range(4):
                pool.wait_ge(bm_e, j + 1)
                split_lo(GK, None, j)
            with pool.Fori(0, 2) as i:
                for j in range(4):
                    split_lo(GK + 4, i, j, 8)
                for j in range(4):
                    split_lo(GK + 8, i, j, 8)
            for t0 in (GO, GG):
                with pool.Fori(0, 2) as i:
                    for j in range(4):
                        split_lo(t0 + 4, i, j)
            with pool.Fori(0, 2) as i:
                for j in range(4):
                    pool.wait_ge(x_e, 4 * i + (j + 1))
                    split_lo(BG + 4, i, j)
            pool.wait_ge(norm["rstd"], so_far(2, "rstd") + 1)
            clear_sum(3)
            with pool.Fori(0, 2) as i:
                for j in range(4):
                    c = 4 * i + j
                    add_square(3, c, j % 2)
                    pool.wait_ge(norm["h"], so_far(3, "h") + c + 1)
                    split_lo(WO + 4, i, j)

            def quarter(i):
                t0 = FF + 48 * (i is None)
                for b in range(8):
                    split_lo(t0 + 4 + (b // 4) * 4, i, b % 4, 16)
                for b in range(8 if i is not None else 4):
                    pool.wait_ge(f_h, 24 + b + 1 if i is None else 8 * i + (b + 1))
                    split_lo(t0 + 12 + (b // 4) * 4, i, b % 4, 16)

            with pool.Fori(0, 3) as i:
                quarter(i)
            quarter(None)

        @block.scalar
        def _(act):
            def split_hi(t0, i, j, per=4):
                act.wait_ge(raw_full[j % 2], raw_count(t0, i, j, per))
                act.activation(WH[:, j, :], RAW[:, j % 2, :], ACT.Copy).then_inc(hi_done, 1)

            act.wait_ge(cols_done, 1)
            for n in range(2):
                act.activation(CACT[:, :, n], COLS[:, 8 * n:8 * n + 8], ACT.Silu).then_inc(cact_done, 1)
            act.wait_ge(s_x, 16)
            for m in range(TT):
                if m >= 1:
                    act.wait_ge(row_ss, m)
                act.activation(JUNK[:], XTOK[:, m, :], ACT.Square, accum_out=RSC[:, m:m + 1]).then_inc(row_ss, 1)
            act.wait_ge(s_ctx, 16)
            for m in range(TC // P):
                act.wait_ge(row_ss, TT + m)
                act.activation(JUNK[:], CTOK[:, m, :], ACT.Square, accum_out=RSC[:, TT + m:TT + m + 1]).then_inc(row_ss, 1)
            act.wait_ge(row_ss, 6)
            act.wait_ge(ones_set, 3)
            act.activation(RSC[:, 0:6], RSC[:, 0:6], ACT.Sqrt, scale=1.0 / D, bias=EPST[:]).then_inc(row_ss, 1)
            for c in range(KC):
                act.wait_ge(x_t, c + 1)
                act.activation(HT[:, c, :], bank(c % 4), ACT.Copy).then_inc(x_copied, 1)
            for q in range(4):
                act.wait_ge(ada_mm, q + 1)
                act.activation(AROW[:, q, :], bank(6)[0:2, :], ACT.Copy).then_inc(ada_row, 1)
            for j in range(4):
                split_hi(A0, None, j)
            for n in range(2 * KC):
                c, lat = n % KC, n < KC
                act.wait_ge(u0_e, n + 1)
                act.activation(UH[:, c, :] if lat else UCH[:, c, :], E[:, n % 2, 0:T if lat else TC], ACT.Copy).then_inc(u0_hi, 1)

            for j in range(4):
                act.wait_ge(tile_done, j + 1)
                if j < 2:
                    act.activation(CQ[:, j, :], bank(j), ACT.Copy).then_inc(a_raw, 1)
                    act.activation(SQ[:, j, :], bank(j), ACT.Square).then_inc(a_sq, 1)
                elif j == 2:
                    act.wait_ge(a_ss, 2)
                    act.activation(CK[:, 0:TC], bank(4, TC), ACT.Copy)
                    act.activation(SQ[:, 1, 0:TC], bank(4, TC), ACT.Square).then_inc(a_sq, 1)
                    act.activation(SQ[:, 0, :], bank(2), ACT.Square).then_inc(a_sq, 1)
                    act.activation(CK[:, TC:TK], bank(2), ACT.Copy).then_inc(a_raw, 1)
                else:
                    act.wait_ge(a_n, 1)
                    act.activation(KP[:, 0:TC], bank(5, TC)[0:ROPE, :], ACT.Copy).then_inc(a_raw, 1)
                split_hi(G1, None, j)
            act.wait_ge(a_ss, 2)
            act.activation(RQ[:], bank(6), ACT.Sqrt, scale=1.0 / QL, bias=EPST[:]).then_inc(a_sqrt, 1)
            act.wait_ge(a_ss, 4)
            act.activation(RKV[:, 0:TC], bank(4, TC, TC), ACT.Sqrt, scale=1.0 / KVL, bias=EPST[:])
            act.activation(RKV[:, TC:TK], bank(7), ACT.Sqrt, scale=1.0 / KVL, bias=EPST[:]).then_inc(a_sqrt, 1)
            act.wait_ge(a_raw, 4)
            act.activation(KPH[:], KP[:], ACT.Copy).then_inc(a_hi, 1)
            act.wait_ge(a_n, 2)
            act.activation(CQH[:], CQ[:], ACT.Copy).then_inc(a_hi, 1)
            act.wait_ge(a_n, 3)
            act.activation(CKH[:], CK[:], ACT.Copy).then_inc(a_hi, 1)

            with act.Fori(0, 2) as i:
                for j in range(4):
                    act.wait_ge(tile_done, tile_no(G1 + 1, i, j))
                    act.activation(SG[:, 4 * i + j, :], bank(j), ACT.Silu).then_inc(sg1, 1)
                    split_hi(G1 + 4, i, j)

            with act.Fori(0, 2) as i:
                def unit(j, u):
                    par = j % 2
                    if u == 5:
                        act.wait_ge(tile_done, tile_no(HD + 1, i, j))
                    elif u != 1:
                        act.wait_ge(un_mm, (UPR - 4) * i + unit_mm_no(j, u))
                    if u == 0:
                        act.activation(QNH[:, par, :], bank(0), ACT.Copy).then_inc(un_hi, 1)
                    elif u == 1:
                        act.wait_ge(un_e, 4 * i + (j + 1))
                        act.activation(QPH[:, par, :], QPF[:], ACT.Copy).then_inc(un_hi, 1)
                    elif u == 2:
                        act.activation(KNH[par][:, TC:TK], bank(0), ACT.Copy).then_inc(un_hi, 1)
                    elif u == 3:
                        act.activation(KNH[par][:, 0:TC], bank(0, TC), ACT.Copy).then_inc(un_hi, 1)
                    elif u == 4:
                        act.activation(VAH[:, 0:4, :], bank(0), ACT.Copy).then_inc(un_hi, 1)
                    else:
                        act.activation(VAH[:, 4:6, :], bank(0, TC), ACT.Copy).then_inc(un_hi, 1)

                def exps(j, q):
                    n = 16 * i + (4 * j + q)
                    act.wait_ge(s_max, n + 1)
                    act.activation(PA[:, q % 2, :], PB[:, (4 + 2 * (q % 2)) * T:(4 + 2 * (q % 2)) * T + TK], ACT.Exp, scale=MLA_SCALE,
                                   bias=NMAX[:, q % 2:q % 2 + 1], accum_out=PSUM_[:, q % 2:q % 2 + 1]).then_inc(s_exp, 1)

                def turned(j, q):
                    n = 16 * i + (4 * j + q)
                    act.wait_ge(t_mm, n + 1)
                    act.activation(PTH[:, :, q * P:(q + 1) * P], PB[:, 2 * T:2 * T + TK].rearrange("p (k n) -> p k n", n=P),
                                   ACT.Copy).then_inc(t_hi, 1)

                def output(j):
                    act.wait_ge(o_e, 4 * i + (j + 1))
                    act.activation(UH[:, 4 * i + j, :], E[:, 1, :], ACT.Copy).then_inc(o_hi, 1)

                for u in range(4):
                    unit(0, u)
                exps(0, 0)
                exps(0, 1)
                for j in range(4):
                    for q in range(4):
                        if q == 0:
                            if j < 3:
                                unit(j + 1, 0)
                            unit(j, 4)
                        elif q == 1 and j < 3:
                            unit(j + 1, 1)
                        elif q == 2 and j < 3:
                            unit(j + 1, 3)
                        turned(j, q)
                        if 4 * j + q + 2 < 16:
                            exps(j + (q + 2) // 4, (q + 2) % 4)
                        if q == 0:
                            unit(j, 5)
                            if j:
                                output(j - 1)
                            split_hi(HD + 4, i, j)
                        elif q == 1 and j < 3:
                            unit(j + 1, 2)
                output(3)

            def square_steps(n, t0):
                with act.Fori(0, 2) as i:
                    for j in range(4):
                        c = 4 * i + j
                        act.wait_ge(norm["h"], so_far(n, "h") + c + 1)
                        act.wait_ge(norm["acc"], so_far(n, "acc") + c + 1)
                        act.activation(SQ[:, j % 2, :], HT[:, c, :], ACT.Square).then_inc(norm["sq"], 1)
                        split_hi(t0 + 4, i, j)

            def root(n, b):
                act.wait_ge(norm["ss"], so_far(n, "ss") + 1)
                act.activation(RS[:], bank(b), ACT.Sqrt, scale=1.0 / D, bias=EPST[:]).then_inc(norm["sqrt"], 1)

            square_steps(0, MO)
            root(0, 4)
            for c in range(KC):
                act.wait_ge(norm["e"], so_far(0, "e") + c + 1)
                act.activation(UH[:, c, :], E[:, c % 2, :], ACT.Identity, bias=ADAL[1][:, c:c + 1]).then_inc(norm["hi"], 1)
            act.wait_ge(s_dft, 80)
            act.activation(CDH[:], CDR[:], ACT.Copy).then_inc(df_hi, 1)
            act.activation(DFH[:], DFR[:], ACT.Copy).then_inc(df_hi, 1)
            with act.Fori(0, 2) as i:
                for j in range(4):
                    act.wait_ge(tile_done, tile_no(FG + 1, i, j))
                    act.activation(SG[:, 4 * i + j, :], bank(j), ACT.Silu).then_inc(sg1, 1)
                    split_hi(FG + 4, i, j)
            with act.Fori(0, 2) as i:
                def z_in(j):
                    act.wait_ge(tile_done, tile_no(FZ + 1, i, j))
                    if j >= 2:
                        act.wait_ge(z_fold, 4 * i + (j - 1))
                    act.activation(ZR[:, j % 2, :], bank(j), ACT.Copy).then_inc(z_raw, 1)
                    split_hi(FZ + 4, i, j)
                    act.wait_ge(z_fold, 4 * i + (j + 1))
                    act.activation(ZH[:, j % 2, :], ZF[:, j % 2, :], ACT.Copy).then_inc(z_hi, 1)

                def a_in(j):
                    act.wait_ge(d_mm, 4 * i + (j + 1))
                    act.activation(AH[:, j % 2, :], PB[:, 4 * T:6 * T], ACT.Copy).then_inc(d_hi, 1)

                def y_in(j):
                    act.wait_ge(f_e, 4 * i + (j + 1))
                    act.activation(YH[:, 4 * i + j, :], E[:, j % 2, :], ACT.Copy).then_inc(f_hi, 1)

                z_in(0)
                z_in(1)
                a_in(0)
                z_in(2)
                a_in(1)
                y_in(0)
                z_in(3)
                a_in(2)
                y_in(1)
                a_in(3)
                y_in(2)
                y_in(3)
            square_steps(1, FO)

            root(1, 4)
            for c in range(KC):
                act.wait_ge(norm["h"], so_far(2, "h") + c + 1)
                act.wait_ge(norm["acc"], so_far(2, "acc") + c + 1)
                act.activation(SQ[:, c % 2, :], HT[:, c, :], ACT.Square).then_inc(norm["sq"], 1)
            root(2, 5)

            def u_hi(n):
                for c in range(KC):
                    act.wait_ge(norm["e"], so_far(n, "e") + c + 1)
                    act.activation(UH[:, c, :], E[:, c % 2, :], ACT.Copy).then_inc(norm["hi"], 1)

            u_hi(2)
            for m in range(TT):
                act.wait_ge(tile_done, MV + m + 1)
                act.activation(VH[:, m, :], bank(m), ACT.Copy).then_inc(v_hi, 1)
            for j in range(4):
                split_hi(MQ, None, j)
            with act.Fori(0, 2) as i:
                def sq(j):
                    act.wait_ge(tile_done, tile_no(MQ + 1, i, j))
                    if j >= 2:
                        act.wait_ge(q_ss, 4 * i + (j - 1))
                    act.activation(SQ[:, j % 2, :], bank(j), ACT.Square).then_inc(q_sq, 1)

                def rt(j):
                    act.wait_ge(q_ss, 4 * i + (j + 1))
                    if j >= 2:
                        act.wait_ge(q_e, 4 * i + (j - 1))
                    act.activation(RQS[:, j % 2, :], bank(4 + j % 2), ACT.Sqrt, scale=1.0 / MD, bias=EPST[:]).then_inc(q_rt, 1)

                sq(0)
                sq(1)
                rt(0)
                sq(2)
                rt(1)
                sq(3)
                rt(2)
                rt(3)
                for j in range(4):
                    act.wait_ge(q_e, 4 * i + (j + 1))
                    act.activation(QKH[:, j, :], E[:, j % 2, :], ACT.Copy).then_inc(q_hi, 1)

                def exps(m, q):
                    act.wait_ge(s_max, 16 * i + (M0 + 4 * m + q + 1))
                    w = (q + 1) * P
                    act.activation(MP[:, q % 2, 0:w], MP[:, q % 2, 0:w], ACT.Exp, bias=NMAX[:, q % 2:q % 2 + 1],
                                   accum_out=PSUM_[:, q % 2:q % 2 + 1]).then_inc(s_exp, 1)

                def turned(m, q):
                    act.wait_ge(t_mm, 16 * i + (M0 + 4 * m + q + 1))
                    act.activation(MTH[:, 0:q + 1, q * P:(q + 1) * P],
                                   bank(6 + q % 2, (q + 1) * P).rearrange("p (k n) -> p k n", n=P), ACT.Copy).then_inc(t_hi, 1)

                for m in range(4):
                    exps(m, 0)
                    exps(m, 1)
                    turned(m, 0)
                    exps(m, 2)
                    turned(m, 1)
                    exps(m, 3)
                    turned(m, 2)
                    turned(m, 3)
                    rows = slice(MD * (m % 2), MD * (m % 2 + 1))
                    act.wait_ge(o_mm, 4 * i + (HEADS + m + 1))
                    act.activation(YH[rows, 2 * i + m // 2, :], bank(m)[rows, :], ACT.Copy).then_inc(o_hi, 1)
                    split_hi(MQ + 4, i, m)
            with act.Fori(0, 2) as i:
                for j in range(4):
                    act.wait_ge(tile_done, tile_no(GM + 1, i, j))
                    act.activation(MX[:, 4 * i + j, :], bank(j), ACT.Sigmoid).then_inc(gm_s, 1)
                    split_hi(GM + 4, i, j)
            for j in range(4):
                act.wait_ge(tile_done, BM + j + 1)
                split_hi(GK, None, j)
            act.wait_ge(s_low, 32)
            act.activation(LWH[:], LWR[:], ACT.Copy).then_inc(l_hi, 1)
            act.wait_ge(l_mm, 1)
            act.activation(GLO[:], bank(4)[0:RANK, :], ACT.Copy).then_inc(l_cp, 1)
            gb = ROW["gate_bias"]
            for h in range(GH):
                act.wait_ge(l_min, h + 1)
                act.activation(BT[:, h, :], bank(h), ACT.Abs, bias=COLS[:, gb + h:gb + h + 1]).then_inc(l_abs, 1)
            act.wait_ge(l_abs, GH)
            act.activation(BT[:], BT[:], ACT.Exp, scale=-1.0).then_inc(l_abs, 1)
            act.wait_ge(l_abs, GH + 1)
            act.activation(BT[:], BT[:], ACT.Ln, bias=1.0).then_inc(l_ln, 1)
            act.wait_ge(b_done, GH)
            with act.Fori(0, 2) as i:
                for j in range(4):
                    act.wait_ge(tile_done, tile_no(GK + 1, i, j, 8))
                    act.activation(GQK[:, j, :], bank(j), ACT.Copy).then_inc(g_raw, 1)
                    split_hi(GK + 4, i, j, 8)
                for m in range(TT):
                    act.wait_ge(tile_done, tile_no(GK + 5, i, m, 8))
                    act.activation(GVH[:, m, :], bank(4 + m), ACT.Copy).then_inc(gv_hi, 1)
                for j in range(4):
                    split_hi(GK + 8, i, j, 8)
                for hh in range(2):
                    n = 2 * i + hh
                    act.activation(EB[:], BT[:, n, :], ACT.Exp, scale=1.0 / TAU).then_inc(g_ex, 1)
                    act.activation(EN[:], BT[:, n, :], ACT.Exp, scale=-1.0 / TAU).then_inc(g_ex, 1)
                    act.wait_ge(g_e, 4 * i + (2 * hh + 1))
                    act.activation(QDH[:], E[:, 0, :], ACT.Copy).then_inc(g_hi, 1)
                    act.wait_ge(g_e, 4 * i + (2 * hh + 2))
                    act.activation(KIH[:], E[:, 1, :], ACT.Copy).then_inc(g_hi, 1)
                    act.wait_ge(kd_d, n + 1)
                    act.activation(SQ[:, 0, :], SQ[:, 0, :], ACT.Exp, scale=1.0 / TAU).then_inc(kd_x, 1)
                    act.wait_ge(am_f, n + 1)
                    act.activation(AMH[:], AMF[:], ACT.Copy).then_inc(am_hi, 1)
                    act.wait_ge(kd_t, n + 1)
                    act.activation(KDH[:], bank(1).rearrange("p (k n) -> p k n", n=P), ACT.Copy).then_inc(kd_hi, 1)
                    act.wait_ge(st_f, n + 1)
                    act.activation(SH[:], SALL[:], ACT.Copy).then_inc(st_hi, 1)
                    for x in range(2):
                        act.wait_ge(go_mm, 4 * i + (2 * hh + x + 1))
                        act.activation(SQ[:, x, :], bank(2 + x), ACT.Square).then_inc(go_sq, 1)
                    act.wait_ge(go_ss, n + 1)
                    act.activation(E[:, 0, :], bank(0), ACT.Sqrt, scale=1.0 / DV, bias=EPST[:]).then_inc(go_rt, 1)
            with act.Fori(0, 2) as i:
                for j in range(4):
                    c = 4 * i + j
                    act.wait_ge(tile_done, tile_no(GO + 1, i, j))
                    act.activation(E[:, j % 2, :], bank(j), ACT.Silu).then_inc(y_s, 1)
                    split_hi(GO + 4, i, j)
                    act.wait_ge(y_e, c + 1)
                    act.activation(YH[:, c, :], SQ[:, j % 2, :], ACT.Copy).then_inc(y_hi, 1)
            with act.Fori(0, 2) as i:
                for j in range(4):
                    act.wait_ge(tile_done, tile_no(GG + 1, i, j))
                    act.activation(SG[:, 4 * i + j, :], bank(j), ACT.Sigmoid).then_inc(gg_s, 1)
                    split_hi(GG + 4, i, j)
            with act.Fori(0, 2) as i:
                for j in range(4):
                    c = 4 * i + j
                    act.wait_ge(tile_done, tile_no(BG + 1, i, j))
                    split_hi(BG + 4, i, j)
                    act.wait_ge(x_e, c + 1)
                    act.activation(UH[:, c, :], E[:, j % 2, :], ACT.Copy).then_inc(x_hi, 1)
            square_steps(3, WO)
            root(3, 4)
            u_hi(3)

            def quarter(i):
                t0 = FF + 48 * (i is None)
                at8 = lambda k: 24 + k if i is None else 8 * i + k
                for b in range(8):
                    j = b % 4
                    act.wait_ge(tile_done, tile_no(t0 + (b // 4) * 4 + 1, i, j, 16))
                    if b >= 2:
                        act.wait_ge(f_ylo, at8(b - 1))
                    act.activation(E[:, b % 2, :], bank(j), ACT.Relu).then_inc(f_r, 1)
                    split_hi(t0 + (b // 4) * 4 + 4, i, j, 16)
                    act.wait_ge(f_r, at8(b + 1))
                    act.activation(YH[:, b, :], E[:, b % 2, :], ACT.Square).then_inc(f_sq, 1)
                act.wait_ge(f_ylo, at8(8))
                for b in range(8 if i is not None else 4):
                    j = b % 4
                    act.wait_ge(tile_done, tile_no(t0 + 8 + (b // 4) * 4 + 1, i, j, 16))
                    split_hi(t0 + (b // 4) * 4 + 12, i, j, 16)

            with act.Fori(0, 3) as i:
                quarter(i)
            quarter(None)

            for m in range(8):
                act.wait_ge(out_t, m + 1)
                act.activation(OUT[:, m % 4, (m // 4) * T:(m // 4 + 1) * T], bank(m), ACT.Copy).then_inc(out_c, 1)

        @block.vector
        def _(v):
            steps = Steps(link_s)

            def link(ins):
                ins.then_inc(link_s, 1)
                steps.k += 1
                v.wait_ge(link_s, steps.now())

            v.memset(ONES[:], 1.0).then_inc(ones_set, 1)
            v.memset(EPST[:], EPS).then_inc(ones_set, 1)
            v.memset(RSC[:], 0.0).then_inc(ones_set, 1)
            v.wait_ge(cols_t, 1)
            v.tensor_copy(COLS[:, 0:NROWS], bank(7, NROWS)).then_inc(cols_done, 1)
            v.wait_ge(cols_done, 1)
            v.wait_ge(row_ss, 7)
            v.reciprocal(RSC[:, 0:6], RSC[:, 0:6]).then_inc(row_rstd, 1)
            v.wait_ge(row_rstd, 1)
            v.wait_ge(x_t, KC)
            for m in range(TT):
                v.tensor_scalar(XTOK[:, m, :], XTOK[:, m, :], RSC[:, m:m + 1], None, ALU.mult).then_inc(x_scaled, 1)
            for m in range(TC // P):
                v.tensor_scalar(CTOK[:, m, :], CTOK[:, m, :], RSC[:, TT + m:TT + m + 1], None, ALU.mult).then_inc(x_scaled, 1)
            v.wait_ge(bias_mm, 1)
            v.wait_ge(s_t5, 48)
            v.tensor_tensor(BROW[:], PB[0:MH, 4 * T:4 * T + TOEP], MROW[:], ALU.add).then_inc(bias_row, 1)
            b0 = ROW["b_ada"]
            v.wait_ge(ada_t, 4)
            mod = bank(7, 32).rearrange("p (c n) -> p c n", n=2)
            v.tensor_tensor(ADAL[0][:, 0:16], mod[:, 0:16, 0], COLS[:, b0:b0 + 16], ALU.add)
            link(v.tensor_tensor(ADAC[:], mod[:, 0:16, 1], COLS[:, b0:b0 + 16], ALU.add))
            g0 = ROW["norm_g"]
            v.scalar_tensor_tensor(MULL[0][:], ADAL[0][:, 8:16], 1.0, COLS[:, g0:g0 + 8], ALU.add, ALU.mult)
            link(v.scalar_tensor_tensor(MULC[:], ADAC[:, 8:16], 1.0, COLS[:, g0:g0 + 8], ALU.add, ALU.mult))

            for n in range(2 * KC + 1):
                if n < 2 * KC:
                    c, lat = n % KC, n < KC
                    mul, add = (MULL[0], ADAL[0]) if lat else (MULC, ADAC)
                    v.wait_ge(xn_t, n + 1)
                    if n >= 2:
                        v.wait_ge(u0_lo, n - 1)
                    v.tensor_scalar(E[:, n % 2, 0:T if lat else TC], bank(c % 4) if lat else bank(4 + c % 2, TC),
                                    mul[:, c:c + 1], add[:, c:c + 1], ALU.mult, ALU.add).then_inc(u0_e, 1)
                if n >= 1:
                    m = n - 1
                    c, lat = m % KC, m < KC
                    hi, lo = (UH, UL) if lat else (UCH, UCL)
                    v.wait_ge(u0_hi, n)
                    v.tensor_tensor(lo[:, c, :], E[:, m % 2, 0:T if lat else TC], f(hi[:, c, :]), ALU.subtract).then_inc(u0_lo, 1)
            swap = [16 + x for x in range(16)] + list(range(16))

            def rotate(out, src, tmp):
                v.tensor_tensor(out, src, COS[:], ALU.mult)
                link(v.stream_shuffle(tmp, src, swap))
                link(v.tensor_tensor(tmp, tmp, SIN[:], ALU.mult))
                return v.tensor_tensor(out, out, tmp, ALU.add)

            link(v.tensor_scalar(QGAIN[:], COLS[:, ROW["q_norm"]:ROW["q_norm"] + 1], MD ** -0.5, None, ALU.mult))

            v.wait_ge(s_rope, 32)
            v.wait_ge(tile_done, 4)
            rotate(KP[:, TC:TK], bank(3)[0:ROPE, :], E[0:ROPE, 0, :]).then_inc(a_n, 1)
            v.wait_ge(a_sqrt, 1)
            link(v.reciprocal(RQ[:], RQ[:]))
            gq, gk = ROW["g_qa"], ROW["g_kva"]
            v.scalar_tensor_tensor(CQ[:, 0, :], CQ[:, 0, :], COLS[:, gq:gq + 1], RQ[:], ALU.mult, ALU.mult)
            v.scalar_tensor_tensor(CQ[:, 1, :], CQ[:, 1, :], COLS[:, gq + 1:gq + 2], RQ[:], ALU.mult, ALU.mult).then_inc(a_n, 1)
            v.wait_ge(a_sqrt, 2)
            link(v.reciprocal(RKV[:], RKV[:]))
            v.scalar_tensor_tensor(CK[:], CK[:], COLS[:, gk:gk + 1], RKV[:], ALU.mult, ALU.mult).then_inc(a_n, 1)
            for n, (lo, hi, src) in enumerate(((KPL, KPH, KP), (CQL, CQH, CQ), (CKL, CKH, CK))):
                v.wait_ge(a_hi, n + 1)
                v.tensor_tensor(lo[:], src[:], f(hi[:]), ALU.subtract).then_inc(a_lo, 1)

            for r in range(8):
                v.wait_ge(s_adaw[r % 2], 16 * (2 + r // 2 + 1))
                if r >= 2:
                    v.wait_ge(ada_mm, 4 + r - 1)
                acc, w = E[:, r % 2, :], AB[r % 2]
                link(v.tensor_scalar(acc, w[:, 0, :], CACT[:, 0, 0:1], None, ALU.mult))
                for k in range(1, KC):
                    ins = v.scalar_tensor_tensor(acc, w[:, k, :], CACT[:, k, 0:1], acc, ALU.mult, ALU.add)
                    if k < KC - 1:
                        link(ins)
                ins.then_inc(ada_used, 1)
            v.wait_ge(ada_mm, 12)
            mod = bank(5, 64).rearrange("p (c n) -> p c n", n=2)
            v.tensor_tensor(ADAL[0][:, 16:24], mod[:, 0:8, 0], COLS[:, b0 + 16:b0 + 24], ALU.add)
            link(v.tensor_tensor(ADAL[1][:], mod[:, 8:32, 0], COLS[:, b0 + 24:b0 + 48], ALU.add))
            link(v.scalar_tensor_tensor(MULL[1][:], ADAL[1][:, 8:16], 1.0, COLS[:, g0 + 8:g0 + 16], ALU.add, ALU.mult))

            with v.Fori(0, 2) as i:
                steps.loop(i, 4 * 10)

                def unit(j, u):
                    par = j % 2
                    if u == 1:
                        v.wait_ge(un_mm, (UPR - 4) * i + unit_mm_no(j, u))
                        rotate(QPF[:], bank(0)[0:ROPE, :], SQ[0:ROPE, 0, :]).then_inc(un_e, 1)
                    v.wait_ge(un_hi, UPR * i + unit_no(j, u))
                    if u == 0:
                        v.tensor_tensor(QNL[:, par, :], bank(0), f(QNH[:, par, :]), ALU.subtract).then_inc(un_lo, 1)
                    elif u == 1:
                        v.tensor_tensor(QPL[:, par, :], QPF[:], f(QPH[:, par, :]), ALU.subtract).then_inc(un_lo, 1)
                    elif u == 2:
                        v.tensor_tensor(KNL[par][:, TC:TK], bank(0), f(KNH[par][:, TC:TK]), ALU.subtract).then_inc(un_lo, 1)
                    elif u == 3:
                        v.tensor_tensor(KNL[par][:, 0:TC], bank(0, TC), f(KNH[par][:, 0:TC]), ALU.subtract).then_inc(un_lo, 1)
                    else:
                        blocks, n = (slice(0, 4), T) if u == 4 else (slice(4, 6), TC)
                        v.tensor_tensor(VAL[:, blocks, :], bank(0, n).rearrange("p (k n) -> p k n", n=P), f(VAH[:, blocks, :]), ALU.subtract)\
                            .then_inc(un_lo, 1)

                def scale(j, q):
                    n, par = 16 * i + (4 * j + q), q % 2
                    v.wait_ge(s_exp, n + 1)
                    link(v.reciprocal(PSUM_[:, 2 + par:3 + par], PSUM_[:, par:par + 1]))
                    v.tensor_scalar(PA[:, par, :], PA[:, par, :], PSUM_[:, 2 + par:3 + par], None, ALU.mult).then_inc(s_scaled, 1)

                def turned(j, q):
                    n = 16 * i + (4 * j + q)
                    v.wait_ge(t_hi, n + 1)
                    v.tensor_tensor(PTL[:, :, q * P:(q + 1) * P], PB[:, 2 * T:2 * T + TK].rearrange("p (k n) -> p k n", n=P),
                                    f(PTH[:, :, q * P:(q + 1) * P]), ALU.subtract).then_inc(t_lo, 1)

                def top(j, q):
                    n, par = 16 * i + (4 * j + q), q % 2
                    v.wait_ge(s_mm, n + 1)
                    link(v.reduce_max(NMAX[:, 2 + par:3 + par], PB[:, (4 + 2 * par) * T:(4 + 2 * par) * T + TK], AX))
                    v.tensor_scalar(NMAX[:, par:par + 1], NMAX[:, 2 + par:3 + par], -MLA_SCALE, None, ALU.mult).then_inc(s_max, 1)

                def output(j):
                    v.wait_ge(o_mm, 4 * i + (j + 1))
                    v.tensor_tensor(E[:, 1, :], bank(1), SG[:, 4 * i + j, :], ALU.mult).then_inc(o_e, 1)

                def output_lo(j):
                    v.wait_ge(o_hi, 4 * i + (j + 1))
                    v.tensor_tensor(UL[:, 4 * i + j, :], E[:, 1, :], f(UH[:, 4 * i + j, :]), ALU.subtract).then_inc(o_lo, 1)

                for u in range(4):
                    unit(0, u)
                top(0, 0)
                top(0, 1)
                scale(0, 0)
                for j in range(4):
                    for q in range(4):
                        n = 4 * j + q
                        if n + 2 < 16 and q != 2:
                            top((n + 2) // 4, (n + 2) % 4)
                        if n + 1 < 16:
                            scale((n + 1) // 4, (n + 1) % 4)
                        if q == 0:
                            if j < 3:
                                unit(j + 1, 0)
                            if j:
                                output(j - 1)
                            unit(j, 4)
                        elif q == 1 and j < 3:
                            unit(j + 1, 1)
                        elif q == 2 and j < 3:
                            unit(j + 1, 3)
                        turned(j, q)
                        if n + 2 < 16 and q == 2:
                            top((n + 2) // 4, (n + 2) % 4)
                        if q == 0:
                            unit(j, 5)
                            if j:
                                output_lo(j - 1)
                        elif q == 1 and j < 3:
                            unit(j + 1, 2)
                output(3)
                output_lo(3)
            steps.leave(2)

            def residual(n, t0, gate):
                with v.Fori(0, 2) as i:
                    for j in range(4):
                        c = 4 * i + j
                        v.wait_ge(tile_done, tile_no(t0 + 1, i, j))
                        v.scalar_tensor_tensor(HT[:, c, :], bank(j), gate[:, bass.ds(4 * i + (16 + j), 1)], HT[:, c, :], ALU.mult, ALU.add)\
                            .then_inc(norm["h"], 1)

            def rstd(n):
                v.wait_ge(norm["sqrt"], so_far(n, "sqrt") + 1)
                v.reciprocal(RS[:], RS[:]).then_inc(norm["rstd"], 1)
                v.wait_ge(norm["rstd"], so_far(n, "rstd") + 1)

            residual(0, MO, ADAL[0])
            rstd(0)
            for c in range(KC + 1):
                if c < KC:
                    if c >= 2:
                        v.wait_ge(norm["lo"], so_far(0, "lo") + c - 1)
                    v.scalar_tensor_tensor(E[:, c % 2, :], HT[:, c, :], MULL[1][:, c:c + 1], RS[:], ALU.mult, ALU.mult).then_inc(norm["e"], 1)
                if c >= 1:
                    m = c - 1
                    v.wait_ge(norm["hi"], so_far(0, "hi") + c)
                    v.scalar_tensor_tensor(UL[:, m, :], E[:, m % 2, :], ADAL[1][:, m:m + 1], f(UH[:, m, :]), ALU.add, ALU.subtract)\
                        .then_inc(norm["lo"], 1)
            v.wait_ge(df_hi, 1)
            v.tensor_tensor(CDL[:], CDR[:], f(CDH[:]), ALU.subtract).then_inc(df_lo, 1)
            v.wait_ge(df_hi, 2)
            v.tensor_tensor(DFL[:], DFR[:], f(DFH[:]), ALU.subtract).then_inc(df_lo, 1)
            with v.Fori(0, 2) as i:
                def z_in(j):
                    v.wait_ge(z_raw, 4 * i + (j + 1))
                    if j >= 2:
                        v.wait_ge(z_lo, 4 * i + (j - 1))
                    v.tensor_tensor(ZF[:, j % 2, 0:HALF], ZR[:, j % 2, 0:HALF], ZR[:, j % 2, HALF:T], ALU.add)
                    v.tensor_tensor(ZF[:, j % 2, HALF:T], ZR[:, j % 2, 0:HALF], ZR[:, j % 2, HALF:T], ALU.subtract).then_inc(z_fold, 1)
                    v.wait_ge(z_hi, 4 * i + (j + 1))
                    v.tensor_tensor(ZL[:, j % 2, :], ZF[:, j % 2, :], f(ZH[:, j % 2, :]), ALU.subtract).then_inc(z_lo, 1)

                def a_in(j):
                    v.wait_ge(d_hi, 4 * i + (j + 1))
                    v.tensor_tensor(AL[:, j % 2, :], PB[:, 4 * T:6 * T], f(AH[:, j % 2, :]), ALU.subtract).then_inc(d_lo, 1)

                def y_in(j):
                    v.wait_ge(f_mm, 4 * i + (j + 1))
                    if j >= 2:
                        v.wait_ge(f_lo, 4 * i + (j - 1))
                    two = "p (t two) -> p two t"
                    v.tensor_tensor(E[:, j % 2, :].rearrange(two, two=2), bank(6 + j % 2).rearrange("p (two t) -> p two t", two=2),
                                    SG[:, 4 * i + j, :].rearrange(two, two=2), ALU.mult).then_inc(f_e, 1)
                    v.wait_ge(f_hi, 4 * i + (j + 1))
                    v.tensor_tensor(YL[:, 4 * i + j, :], E[:, j % 2, :], f(YH[:, 4 * i + j, :]), ALU.subtract).then_inc(f_lo, 1)

                z_in(0)
                z_in(1)
                a_in(0)
                z_in(2)
                a_in(1)
                y_in(0)
                z_in(3)
                a_in(2)
                y_in(1)
                a_in(3)
                y_in(2)
                y_in(3)
            residual(1, FO, ADAL[1])
            rstd(1)
            fg = ROW["final_g"]
            for c in range(KC):
                v.scalar_tensor_tensor(HT[:, c, :], HT[:, c, :], COLS[:, fg + c:fg + c + 1], RS[:], ALU.mult, ALU.mult).then_inc(norm["h"], 1)

            def u_split(n, gain):
                rstd(n)
                for c in range(KC + 1):
                    if c < KC:
                        if c >= 2:
                            v.wait_ge(norm["lo"], so_far(n, "lo") + c - 1)
                        v.scalar_tensor_tensor(E[:, c % 2, :], HT[:, c, :], COLS[:, gain + c:gain + c + 1], RS[:], ALU.mult, ALU.mult)\
                            .then_inc(norm["e"], 1)
                    if c >= 1:
                        m = c - 1
                        v.wait_ge(norm["hi"], so_far(n, "hi") + c)
                        v.tensor_tensor(UL[:, m, :], E[:, m % 2, :], f(UH[:, m, :]), ALU.subtract).then_inc(norm["lo"], 1)

            u_split(2, ROW["norm1"])
            for m in range(TT):
                v.wait_ge(v_hi, m + 1)
                v.tensor_tensor(VL[:, m, :], bank(m), f(VH[:, m, :]), ALU.subtract).then_inc(v_lo, 1)
            v.wait_ge(s_bias, 16)
            with v.Fori(0, 2) as i:
                steps.loop(i, 4 + 32)

                def normed(j):
                    v.wait_ge(q_rt, 4 * i + (j + 1))
                    if j >= 2:
                        v.wait_ge(q_lo, 4 * i + (j - 1))
                    link(v.reciprocal(RQS[:, j % 2, :], RQS[:, j % 2, :]))
                    gain = QGAIN[:] if j < 2 else COLS[:, ROW["k_norm"]:ROW["k_norm"] + 1]
                    v.scalar_tensor_tensor(E[:, j % 2, :], bank(j), gain, RQS[:, j % 2, :], ALU.mult, ALU.mult).then_inc(q_e, 1)

                def low(j):
                    v.wait_ge(q_hi, 4 * i + (j + 1))
                    v.tensor_tensor(QKL[:, j, :], E[:, j % 2, :], f(QKH[:, j, :]), ALU.subtract).then_inc(q_lo, 1)

                normed(0)
                normed(1)
                low(0)
                normed(2)
                low(1)
                normed(3)
                low(2)
                low(3)

                def top(m, q):
                    par, w = q % 2, (q + 1) * P
                    v.wait_ge(s_mm, 16 * i + (M0 + 4 * m + q + 1))
                    link(v.tensor_tensor(MP[:, par, 0:w], bank(4 + par, w), BIAS[:, 4 * i + m, T - w:T], ALU.add))
                    v.reduce_max(NMAX[:, par:par + 1], MP[:, par, 0:w], AX, negate=True).then_inc(s_max, 1)

                def scale(m, q):
                    par, w = q % 2, (q + 1) * P
                    v.wait_ge(s_exp, 16 * i + (M0 + 4 * m + q + 1))
                    link(v.reciprocal(PSUM_[:, 2 + par:3 + par], PSUM_[:, par:par + 1]))
                    v.tensor_scalar(MP[:, par, 0:w], MP[:, par, 0:w], PSUM_[:, 2 + par:3 + par], None, ALU.mult).then_inc(s_scaled, 1)

                def turned(m, q):
                    v.wait_ge(t_hi, 16 * i + (M0 + 4 * m + q + 1))
                    s = slice(q * P, (q + 1) * P)
                    v.tensor_tensor(MTL[:, 0:q + 1, s], bank(6 + q % 2, (q + 1) * P).rearrange("p (k n) -> p k n", n=P),
                                    f(MTH[:, 0:q + 1, s]), ALU.subtract).then_inc(t_lo, 1)

                for m in range(4):
                    top(m, 0)
                    top(m, 1)
                    scale(m, 0)
                    scale(m, 1)
                    turned(m, 0)
                    top(m, 2)
                    scale(m, 2)
                    turned(m, 1)
                    top(m, 3)
                    scale(m, 3)
                    turned(m, 2)
                    turned(m, 3)
                    rows = slice(MD * (m % 2), MD * (m % 2 + 1))
                    v.wait_ge(o_hi, 4 * i + (HEADS + m + 1))
                    v.tensor_tensor(YL[rows, 2 * i + m // 2, :], bank(m)[rows, :], f(YH[rows, 2 * i + m // 2, :]), ALU.subtract)\
                        .then_inc(o_lo, 1)
            steps.leave(2)
            for j in range(4):
                v.wait_ge(tile_done, BM + j + 1)
                v.wait_ge(gm_s, 2 * j + 2)
                v.tensor_tensor(MX[:, 2 * j, :], MX[:, 2 * j, :], bank(j), ALU.mult)
                v.tensor_tensor(MX[:, 2 * j + 1, :], MX[:, 2 * j + 1, :], bank(4 + j), ALU.mult).then_inc(bm_e, 1)
            v.wait_ge(l_hi, 1)
            v.tensor_tensor(LWL[:], LWR[:], f(LWH[:]), ALU.subtract).then_inc(l_lo, 1)
            link(v.memset(RST[:], 1.0))
            link(v.memset(RST[:].rearrange("p (n c) -> p n c", c=CH)[:, :, 0:1], 0.0))
            v.memset(AMF[:], 0.0).then_inc(on_done, 1)
            gb = ROW["gate_bias"]
            for h in range(GH):
                v.wait_ge(l_up, h + 1)
                v.tensor_scalar(MN[:, h, :], bank(h), COLS[:, gb + h:gb + h + 1], 0.0, ALU.add, ALU.min).then_inc(l_min, 1)
            v.wait_ge(l_ln, 1)
            v.wait_ge(l_min, GH)
            link(v.tensor_tensor(MN[:], MN[:], BT[:], ALU.subtract))
            for h in range(GH):
                v.tensor_tensor_scan(BT[:, h, :], RST[:], MN[:, h, :], 0.0, ALU.mult, ALU.add).then_inc(b_done, 1)
            v.wait_ge(s_mask, 16)
            with v.Fori(0, 2) as i:
                steps.loop(i, 2 * 7)
                for m in range(TT):
                    v.wait_ge(gv_hi, 4 * i + (m + 1))
                    v.tensor_tensor(GVL[:, m, :], bank(4 + m), f(GVH[:, m, :]), ALU.subtract).then_inc(gv_lo, 1)
                for hh in range(2):
                    n = 2 * i + hh
                    v.wait_ge(g_raw, 4 * i + 4)
                    v.wait_ge(g_ex, 4 * i + (2 * hh + 1))
                    v.scalar_tensor_tensor(E[:, 0, :], GQK[:, hh, :], DK ** -0.5, EB[:], ALU.mult, ALU.mult).then_inc(g_e, 1)
                    v.wait_ge(g_ex, 4 * i + (2 * hh + 2))
                    v.tensor_tensor(E[:, 1, :], GQK[:, 2 + hh, :], EN[:], ALU.mult).then_inc(g_e, 1)
                    b3 = BT[:, n, :].rearrange("p (n c) -> p n c", c=CH)
                    v.tensor_tensor(SQ[:, 0, :].rearrange("p (n c) -> p n c", c=CH), b3[:, :, CH - 1:CH].to_broadcast([P, NCH, CH]), b3,
                                    ALU.subtract).then_inc(kd_d, 1)
                    v.wait_ge(g_hi, 4 * i + (2 * hh + 1))
                    v.tensor_tensor(QDL[:], E[:, 0, :], f(QDH[:]), ALU.subtract).then_inc(g_lo, 1)
                    v.wait_ge(g_hi, 4 * i + (2 * hh + 2))
                    v.tensor_tensor(KIL[:], E[:, 1, :], f(KIH[:]), ALU.subtract).then_inc(g_lo, 1)
                    v.wait_ge(kd_x, n + 1)
                    v.tensor_tensor(SQ[:, 1, :], GQK[:, 2 + hh, :], SQ[:, 0, :], ALU.mult).then_inc(kd_e, 1)
                    v.wait_ge(at_mm, n + 1)
                    v.tensor_copy(DUMMY[:, 0:1], EPST[:])
                    v.copy_predicated(AMF[:].rearrange("p (k n) -> p k n", n=P),
                                      CMASK[:].unsqueeze(1).to_broadcast([P, TT, P]),
                                      bank(0).rearrange("p (k n) -> p k n", n=P)).then_inc(am_f, 1)
                    v.wait_ge(am_hi, n + 1)
                    v.tensor_tensor(AML[:], AMF[:], f(AMH[:]), ALU.subtract).then_inc(am_lo, 1)
                    v.wait_ge(kd_hi, n + 1)
                    v.tensor_tensor(KDL[:], bank(1).rearrange("p (k n) -> p k n", n=P), f(KDH[:]), ALU.subtract).then_inc(kd_lo, 1)
                    v.wait_ge(kv_mm, n + 1)
                    ins = v.tensor_copy(SALL[:, 0, :], kv_bank(0))
                    for c in range(1, NCH - 1):
                        link(ins)
                        ins = v.scalar_tensor_tensor(SALL[:, c, :], SALL[:, c - 1, :], EB[:, CH * c + CH - 1:CH * c + CH],
                                                     kv_bank(c), ALU.mult, ALU.add)
                    ins.then_inc(st_f, 1)
                    v.wait_ge(st_hi, n + 1)
                    v.tensor_tensor(SL[:], SALL[:], f(SH[:]), ALU.subtract).then_inc(st_lo, 1)
                    v.wait_ge(go_rt, n + 1)
                    link(v.reciprocal(E[:, 0, :], E[:, 0, :]))
                    og = ROW["out_norm"]
                    v.scalar_tensor_tensor(SG[:, 4 * i + 2 * hh, :], bank(2), COLS[:, og:og + 1], E[:, 0, :], ALU.mult, ALU.mult)
                    v.scalar_tensor_tensor(SG[:, 4 * i + 2 * hh + 1, :], bank(3), COLS[:, og + 1:og + 2], E[:, 0, :], ALU.mult, ALU.mult)\
                        .then_inc(on_done, 1)
                    v.wait_ge(on_done, n + 2)
            steps.leave(2)
            with v.Fori(0, 2) as i:
                for j in range(4):
                    c = 4 * i + j
                    v.wait_ge(y_s, c + 1)
                    v.tensor_tensor(SQ[:, j % 2, :], E[:, j % 2, :], SG[:, c, :], ALU.mult).then_inc(y_e, 1)
                    v.wait_ge(y_hi, c + 1)
                    v.tensor_tensor(YL[:, c, :], SQ[:, j % 2, :], f(YH[:, c, :]), ALU.subtract).then_inc(y_lo, 1)
            with v.Fori(0, 2) as i:
                steps.loop(i, 4)
                for j in range(4):
                    c = 4 * i + j
                    v.wait_ge(tile_done, tile_no(BG + 1, i, j))
                    v.wait_ge(gg_s, c + 1)
                    link(v.tensor_tensor(E[:, j % 2, :], bank(j), SG[:, c, :], ALU.mult))
                    v.tensor_tensor(E[:, j % 2, :], E[:, j % 2, :], MX[:, c, :], ALU.add).then_inc(x_e, 1)
                    v.wait_ge(x_hi, c + 1)
                    v.tensor_tensor(UL[:, c, :], E[:, j % 2, :], f(UH[:, c, :]), ALU.subtract).then_inc(x_lo, 1)
            steps.leave(2)
            with v.Fori(0, 2) as i:
                for j in range(4):
                    c = 4 * i + j
                    v.wait_ge(tile_done, tile_no(WO + 1, i, j))
                    v.tensor_tensor(HT[:, c, :], bank(j), HT[:, c, :], ALU.add).then_inc(norm["h"], 1)
            u_split(3, ROW["norm2"])

            def quarter(i):
                t0 = FF + 48 * (i is None)
                at8 = lambda k: 24 + k if i is None else 8 * i + k
                for b in range(8):
                    v.wait_ge(f_r, at8(b + 1))
                    link(v.tensor_tensor(SQ[:, b % 2, :], E[:, b % 2, :], E[:, b % 2, :], ALU.mult))
                    v.wait_ge(f_sq, at8(b + 1))
                    v.tensor_tensor(YL[:, b, :], SQ[:, b % 2, :], f(YH[:, b, :]), ALU.subtract).then_inc(f_ylo, 1)
                for b in range(8):
                    v.wait_ge(tile_done, tile_no(t0 + 8 + (b // 4) * 4 + 1, i, b % 4, 16))
                    v.tensor_tensor(HT[:, b, :], bank(b % 4), HT[:, b, :], ALU.add).then_inc(f_h, 1)

            with v.Fori(0, 3) as i:
                steps.loop(i, 8)
                quarter(i)
            steps.leave(3)
            quarter(None)

        @block.tensor
        def _(pe):
            def three(out, ah, al, bh, bl, first, last):
                pe.matmul(out, ah, bh, start=first, stop=False)
                pe.matmul(out, ah, bl, start=False, stop=False)
                return pe.matmul(out, al, bh, start=False, stop=last)

            def wsl(w, j, k):
                return w[:, j, k * P:(k + 1) * P]

            def product(t, j, xh, xl, n=KC, ready=None, before=0):
                pe.wait_ge(lo_done, t + 1)
                for k in range(n):
                    if ready is not None:
                        pe.wait_ge(ready, before + (k + 1))
                    mm = three(bank(j), wsl(WH, j, k), wsl(WL, j, k), xh[:, k, :], xl[:, k, :], k == 0, k == n - 1)
                mm.then_inc(tile_done, 1)

            def linear(t0, xh, xl, ready=None, before=0):
                with pe.Fori(0, 2) as i:
                    for j in range(4):
                        product(tile_no(t0, i, j), j, xh, xl, ready=ready if j == 0 else None, before=before)

            pe.wait_ge(s_const, 32)
            pe.wait_ge(s_vec, 16 * (len(VECS) + 2))
            pe.transpose(bank(7, NROWS), VROWS[:], IDENT[0:NROWS, 0:NROWS]).then_inc(cols_t, 1)
            pe.wait_ge(s_t5, 48)
            pe.matmul(PB[0:MH, 4 * T:5 * T], T5[:], HOT[:, 0:T], start=True, stop=True)
            pe.matmul(PB[0:MH, 5 * T:5 * T + P], T5[:], HOT[:, T:TOEP], start=True, stop=True).then_inc(bias_mm, 1)
            pe.wait_ge(s_x, 16)
            for c in range(KC):
                if c >= 4:
                    pe.wait_ge(x_copied, c - 3)
                for m in range(TT):
                    mm = pe.transpose(bank(c % 4, P, m * P), XTOK[:, m, c * P:(c + 1) * P], IDENT[:])
                mm.then_inc(x_t, 1)

            def ada(q):
                if q < 4:
                    pe.wait_ge(s_adaw[q % 2], 16 * (q // 2 + 1))
                    if q >= 1:
                        pe.wait_ge(ada_row, q)
                    for k in range(KC):
                        mm = pe.matmul(bank(6)[0:2, :], CACT[:, k, :], AD[q % 2][:, k, :], start=k == 0, stop=k == KC - 1)
                    mm.then_inc(ada_mm, 1)
                if q >= 1:
                    pe.wait_ge(ada_row, q)
                    for b in range(4):
                        mm = pe.transpose(bank(7, 2, 2 * (4 * (q - 1) + b)), AROW[:, q - 1, b * P:(b + 1) * P], IDENT[0:2, 0:2])
                    mm.then_inc(ada_t, 1)

            pe.wait_ge(cact_done, 2)
            for q in range(5):
                ada(q)
            pe.wait_ge(x_scaled, 4)
            pe.wait_ge(x_copied, KC)
            for n in range(2 * KC):
                c, lat = n % KC, n < KC
                if lat and c >= 4:
                    pe.wait_ge(u0_e, n - 3)
                if n == KC:
                    pe.wait_ge(x_scaled, 6)
                    pe.wait_ge(bias_row, 1)
                if not lat and c >= 2:
                    pe.wait_ge(u0_e, n - 1)
                for m in range(TT if lat else TC // P):
                    src = XTOK if lat else CTOK
                    dst = bank(c % 4, P, m * P) if lat else bank(4 + c % 2, P, m * P)
                    mm = pe.transpose(dst, src[:, m, c * P:(c + 1) * P], IDENT[:])
                mm.then_inc(xn_t, 1)
            pe.wait_ge(u0_e, 2 * KC)
            for j in range(4):
                pe.wait_ge(lo_done, j + 1)
                for k in range(KC):
                    if j == 0:
                        pe.wait_ge(u0_lo, k + 1)
                    mm = three(bank(j), wsl(WH, j, k), wsl(WL, j, k), UH[:, k, :], UL[:, k, :], k == 0, k == KC - 1)
                if j >= 2:
                    for k in range(KC):
                        pe.wait_ge(u0_lo, KC + k + 1)
                        mm = three(bank(2 + j, TC), wsl(WH, j, k), wsl(WL, j, k), UCH[:, k, :], UCL[:, k, :], k == 0, k == KC - 1)
                mm.then_inc(tile_done, 1)
                if j == 2:
                    for n in range(2):
                        pe.wait_ge(a_sq, n + 1)
                        pe.matmul(bank(6), ONES[:], SQ[:, n, :], start=n == 0, stop=n == 1).then_inc(a_ss, 1)
            pe.wait_ge(a_sq, 3)
            pe.matmul(bank(4, TC, TC), ONES[:], SQ[:, 1, 0:TC], start=True, stop=True).then_inc(a_ss, 1)
            pe.wait_ge(a_sq, 4)
            pe.matmul(bank(7), ONES[:], SQ[:, 0, :], start=True, stop=True).then_inc(a_ss, 1)
            pe.wait_ge(a_raw, 4)
            for r in range(8):
                product(G1 + r, r % 4, UH, UL)
                pe.wait_ge(ada_used, r + 1)
                for b in range(4):
                    mm = pe.matmul(bank(5, 2, 2 * (4 * r + b)), E[:, r % 2, b * P:(b + 1) * P], ONES[:, 0:2], start=True, stop=True)
                mm.then_inc(ada_mm, 1)

            pe.wait_ge(a_lo, 3)
            with pe.Fori(0, 2) as i:
                def unit(j, u):
                    if u == 0:
                        pe.wait_ge(lo_done, tile_no(HD + 1, i, j))
                    if unit_no(j, u) > 1:
                        pe.wait_ge(un_lo, UPR * i + (unit_no(j, u) - 1))
                    wq = lambda w, k, o: w[:, j, 192 * k + o:192 * k + o + P]
                    wk = lambda w, o: w[:, j, 2 * 192 + o:2 * 192 + o + P]
                    if u < 2:
                        for k in range(2):
                            mm = three(bank(0), wq(WH, k, NOPE * u), wq(WL, k, NOPE * u), CQH[:, k, :], CQL[:, k, :], k == 0, k == 1)
                    elif u == 2:
                        mm = three(bank(0), wk(WH, 0), wk(WL, 0), CKH[:, TC:TK], CKL[:, TC:TK], True, True)
                    elif u == 3:
                        mm = three(bank(0, TC), wk(WH, 0), wk(WL, 0), CKH[:, 0:TC], CKL[:, 0:TC], True, True)
                    else:
                        first = 4 * (u - 4)
                        for m in range(first, min(first + 4, TK // P)):
                            s = slice(m * P, (m + 1) * P)
                            mm = three(bank(0, P, (m - first) * P), CKH[:, s], CKL[:, s], wk(WH, P), wk(WL, P), True, True)
                    mm.then_inc(tile_done if u == 5 else un_mm, 1)

                def scores(j, q):
                    n, par = 16 * i + (4 * j + q), q % 2
                    if q == 0:
                        pe.wait_ge(un_lo, UPR * i + unit_no(j, 3))
                    if q >= 2:
                        pe.wait_ge(s_exp, n - 1)
                    s = slice(q * P, (q + 1) * P)
                    for b, (k0, k1) in enumerate(((0, T), (T, TK))):
                        out = bank(4 + 2 * par + b, k1 - k0)
                        three(out, QNH[:, j % 2, s], QNL[:, j % 2, s], KNH[j % 2][:, k0:k1], KNL[j % 2][:, k0:k1], True, False)
                        mm = three(out, QPH[:, j % 2, s], QPL[:, j % 2, s], KPH[:, k0:k1], KPL[:, k0:k1], False, True)
                    mm.then_inc(s_mm, 1)

                def turn(j, q):
                    n = 16 * i + (4 * j + q)
                    pe.wait_ge(s_scaled, n + 1)
                    if q >= 1:
                        pe.wait_ge(t_lo, n)
                    for k in range(TK // P):
                        mm = pe.transpose(bank(2, P, k * P), PA[:, q % 2, k * P:(k + 1) * P], IDENT[:])
                    mm.then_inc(t_mm, 1)

                def output(j):
                    pe.wait_ge(un_lo, UPR * i + unit_no(j, 5))
                    pe.wait_ge(t_lo, 16 * i + (4 * j + 4))
                    for k in range(TK // P):
                        mm = three(bank(1), VAH[:, k, :], VAL[:, k, :], PTH[:, k, :], PTL[:, k, :], k == 0, k == TK // P - 1)
                    mm.then_inc(o_mm, 1)

                for u in range(4):
                    unit(0, u)
                scores(0, 0)
                scores(0, 1)
                for j in range(4):
                    for q in range(4):
                        n = 4 * j + q
                        if n + 2 < 16 and q != 2:
                            scores((n + 2) // 4, (n + 2) % 4)
                        if q == 0:
                            if j < 3:
                                unit(j + 1, 0)
                            if j:
                                output(j - 1)
                            unit(j, 4)
                        elif q == 1 and j < 3:
                            unit(j + 1, 1)
                        elif q == 2 and j < 3:
                            unit(j + 1, 3)
                        turn(j, q)
                        if n + 2 < 16 and q == 2:
                            scores((n + 2) // 4, (n + 2) % 4)
                        if q == 0:
                            unit(j, 5)
                        elif q == 1 and j < 3:
                            unit(j + 1, 2)
                output(3)

            linear(MO, UH, UL, ready=o_lo)

            def sums(n, b):
                pe.wait_ge(norm["acc"], so_far(n, "acc") + KC + 2)
                pe.matmul(bank(b), ONES[:], ACC[:], start=True, stop=True).then_inc(norm["ss"], 1)

            sums(0, 4)
            linear(FG, UH, UL, ready=norm["lo"], before=so_far(0, "lo"))
            pe.wait_ge(df_lo, 2)
            with pe.Fori(0, 2) as i:
                def dims(j):
                    pe.wait_ge(z_lo, 4 * i + (j + 1))
                    if j >= 1:
                        pe.wait_ge(d_lo, 4 * i + j)
                    for q in range(4):
                        s = slice(q * P, (q + 1) * P)
                        mm = three(bank(4, 2 * GROUP, 2 * GROUP * q), ZH[:, j % 2, s], ZL[:, j % 2, s], CDH[:], CDL[:], True, True)
                    mm.then_inc(d_mm, 1)

                def toks(j):
                    pe.wait_ge(d_lo, 4 * i + (j + 1))
                    if j >= 2:
                        pe.wait_ge(f_e, 4 * i + (j - 1))
                    for odd in range(2):
                        for k in range(4):
                            q, sine = 2 * odd + k // 2, k % 2
                            s = slice(2 * GROUP * q + GROUP * sine, 2 * GROUP * q + GROUP * (sine + 1))
                            mat = 2 * (2 * odd + sine) + k // 2
                            mm = three(bank(6 + j % 2, HALF, HALF * odd), AH[:, j % 2, s], AL[:, j % 2, s],
                                       DFH[:, mat, :], DFL[:, mat, :], k == 0, k == 3)
                    mm.then_inc(f_mm, 1)

                def lin(j):
                    product(tile_no(FZ, i, j), j, UH, UL)

                lin(0)
                lin(1)
                dims(0)
                lin(2)
                dims(1)
                toks(0)
                lin(3)
                dims(2)
                toks(1)
                dims(3)
                toks(2)
                toks(3)
            linear(FO, YH, YL, ready=f_lo)

            sums(1, 4)
            sums(2, 5)

            def rows_product(t0, m, b, ready=None, before=0):
                s = slice(m * P, (m + 1) * P)
                out = bank(b).rearrange("p (a n) -> p a n", n=P)
                for k in range(KC):
                    if ready is not None:
                        pe.wait_ge(ready, before + k + 1)
                    mm = three(out, UH[:, k, s], UL[:, k, s], WH[:, :, k * P:(k + 1) * P], WL[:, :, k * P:(k + 1) * P],
                               k == 0, k == KC - 1)
                mm.then_inc(tile_done, 1)

            pe.wait_ge(lo_done, MV + 4)
            for m in range(TT):
                rows_product(MV, m, m, ready=norm["lo"] if m == 0 else None, before=so_far(2, "lo"))
            with pe.Fori(0, 2) as i:
                def lin(j):
                    product(tile_no(MQ, i, j), j, UH, UL)

                def ss(j):
                    pe.wait_ge(q_sq, 4 * i + (j + 1))
                    pe.matmul(bank(4 + j % 2), HONES[:], SQ[:, j % 2, :], start=True, stop=True).then_inc(q_ss, 1)

                lin(0)
                lin(1)
                ss(0)
                lin(2)
                ss(1)
                lin(3)
                ss(2)
                ss(3)

                def scores(m, q):
                    n, w = 16 * i + (M0 + 4 * m + q), (q + 1) * P
                    if m == 0 and q == 0:
                        pe.wait_ge(q_lo, 4 * i + 4)
                    if q >= 2:
                        pe.wait_ge(s_max, n - 1)
                    rows = slice(MD * (m % 2), MD * (m % 2 + 1))
                    s = slice(q * P, (q + 1) * P)
                    three(bank(4 + q % 2, w), QKH[rows, m // 2, s], QKL[rows, m // 2, s],
                          QKH[rows, 2 + m // 2, 0:w], QKL[rows, 2 + m // 2, 0:w], True, True).then_inc(s_mm, 1)

                def turn(m, q):
                    n = 16 * i + (M0 + 4 * m + q)
                    pe.wait_ge(s_scaled, n + 1)
                    if q >= 2:
                        pe.wait_ge(t_lo, n - 1)
                    for k in range(q + 1):
                        mm = pe.transpose(bank(6 + q % 2, P, k * P), MP[:, q % 2, k * P:(k + 1) * P], IDENT[:])
                    mm.then_inc(t_mm, 1)

                for m in range(4):
                    scores(m, 0)
                    scores(m, 1)
                    turn(m, 0)
                    scores(m, 2)
                    turn(m, 1)
                    scores(m, 3)
                    turn(m, 2)
                    turn(m, 3)
                    pe.wait_ge(t_lo, 16 * i + (M0 + 4 * m + 4))
                    if m == 0:
                        pe.wait_ge(vs_done, 4 * i + 4)
                    for k in range(TT):
                        mm = three(bank(m, T - k * P, k * P), VSH[:, m // 2, k, :], VSL[:, m // 2, k, :],
                                   MTH[:, k, k * P:T], MTL[:, k, k * P:T], k == 0, k == TT - 1)
                    mm.then_inc(o_mm, 1)
            linear(GM, UH, UL)
            for j in range(4):
                pe.wait_ge(lo_done, BM + j + 1)
                if j == 0:
                    pe.wait_ge(o_lo, HEADS + MH)
                for o in range(2):
                    for k in range(4):
                        s = slice(2 * P * k + P * o, 2 * P * k + P * (o + 1))
                        mm = three(bank(4 * o + j), WH[:, j, s], WL[:, j, s], YH[:, k, :], YL[:, k, :], k == 0, k == 3)
                mm.then_inc(tile_done, 1)
            pe.wait_ge(l_lo, 1)
            pe.wait_ge(bm_e, 4)
            for k in range(KC):
                mm = three(bank(4), LWH[:, k, :], LWL[:, k, :], UH[:, k, :], UL[:, k, :], k == 0, k == KC - 1)
            mm.then_inc(l_mm, 1)
            pe.wait_ge(s_low, 32)
            pe.wait_ge(l_cp, 1)
            for h in range(GH):
                pe.matmul(bank(h), GUP[:, h * DK:(h + 1) * DK], GLO[:], start=True, stop=True).then_inc(l_up, 1)
            pe.wait_ge(l_min, GH)
            pe.wait_ge(l_ln, 1)
            with pe.Fori(0, 2) as i:
                pe.wait_ge(on_done, 2 * i + 1)
                for j in range(4):
                    product(tile_no(GK, i, j, 8), j, UH, UL)
                pe.wait_ge(lo_done, tile_no(GK + 8, i, 0, 8))
                for m in range(TT):
                    rows_product(GK + 4, m, 4 + m)
                for hh in range(2):
                    n = 2 * i + hh
                    pe.wait_ge(g_lo, 4 * i + (2 * hh + 2))
                    if hh == 1:
                        pe.wait_ge(go_rt, n)
                    for k in range(TT):
                        s = slice(k * P, (k + 1) * P)
                        mm = three(bank(0, P, k * P), KIH[:, s], KIL[:, s], QDH[:, s], QDL[:, s], True, True)
                    mm.then_inc(at_mm, 1)
                    pe.wait_ge(kd_e, n + 1)
                    for k in range(TT):
                        mm = pe.transpose(bank(1, P, k * P), SQ[:, 1, k * P:(k + 1) * P], IDENT[:])
                    mm.then_inc(kd_t, 1)
                    pe.wait_ge(kd_lo, n + 1)
                    if hh == 0:
                        pe.wait_ge(gv_lo, 4 * i + 4)
                    for c in range(NCH - 1):
                        rows = slice(CH * (c % 2), CH * (c % 2 + 1))
                        vals = slice(hh * DV, (hh + 1) * DV)
                        mm = three(kv_bank(c), KDH[rows, c // 2, :], KDL[rows, c // 2, :],
                                   GVH[rows, c // 2, vals], GVL[rows, c // 2, vals], True, True)
                    mm.then_inc(kv_mm, 1)
                    pe.wait_ge(am_lo, n + 1)
                    if hh == 1:
                        pe.wait_ge(on_done, n + 1)
                    for x in range(2):
                        for k in range(TT):
                            vals = slice(hh * DV + x * P, hh * DV + (x + 1) * P)
                            s = slice(k * P, (k + 1) * P)
                            three(bank(2 + x, P, k * P), GVH[:, k, vals], GVL[:, k, vals], AMH[:, s], AML[:, s], k == 0, False)
                    pe.wait_ge(st_lo, n + 1)
                    for x in range(2):
                        for c in range(1, NCH):
                            s, vals = slice(c * CH, (c + 1) * CH), slice(x * P, (x + 1) * P)
                            mm = three(bank(2 + x, CH, c * CH), SH[:, c - 1, vals], SL[:, c - 1, vals], QDH[:, s], QDL[:, s],
                                       False, c == NCH - 1)
                        mm.then_inc(go_mm, 1)
                    for x in range(2):
                        pe.wait_ge(go_sq, 4 * i + (2 * hh + x + 1))
                        mm = pe.matmul(bank(0), ONES[:], SQ[:, x, :], start=x == 0, stop=x == 1)
                    mm.then_inc(go_ss, 1)
            pe.wait_ge(on_done, GH + 1)
            linear(GO, UH, UL)
            linear(GG, UH, UL)
            linear(BG, YH, YL, ready=y_lo)
            linear(WO, UH, UL, ready=x_lo)
            sums(3, 4)

            def quarter(i):
                t0 = FF + 48 * (i is None)
                for b in range(8):
                    product(tile_no(t0 + (b // 4) * 4, i, b % 4, 16), b % 4, UH, UL, ready=norm["lo"] if b == 0 else None, before=so_far(3, "lo"))
                for b in range(8):
                    product(tile_no(t0 + 8 + (b // 4) * 4, i, b % 4, 16), b % 4, YH, YL, ready=f_ylo if b == 0 else None,
                            before=24 if i is None else 8 * i)

            with pe.Fori(0, 3) as i:
                quarter(i)
            quarter(None)

            pe.wait_ge(f_h, 4 * KC)
            for m in range(8):
                for c in range(4):
                    mm = pe.transpose(bank(m, P, c * P), HT[:, 4 * (m // 4) + c, (m % 4) * P:(m % 4 + 1) * P], IDENT[:])
                mm.then_inc(out_t, 1)


_INPUTS = ["x", "c", "ctx", "c_ctx", "norm_g", "w_ada", "b_ada", "mla_w_in", "mla_g_qa", "mla_w_qup", "mla_g_kva",
           "mla_w_kvup", "mla_w_out", "fno_w_in", "fno_w_out", "final_g", "norm1_g_2", "w_in_2", "moba_q_norm_g_2",
           "moba_k_norm_g_2", "t5_bias_2", "gla_gate_up_2", "gla_gate_bias_2", "gla_out_norm_g_2", "w_branch_moba_2",
           "w_branch_gla_2", "w_out_2", "norm2_g_2", "w_up_2", "w_down_2"]
_VEC_INPUTS = {"c": "c", "c_ctx": "c_ctx", "norm_g": "norm_g", "b_ada": "b_ada", "final_g": "final_g", "norm1": "norm1_g_2",
               "norm2": "norm2_g_2", "g_qa": "mla_g_qa", "g_kva": "mla_g_kva", "gate_bias": "gla_gate_bias_2",
               "out_norm": "gla_out_norm_g_2", "q_norm": "moba_q_norm_g_2", "k_norm": "moba_k_norm_g_2"}


def kernel(**inputs):
    import numpy as _np
    import concourse.bacc as _bacc
    from concourse import mybir as _mybir
    from concourse.bass_utils import run_bass_kernel_spmd as _run

    nc = _bacc.Bacc("TRN2", target_bir_lowering=False, num_devices=1)
    arrays, d = {}, {}
    vec_of = {v: k for k, v in _VEC_INPUTS.items()}
    for name in _INPUTS:
        a = _np.ascontiguousarray(inputs[name])
        key = name
        if name in vec_of:
            key = vec_of[name]
            a = a.reshape(-1, MD if key in ("q_norm", "k_norm") else P)
        elif a.ndim == 3 and a.shape[0] == 1:
            a = a[0]
        arrays[f"in_{name}"] = a
        d[key] = nc.dram_tensor(f"in_{name}", a.shape, _mybir.dt.from_np(a.dtype), kind="ExternalInput").ap()
    for name, a in shape_constants().items():
        arrays[f"const_{name}"] = a
        d[name] = nc.dram_tensor(f"const_{name}", a.shape, _mybir.dt.from_np(a.dtype), kind="ExternalInput").ap()
    d["out"] = nc.dram_tensor("out", (T, D), _mybir.dt.float32, kind="ExternalOutput").ap()
    build(nc, d)
    r = _run(nc, [arrays], core_ids=[0])
    return r.results[0]["out"].reshape(1, T, D)
```

```python
import math
from contextlib import ExitStack

import numpy as np

import concourse.bass as bass
from concourse import mybir

P = 128
T = 512
TC = 256
TK = T + TC
D = 1024
KC = D // P
TT = T // P
EPS = 1e-6
NEG = -1e30

HEADS = 8
NOPE = 128
ROPE = 64
QL = 256
KVL = 128
MLA_SCALE = 1.0 / math.sqrt(NOPE + ROPE)
GRID_W = 64
GROUP = 128
HALF = T // 2
MH = 8
MD = 64
BUCKETS = 32
MAX_DIST = 128
TOEP = T + P
GH = 4
DK = 128
DV = 256
RANK = 16
TAU = 16.0
CH = 64
NCH = T // CH

A0, G1, HD, MO, FG, FZ, FO, MV, MQ, BM, GK, GG, BG, WO, FF = (
    0, 4, 12, 20, 28, 36, 44, 52, 56, 72, 76, 100, 108, 116, 124)

VECS = [("c", 8), ("c_ctx", 8), ("norm_g", 16), ("b_ada", 48), ("final_g", 8), ("norm1", 8), ("norm2", 8),
        ("g_qa", 2), ("g_kva", 1), ("gate_bias", 4), ("out_norm", 2), ("q_norm", 1), ("k_norm", 1)]
ROW = {}
for _n, _r in VECS:
    ROW[_n] = sum(r for _, r in VECS[:len(ROW)])
NROWS = sum(r for _, r in VECS)


def shape_constants():
    out = {}
    out["identity"] = np.eye(P, dtype=np.float32)
    pick = np.zeros((P, 224), np.float32)
    pick[:MD, 96], pick[MD:, 97] = 1.0, 1.0
    out["head_pick"] = pick
    spread = np.zeros((P, P), np.float32)
    spread[0::32, :MD], spread[1::32, MD:] = 1.0, 1.0
    out["head_spread"] = spread
    e, c = np.meshgrid(np.arange(P), np.arange(P), indexing="ij")
    out["chunk_causal"] = ((e // CH == c // CH) & (e <= c)).astype(np.int32)
    axis_dim = ROPE // 2
    inv = (1.0 / (np.float32(10000.0) ** (np.arange(0, axis_dim, 2, dtype=np.float32) / np.float32(axis_dim)))).astype(np.float32)
    row = np.repeat(np.arange(T // GRID_W), GRID_W).astype(np.float32)
    col = np.tile(np.arange(GRID_W), T // GRID_W).astype(np.float32)
    cos, sin = [], []
    for pos in (row, col):
        ang = (pos[None, :] * inv[:, None]).astype(np.float32).astype(np.float64)
        cos += [np.cos(ang), np.cos(ang)]
        sin += [-np.sin(ang), np.sin(ang)]
    out["rope_cos"] = np.concatenate(cos).astype(np.float32)
    out["rope_sin"] = np.concatenate(sin).astype(np.float32)
    k = np.arange(GROUP)
    ang = 2 * np.pi * ((k[:, None] * k[None, :]) % GROUP) / GROUP
    norm = 1.0 / math.sqrt(T * GROUP)
    out["dft_dim"] = np.concatenate([np.cos(ang), -np.sin(ang)], 1).astype(np.float32) * np.float32(norm)
    t, s = np.arange(HALF)[:, None], np.arange(HALF)[None, :]
    mats = []
    for odd in (0, 1):
        ang = 2 * np.pi * ((t * (2 * s + odd)) % T) / T
        mats += [np.cos(ang), np.sin(ang)]
    out["dft_tok"] = np.stack(mats).astype(np.float32)
    d = T - 1 - np.arange(TOEP)
    exact = BUCKETS // 2
    large = exact + (np.log(np.maximum(d, 1).astype(np.float32) / np.float32(exact))
                     / np.float32(math.log(MAX_DIST / exact)) * np.float32(BUCKETS - exact)).astype(np.int32)
    bucket = np.where(d < exact, np.maximum(d, 0), np.minimum(large, BUCKETS - 1))
    out["bucket_hot"] = ((np.arange(BUCKETS)[:, None] == bucket[None, :]) & (d >= 0)).astype(np.float32)
    out["mask_row"] = np.tile(np.where(d >= 0, 0.0, NEG).astype(np.float32), (MH, 1))
    return out


class Steps:

    def __init__(self, sem):
        self.sem, self.base, self.k = sem, 0, 0
        self.i = None

    def loop(self, i, per):
        self.base, self.i, self.per, self.k = self.base + self.k, i, per, 0

    def leave(self, rounds):
        assert self.k == self.per, (self.k, self.per)
        self.base, self.i, self.k = self.base + rounds * self.per, None, 0

    def now(self):
        here = self.base + self.k
        return here if self.i is None else self.i * self.per + here


def build(nc, d):
    f32, f32r, i32 = mybir.dt.float32, mybir.dt.float32r, mybir.dt.int32
    ACT = mybir.ActivationFunctionType
    ALU = mybir.AluOpType
    AX = mybir.AxisListType.X

    ctx = ExitStack()
    with ctx:
        KB = 1024
        BASE = 16512

        def at(name, kb, shape, dt=f32):
            return nc.alloc_sbuf_tensor_at(name, shape, dt, offset=BASE + int(kb * KB))

        def sem(name):
            return ctx.enter_context(nc.semaphore(name))

        HT = at("residual", 0, [P, KC, T])
        UH = at("u_hi", 16, [P, KC, T], f32r)
        UL = at("u_lo", 32, [P, KC, T], f32r)
        RAW = at("w_raw", 48, [P, 2, KC * P])
        WH = at("w_hi", 56, [P, 4, KC * P], f32r)
        WL = at("w_lo", 72, [P, 4, KC * P], f32r)
        YH = at("y_hi", 88, [P, KC, T], f32r)
        YL = at("y_lo", 104, [P, KC, T], f32r)
        SG = at("gated", 120, [P, KC, T])
        MX = at("mixed", 136, [P, KC, T])
        IDENT = at("ident", 152, [P, P])
        HSPREAD = at("head_spread_sb", 152.5, [P, P])
        ONES = at("ones", 153, [P, P])
        COLS = at("cols", 153.5, [P, P])
        ADAL = [at(f"ada_lat{n}", 154 + 0.125 * n, [P, 24]) for n in range(2)]
        ADAC = at("ada_ctx", 154.25, [P, 16])
        MULL = [at(f"mul_lat{n}", 154.375 + 0.0625 * n, [P, KC]) for n in range(2)]
        MULC = at("mul_ctx", 154.5, [P, KC])
        CACT = at("c_act", 154.5625, [P, KC, 2])
        RSC = at("row_rstd", 154.6875, [P, 8])
        NMAX = at("neg_max", 154.75, [P, 4])
        PSUM_ = at("prob_sum", 154.8125, [P, 4])
        EPST = at("eps", 154.875, [P, 1])
        QGAIN = at("q_gain", 154.90625, [P, 1])
        DUMMY = at("dummy", 154.9375, [P, 2])
        HPICK = at("head_pick_sb", 155, [P, 224])
        RS = at("rstd", 156, [P, T])
        ACC = at("sq_sum", 158, [P, T])
        SQ = at("squares", 160, [P, 2, T])
        E = at("stage", 164, [P, 2, T])

        UCH = at("uc_hi", 88, [P, KC, TC], f32r)
        UCL = at("uc_lo", 96, [P, KC, TC], f32r)
        AROW = at("ada_rows", 88, [2, 4, T])
        XTOK = at("x_tok", 104, [P, TT, D])
        AD = [at("ada_w0", 120, [P, KC, T]), at("ada_w1", 136, [P, KC, T])]
        AB = [at("ada_back0", 104, [P, KC, T]), at("ada_back1", 88, [P, KC, T])]
        AACC = [at("ada_sum0", 156, [P, T]), at("ada_sum1", 158, [P, T]), at("ada_sum2", 204, [P, T])]
        VROWS = at("vec_rows", 168, [NROWS, P])
        JUNK = at("junk", 170, [P, D])
        CTOK = at("ctx_tok", 174, [P, TC // P, D])
        HOT = at("bucket_hot_sb", 184, [BUCKETS, TOEP])
        MROW = at("mask_row_sb", 187, [MH, TOEP])
        BROW = at("bias_row", 190, [MH, TOEP])
        T5 = at("t5", 193, [BUCKETS, MH])
        CQ = at("cq", 136, [P, 2, T])
        CK = at("ckv", 140, [P, TK])
        KP = at("kp", 143, [ROPE, TK])
        RQ = at("cq_rstd", 146, [P, T])
        RKV = at("ckv_rstd", 148, [P, TK])
        CQH, CQL = at("cq_hi", 168, [P, 2, T], f32r), at("cq_lo", 172, [P, 2, T], f32r)
        CKH, CKL = at("ckv_hi", 176, [P, TK], f32r), at("ckv_lo", 179, [P, TK], f32r)
        KPH, KPL = at("kp_hi", 182, [ROPE, TK], f32r), at("kp_lo", 185, [ROPE, TK], f32r)
        KNH = [at("kn_hi0", 188, [P, TK], f32r), at("kn_hi1", 204, [P, TK], f32r)]
        KNL = [at("kn_lo0", 191, [P, TK], f32r), at("kn_lo1", 162, [P, TK], f32r)]
        VAH, VAL = at("va_hi", 194, [P, TK // P, P], f32r), at("va_lo", 197, [P, TK // P, P], f32r)
        COS, SIN = at("cos", 200, [ROPE, T]), at("sin", 202, [ROPE, T])
        QPF, QPR = at("qp", 118, [ROPE, T]), at("qp_raw", 156, [ROPE, T])
        QNH, QNL = at("qn_hi", 136, [P, 2, T], f32r), at("qn_lo", 140, [P, 2, T], f32r)
        QPH, QPL = at("qp_hi", 144, [ROPE, 2, T], f32r), at("qp_lo", 148, [ROPE, 2, T], f32r)
        PTH, PTL = at("pt_hi", 88, [P, TK // P, T], f32r), at("pt_lo", 100, [P, TK // P, T], f32r)
        PA = at("probs", 112, [P, 2, TK])
        DFH, DFL = at("dft_tok_hi", 168, [P, 8, HALF], f32r), at("dft_tok_lo", 176, [P, 8, HALF], f32r)
        CDH, CDL = at("dft_dim_hi", 184, [P, 2 * GROUP], f32r), at("dft_dim_lo", 185, [P, 2 * GROUP], f32r)
        ZH, ZL = at("z_hi", 186, [P, 2, T], f32r), at("z_lo", 190, [P, 2, T], f32r)
        ZF = at("z_fold", 194, [P, 2, T])
        ZR = at("z_raw", 198, [P, 2, T])
        CDR = at("dft_dim_raw", 202, [P, 2 * GROUP])
        DFR = at("dft_tok_raw", 136, [P, 8, HALF])
        AH, AL = at("dim_dft_hi", 136, [P, 2, 4 * 2 * GROUP], f32r), at("dim_dft_lo", 144, [P, 2, 4 * 2 * GROUP], f32r)

        BIAS = at("toeplitz_bias", 120, [P, MH, T])
        VH, VL = at("mv_hi", 168, [P, TT, T], f32r), at("mv_lo", 176, [P, TT, T], f32r)
        QKH, QKL = at("mqk_hi", 184, [P, 4, T], f32r), at("mqk_lo", 192, [P, 4, T], f32r)
        MP = at("m_probs", 200, [P, 3, T])
        MSTAT = at("m_stats", 154.6875, [P, 8])
        VSH, VSL = at("mv_pair_hi", 160, [P, 2, TT, P], f32r), at("mv_pair_lo", 156, [P, 2, TT, P], f32r)
        MTH, MTL = at("m_turned_hi", 96, [P, TT, T], f32r), at("m_turned_lo", 112, [P, TT, T], f32r)
        RROW = at("mqk_rstd", 112, [P, T])
        CMASK = at("causal_mask", 155, [P, P], i32)
        LWR = at("low_raw", 176, [P, KC, P])
        LWH, LWL = at("low_hi", 180, [P, KC, P], f32r), at("low_lo", 184, [P, KC, P], f32r)
        GLO = at("g_low", 188, [RANK, T])
        GUP = at("gate_up", 190, [RANK, T])
        MN = at("log_decay", 192, [P, GH, T])
        RST = at("chunk_starts", 202, [P, T])
        BT = at("decay_sum", 96, [P, GH, T])
        GQK = at("gqk", 168, [P, 4, T])
        SALL = at("states", 176, [P, NCH - 1, DV])
        SH, SL = at("states_hi", 183, [P, NCH - 1, DV], f32r), at("states_lo", 190, [P, NCH - 1, DV], f32r)
        KDH, KDL = at("kdec_hi", 197, [P, TT, DK], f32r), at("kdec_lo", 199, [P, TT, DK], f32r)
        AMH, AML = at("attn_hi", 201, [P, T], f32r), at("attn_lo", 203, [P, T], f32r)
        AMF = at("attn", 205, [P, T])
        EB, EN = at("exp_decay", 156, [P, T]), at("exp_growth", 158, [P, T])
        GVH, GVL = at("gv_hi", 88, [P, TT, T], f32r), at("gv_lo", 104, [P, TT, T], f32r)
        QDH = [at("qdec_hi0", 112, [P, T], f32r), at("qdec_hi1", 168, [P, T], f32r)]
        QDL = [at("qdec_lo0", 114, [P, T], f32r), at("qdec_lo1", 172, [P, T], f32r)]
        DEC = at("chunk_decay", 154.6875, [P, 2, NCH])
        GSIG = at("gate_gla_sb", 168, [P, KC, T])
        KIH, KIL = at("kinv_hi", 116, [P, T], f32r), at("kinv_lo", 118, [P, T], f32r)

        PB = ctx.enter_context(nc.psum_tensor("psum", [P, 8 * T], f32))

        def bank(b, n=T, o=0):
            return PB[:, b * T + o:b * T + o + n]

        def kv_bank(c):
            return bank(4 + 2 * (c % 2) + c // 4, DV, (c // 2) % 2 * DV)

        def f(ap):
            return ap.bitcast(f32)

        raw_full = [sem(f"raw_full{s}") for s in range(2)]
        hi_done = sem("w_hi_done")
        lo_done = sem("w_lo_done")
        tile_done = sem("tile_done")
        s_vec = sem("vec_loaded")
        s_x = sem("x_loaded")
        s_ctx = sem("ctx_loaded")
        s_const = sem("const_loaded")
        s_rope = sem("rope_loaded")
        s_t5 = sem("t5_loaded")
        s_adaw = [sem("ada_loaded0"), sem("ada_loaded1")]
        ones_set = sem("ones_set")
        cols_t = sem("cols_transposed")
        cols_done = sem("cols_done")
        cact_done = sem("c_act_done")
        ada_mm = sem("ada_multiplied")
        ada_row, ada_t, ada_used = sem("ada_rows_copied"), sem("ada_turned"), sem("ada_used")
        x_t = sem("x_transposed")
        x_copied = sem("x_copied")
        row_ss = sem("row_sums")
        row_rstd = sem("row_rstd_done")
        x_scaled = sem("x_scaled")
        xn_t = sem("xn_transposed")
        u0_e, u0_hi, u0_lo = sem("u0_e"), sem("u0_hi"), sem("u0_lo")
        bias_mm = sem("bias_mm")
        bias_row = sem("bias_row_done")
        bias_out = sem("bias_stored")
        link_s = sem("vector_steps")
        a_raw = sem("a0_copied")
        a_sq = sem("a0_squares")
        a_ss = sem("a0_sums")
        a_sqrt = sem("a0_sqrt")
        a_n = sem("a0_normed")
        a_hi, a_lo = sem("a0_hi"), sem("a0_lo")
        sg1 = sem("gate1_done")
        kv_raw = sem("kv_up_loaded")
        un_mm, un_raw, un_e, un_hi, un_lo = sem("unit_mm"), sem("unit_raw"), sem("unit_rope"), sem("unit_hi"), sem("unit_lo")
        s_mm, s_max, s_exp, s_scaled = sem("scores_mm"), sem("scores_max"), sem("scores_exp"), sem("probs_scaled")
        t_mm, t_hi, t_lo = sem("probs_turned"), sem("turned_hi"), sem("turned_lo")
        o_mm, o_e, o_hi, o_lo = sem("pv_mm"), sem("o_gated"), sem("o_hi"), sem("o_lo")

        norm = {k: sem(f"norm_{k}") for k in ("h", "sq", "acc", "ss", "sqrt", "rstd", "e", "hi", "lo")}

        def so_far(n, k):
            return {"h": KC, "sq": KC, "acc": KC + 2, "ss": 1, "sqrt": 1, "rstd": 1}[k] * n if k not in ("e", "hi", "lo") else KC * max(n - 1, 0)

        out_t = sem("out_transposed")
        out_c = sem("out_copied")
        out_s = sem("out_stored")
        s_dft = sem("dft_loaded")
        df_hi, df_lo = sem("dft_hi"), sem("dft_lo")
        z_raw, z_fold, z_hi, z_lo = sem("z_copied"), sem("z_folded"), sem("z_hi_done"), sem("z_lo_done")
        d_mm, d_hi, d_lo = sem("dim_dft_mm"), sem("dim_dft_hi_done"), sem("dim_dft_lo_done")
        f_mm, f_e, f_hi, f_lo = sem("tok_dft_mm"), sem("y_gated"), sem("y_hi_done"), sem("y_lo_done")

        s_bias = sem("bias_loaded")
        s_mask = sem("mask_loaded")
        v_hi, v_lo, vs_done = sem("mv_hi_done"), sem("mv_lo_done"), sem("mv_pair_done")
        q_sq, q_ss, q_rt = sem("mqk_squares"), sem("mqk_sums"), sem("mqk_sqrt")
        q_rs, q_sp, q_g = sem("mqk_rstd"), sem("mqk_rstd_spread"), sem("mqk_gain")
        q_e, q_hi, q_lo = sem("mqk_normed"), sem("mqk_hi_done"), sem("mqk_lo_done")
        M0 = TT * HEADS
        gm_s, bm_e = sem("gate_moba"), sem("branch_moba")
        s_low = sem("low_loaded")
        l_hi, l_lo, l_mm, l_cp, l_up = sem("low_hi_done"), sem("low_lo_done"), sem("low_mm"), sem("low_copied"), sem("gate_up_mm")
        l_abs, l_min, l_ln, b_done = sem("gate_abs"), sem("gate_min"), sem("gate_log"), sem("decay_done")
        g_raw, gv_hi, gv_lo = sem("gqk_copied"), sem("gv_hi_done"), sem("gv_lo_done")
        g_ex, g_e, g_hi, g_lo = sem("exp_done"), sem("qk_decayed"), sem("qk_hi_done"), sem("qk_lo_done")
        kd_d, kd_x, kd_e, kd_t = sem("kdec_exponent"), sem("kdec_exp"), sem("kdec_done"), sem("kdec_turned")
        kd_hi, kd_lo = sem("kdec_hi_done"), sem("kdec_lo_done")
        at_mm, am_f, am_hi, am_lo = sem("attn_mm"), sem("attn_masked"), sem("attn_hi_done"), sem("attn_lo_done")
        kv_mm, st_f, st_hi, st_lo = sem("kv_mm"), sem("states_done"), sem("states_hi_done"), sem("states_lo_done")
        go_mm, go_sq, go_ss, go_rt, on_done = sem("gla_o_mm"), sem("gla_o_sq"), sem("gla_o_sums"), sem("gla_o_sqrt"), sem("gla_o_normed")
        g_si, y_s, y_e, y_hi, y_lo = sem("g_out_silu"), sem("g_out_copied"), sem("g_out_gated"), sem("gy_hi_done"), sem("gy_lo_done")
        gg_s = sem("gate_gla")
        x_e, x_hi, x_lo = sem("mixed_e"), sem("mixed_hi"), sem("mixed_lo")
        f_r, f_sq, f_ylo, f_h = sem("relu_done"), sem("relu_sq_hi"), sem("relu_sq_lo"), sem("ff_added")

        toep = nc.dram_tensor("bias_scratch", (MH, P, TOEP), f32)
        OUT = at("out_rows", 16, [P, TT, D])

        block = ctx.enter_context(nc.Block())

        def raw_count(t0, i, j, per=4):
            return 16 * (t0 // 2 + j // 2 + 1) + (0 if i is None else 8 * per * i)

        def tile_no(t0, i, j, per=4):
            return t0 + j if i is None else per * i + (t0 + j)

        first_units = (1, 0, 2, 3)
        units = [(0, u) for u in first_units]
        for j in range(4):
            units += [(j + 1, u) for u in first_units] * (j < 3) + [(j, 4), (j, 5)]
        UPR = len(units)

        def unit_no(j, u):
            return units.index((j, u)) + 1

        def unit_mm_no(j, u):
            return sum(1 for x in units[:unit_no(j, u)] if x[1] < 5)

        @block.sync
        def _(sp):
            sp.dma_start(IDENT[:], d["identity"]).then_inc(s_const, 16)
            sp.dma_start(XTOK[:], d["x"].rearrange("(m p) n -> p m n", p=P)).then_inc(s_x, 16)
            sp.dma_start(HSPREAD[:], d["head_spread"]).then_inc(s_const, 16)
            sp.dma_start(HPICK[:], d["head_pick"]).then_inc(s_const, 16)
            for name, rows in VECS:
                src = d[name]
                if name in ("q_norm", "k_norm"):
                    for n in range(2):
                        sp.dma_start(VROWS[ROW[name]:ROW[name] + 1, n * MD:(n + 1) * MD], src).then_inc(s_vec, 16)
                else:
                    sp.dma_start(VROWS[ROW[name]:ROW[name] + rows, :], src).then_inc(s_vec, 16)
            sp.dma_start(CTOK[:], d["ctx"].rearrange("(m p) n -> p m n", p=P)).then_inc(s_ctx, 16)
            sp.dma_start(COS[:], d["rope_cos"]).then_inc(s_rope, 16)
            sp.dma_start(SIN[:], d["rope_sin"]).then_inc(s_rope, 16)
            sp.dma_start(T5[:], d["t5_bias_2"]).then_inc(s_t5, 16)
            sp.dma_start(HOT[:], d["bucket_hot"]).then_inc(s_t5, 16)
            sp.dma_start(MROW[:], d["mask_row"]).then_inc(s_t5, 16)

            def load_tile(t0, i, j, src, k, per=4):
                if t0 or j >= 2:
                    sp.wait_ge(lo_done, tile_no(t0 - 1, i, j, per))
                sp.dma_start(RAW[:, j % 2, :].rearrange("p (k n) -> p k n", k=k), src.rearrange("(k p) n -> p k n", p=P))\
                    .then_inc(raw_full[j % 2], 16)

            def load(t0, n, w, c0):
                if n == 1:
                    for j in range(4):
                        load_tile(t0, None, j, w[:, c0 + j * P:c0 + (j + 1) * P], KC)
                else:
                    with sp.Fori(0, n) as i:
                        for j in range(4):
                            load_tile(t0, i, j, w[:, bass.ds(4 * P * i + (c0 + j * P), P)], KC)

            def ada_weights(q):
                return d["w_ada"][q // 6, :, (q % 6) * T:(q % 6 + 1) * T].rearrange("(k p) n -> p k n", p=P)

            for q in range(4):
                if q >= 2:
                    sp.wait_ge(ada_mm, q - 1)
                sp.dma_start(AD[q % 2][:], ada_weights(q)).then_inc(s_adaw[q % 2], 16)
            load(A0, 1, d["mla_w_in"], 0)
            sp.wait_ge(bias_row, 1)
            sp.dma_start(toep.ap(), BROW[:].unsqueeze(1).to_broadcast([MH, P, TOEP])).then_inc(bias_out, 16)
            sp.wait_ge(xn_t, KC)
            def gate_tile(r):
                c0 = QL + KVL + ROPE + r * P
                load_tile(G1 + r - r % 4, None, r % 4, d["mla_w_in"][:, c0:c0 + P], KC)

            gate_tile(0)
            gate_tile(1)
            for r in range(8):
                if r >= 2:
                    sp.wait_ge(ada_used, r - 1)
                if r == 3:
                    gate_tile(2)
                    gate_tile(3)
                    sp.wait_ge(tile_done, 4)
                sp.dma_start((AD[0] if r == 1 else AB[r % 2])[:], ada_weights(4 + r)).then_inc(s_adaw[r % 2], 16)
                if 3 <= r < 7:
                    gate_tile(r + 1)

            def head_weights(i):
                for j in range(4):
                    sp.wait_ge(lo_done, tile_no(HD - 1, i, j))
                    h = 4 * i + j
                    sp.dma_start(RAW[:, j % 2, 2 * 192:2 * 192 + 256], d["mla_w_kvup"][:, bass.ds(256 * i * 4 + 256 * j, 256)])\
                        .then_inc(kv_raw, 16)
                    sp.wait_ge(kv_raw, 16 * h + 16)
                    sp.dma_start(RAW[:, j % 2, 0:2 * 192].rearrange("p (k n) -> p k n", k=2),
                                 d["mla_w_qup"][:, bass.ds(192 * i * 4 + 192 * j, 192)].rearrange("(k p) n -> p k n", p=P))\
                        .then_inc(raw_full[j % 2], 16)

            with sp.Fori(0, 2) as i:
                head_weights(i)
            load(MO, 2, d["mla_w_out"], 0)
            sp.wait_ge(o_lo, HEADS)
            sp.dma_start(CDR[:], d["dft_dim"]).then_inc(s_dft, 16)
            for m in range(4):
                sp.dma_start(DFR[:, 2 * m:2 * m + 2, :], d["dft_tok"][m].rearrange("(k p) n -> p k n", p=P)).then_inc(s_dft, 16)
            load(FG, 2, d["fno_w_in"], D)
            load(FZ, 2, d["fno_w_in"], 0)
            load(FO, 2, d["fno_w_out"], 0)
            w = d["w_in_2"]
            mw, kw, vw = MH * MD, GH * DK, GH * DV
            sp.wait_ge(f_lo, KC)
            sp.wait_ge(bias_out, 16)
            sp.dma_start(BIAS[:], bass.AP(toep, P - 1, [[TOEP - 1, P], [P * TOEP, MH], [1, T]])).then_inc(s_bias, 16)
            load(MV, 1, w, 2 * mw)
            with sp.Fori(0, 2) as i:
                for j in range(4):
                    load_tile(MQ, i, j, w[:, bass.ds(2 * P * i + (mw * (j // 2) + P * (j % 2)), P)], KC, 8)
                for j in range(4):
                    load_tile(MQ + 4, i, j, w[:, bass.ds(4 * P * i + (3 * mw + 2 * kw + vw + RANK + vw + P * j), P)], KC, 8)
            for j in range(4):
                load_tile(BM, None, j, d["w_branch_moba_2"][:, 2 * P * j:2 * P * (j + 1)], 4)
            sp.wait_ge(o_lo, HEADS + MH)
            sp.dma_start(CMASK[:], d["chunk_causal"]).then_inc(s_mask, 16)
            low = 3 * mw + 2 * kw + vw
            sp.dma_start(LWR[:], w[:, low:low + P].rearrange("(k p) n -> p k n", p=P)).then_inc(s_low, 16)
            sp.dma_start(GUP[:], d["gla_gate_up_2"]).then_inc(s_low, 16)
            with sp.Fori(0, 2) as i:
                for j in range(4):
                    load_tile(GK, i, j, w[:, bass.ds(2 * P * i + (3 * mw + kw * (j // 2) + P * (j % 2)), P)], KC, 12)
                for j in range(4):
                    load_tile(GK + 4, i, j, w[:, bass.ds(2 * DV * i + (3 * mw + 2 * kw + P * j), P)], KC, 12)
                for j in range(4):
                    load_tile(GK + 8, i, j, w[:, bass.ds(2 * DV * i + (low + RANK + P * j), P)], KC, 12)
            load(GG, 2, w, low + RANK + vw + D)
            load(BG, 2, d["w_branch_gla_2"], 0)
            load(WO, 2, d["w_out_2"], 0)

            def quarter(i):
                for b in range(8):
                    c = slice(D * 3 + P * b, D * 3 + P * (b + 1)) if i is None else bass.ds(D * i + P * b, P)
                    load_tile(FF + 48 * (i is None) + (b // 4) * 4, i, b % 4, d["w_up_2"][:, c], KC, 16)
                for b in range(8):
                    r = slice(D * 3, D * 4) if i is None else bass.ds(D * i, D)
                    load_tile(FF + 48 * (i is None) + 8 + (b // 4) * 4, i, b % 4, d["w_down_2"][r, P * b:P * (b + 1)], KC, 16)

            with sp.Fori(0, 3) as i:
                quarter(i)
            quarter(None)
            sp.wait_ge(bias_out, 16)
            sp.wait_ge(out_c, 8)
            for m in range(TT):
                sp.dma_start(d["out"][m * P:(m + 1) * P, :], OUT[:, m, :]).then_inc(out_s, 16)
            sp.wait_ge(out_s, 16 * TT)

        @block.gpsimd
        def _(pool):
            def split_lo(t0, i, j, per=4):
                pool.wait_ge(hi_done, tile_no(t0 + 1, i, j, per))
                pool.tensor_tensor(WL[:, j, :], RAW[:, j % 2, :], f(WH[:, j, :]), ALU.subtract).then_inc(lo_done, 1)

            def clear_sum(n):
                pool.memset(ACC[:, 0:T // 2], 0.0).then_inc(norm["acc"], 1)
                pool.memset(ACC[:, T // 2:T], 0.0).then_inc(norm["acc"], 1)
                pool.wait_ge(norm["acc"], so_far(n, "acc") + 2)

            def add_square(n, c, slot):
                pool.wait_ge(norm["sq"], so_far(n, "sq") + c + 1)
                pool.wait_ge(norm["acc"], so_far(n, "acc") + c + 2)
                pool.tensor_tensor(ACC[:], ACC[:], SQ[:, slot, :], ALU.add).then_inc(norm["acc"], 1)

            for j in range(4):
                split_lo(A0, None, j)
            for j in range(4):
                pool.wait_ge(a_raw, j + 1)
                split_lo(G1, None, j)
            with pool.Fori(0, 2) as i:
                for j in range(4):
                    split_lo(G1 + 4, i, j)
            with pool.Fori(0, 2) as i:
                for j in range(4):
                    split_lo(HD + 4, i, j)
            clear_sum(0)
            with pool.Fori(0, 2) as i:
                for j in range(4):
                    c = 4 * i + j
                    add_square(0, c, j % 2)
                    pool.wait_ge(norm["h"], so_far(0, "h") + c + 1)
                    split_lo(MO + 4, i, j)
            with pool.Fori(0, 2) as i:
                for j in range(4):
                    split_lo(FG + 4, i, j)
            with pool.Fori(0, 2) as i:
                for j in range(4):
                    split_lo(FZ + 4, i, j)
            pool.wait_ge(norm["rstd"], so_far(0, "rstd") + 1)
            clear_sum(1)
            with pool.Fori(0, 2) as i:
                for j in range(4):
                    c = 4 * i + j
                    add_square(1, c, j % 2)
                    pool.wait_ge(norm["h"], so_far(1, "h") + c + 1)
                    split_lo(FO + 4, i, j)
            pool.wait_ge(norm["rstd"], so_far(1, "rstd") + 1)
            clear_sum(2)
            for c in range(KC):
                add_square(2, c, c % 2)
            for j in range(4):
                pool.wait_ge(v_lo, j + 1)
                split_lo(MQ, None, j)
            with pool.Fori(0, 2) as i:
                for j in range(4):
                    split_lo(MQ + 4, i, j, 8)
                pool.wait_ge(q_lo, 4 * i + 4)
                for n in range(2):
                    for dst, src in ((VSH, VH), (VSL, VL)):
                        pool.tensor_copy(dst[:, n, :, :], f(src[:, :, bass.ds(2 * P * i + n * P, P)])).then_inc(vs_done, 1)
                for j in range(4):
                    split_lo(MQ + 8, i, j, 8)
            for j in range(4):
                pool.wait_ge(bm_e, j + 1)
                split_lo(GK, None, j)
            with pool.Fori(0, 2) as i:
                for t0 in (GK + 4, GK + 8, GK + 12):
                    for j in range(4):
                        split_lo(t0, i, j, 12)
            with pool.Fori(0, 2) as i:
                for j in range(4):
                    split_lo(GG + 4, i, j)
            with pool.Fori(0, 2) as i:
                for j in range(4):
                    pool.wait_ge(x_e, 4 * i + (j + 1))
                    split_lo(BG + 4, i, j)
            pool.wait_ge(norm["rstd"], so_far(2, "rstd") + 1)
            clear_sum(3)
            with pool.Fori(0, 2) as i:
                for j in range(4):
                    c = 4 * i + j
                    add_square(3, c, j % 2)
                    pool.wait_ge(norm["h"], so_far(3, "h") + c + 1)
                    split_lo(WO + 4, i, j)

            def quarter(i):
                t0 = FF + 48 * (i is None)
                for b in range(8):
                    split_lo(t0 + 4 + (b // 4) * 4, i, b % 4, 16)
                for b in range(8 if i is not None else 4):
                    pool.wait_ge(f_h, 24 + b + 1 if i is None else 8 * i + (b + 1))
                    split_lo(t0 + 12 + (b // 4) * 4, i, b % 4, 16)

            with pool.Fori(0, 3) as i:
                quarter(i)
            quarter(None)

        @block.scalar
        def _(act):
            def split_hi(t0, i, j, per=4):
                act.wait_ge(raw_full[j % 2], raw_count(t0, i, j, per))
                act.activation(WH[:, j, :], RAW[:, j % 2, :], ACT.Copy).then_inc(hi_done, 1)

            act.wait_ge(cols_done, 1)
            for n in range(2):
                act.activation(CACT[:, :, n], COLS[:, 8 * n:8 * n + 8], ACT.Silu).then_inc(cact_done, 1)
            act.wait_ge(s_x, 16)
            for m in range(TT):
                if m >= 1:
                    act.wait_ge(row_ss, m)
                act.activation(JUNK[:], XTOK[:, m, :], ACT.Square, accum_out=RSC[:, m:m + 1]).then_inc(row_ss, 1)
            act.wait_ge(s_ctx, 16)
            for m in range(TC // P):
                act.wait_ge(row_ss, TT + m)
                act.activation(JUNK[:], CTOK[:, m, :], ACT.Square, accum_out=RSC[:, TT + m:TT + m + 1]).then_inc(row_ss, 1)
            act.wait_ge(row_ss, 6)
            act.wait_ge(ones_set, 3)
            act.activation(RSC[:, 0:6], RSC[:, 0:6], ACT.Sqrt, scale=1.0 / D, bias=EPST[:]).then_inc(row_ss, 1)
            for c in range(KC):
                act.wait_ge(x_t, c + 1)
                act.activation(HT[:, c, :], bank(c % 4), ACT.Copy).then_inc(x_copied, 1)
            for q in range(4):
                act.wait_ge(ada_mm, q + 1)
                act.activation(AROW[:, q, :], bank(6)[0:2, :], ACT.Copy).then_inc(ada_row, 1)
            for j in range(4):
                split_hi(A0, None, j)
            for n in range(2 * KC):
                c, lat = n % KC, n < KC
                act.wait_ge(u0_e, n + 1)
                act.activation(UH[:, c, :] if lat else UCH[:, c, :], E[:, n % 2, 0:T if lat else TC], ACT.Copy).then_inc(u0_hi, 1)

            for j in range(4):
                act.wait_ge(tile_done, j + 1)
                if j < 2:
                    act.activation(CQ[:, j, :], bank(j), ACT.Copy).then_inc(a_raw, 1)
                    act.activation(SQ[:, j, :], bank(j), ACT.Square).then_inc(a_sq, 1)
                elif j == 2:
                    act.wait_ge(a_ss, 2)
                    act.activation(CK[:, 0:TC], bank(4, TC), ACT.Copy)
                    act.activation(SQ[:, 1, 0:TC], bank(4, TC), ACT.Square).then_inc(a_sq, 1)
                    act.activation(SQ[:, 0, :], bank(2), ACT.Square).then_inc(a_sq, 1)
                    act.activation(CK[:, TC:TK], bank(2), ACT.Copy).then_inc(a_raw, 1)
                else:
                    act.wait_ge(a_n, 1)
                    act.activation(KP[:, 0:TC], bank(5, TC)[0:ROPE, :], ACT.Copy).then_inc(a_raw, 1)
                split_hi(G1, None, j)
            act.wait_ge(a_ss, 2)
            act.activation(RQ[:], bank(6), ACT.Sqrt, scale=1.0 / QL, bias=EPST[:]).then_inc(a_sqrt, 1)
            act.wait_ge(a_ss, 4)
            act.activation(RKV[:, 0:TC], bank(4, TC, TC), ACT.Sqrt, scale=1.0 / KVL, bias=EPST[:])
            act.activation(RKV[:, TC:TK], bank(7), ACT.Sqrt, scale=1.0 / KVL, bias=EPST[:]).then_inc(a_sqrt, 1)
            act.wait_ge(a_raw, 4)
            act.activation(KPH[:], KP[:], ACT.Copy).then_inc(a_hi, 1)
            act.wait_ge(a_n, 2)
            act.activation(CQH[:], CQ[:], ACT.Copy).then_inc(a_hi, 1)
            act.wait_ge(a_n, 3)
            act.activation(CKH[:], CK[:], ACT.Copy).then_inc(a_hi, 1)

            act.wait_ge(ada_used, 2)
            with act.Fori(0, 2) as i:
                for j in range(4):
                    act.wait_ge(tile_done, tile_no(G1 + 1, i, j))
                    act.activation(SG[:, 4 * i + j, :], bank(j), ACT.Silu).then_inc(sg1, 1)
                    split_hi(G1 + 4, i, j)

            with act.Fori(0, 2) as i:
                def unit(j, u):
                    par = j % 2
                    if u == 5:
                        act.wait_ge(tile_done, tile_no(HD + 1, i, j))
                    elif u != 1:
                        act.wait_ge(un_mm, (UPR - 4) * i + unit_mm_no(j, u))
                    if u == 0:
                        act.activation(QNH[:, par, :], bank(0), ACT.Copy).then_inc(un_hi, 1)
                    elif u == 1:
                        act.wait_ge(un_e, 4 * i + (j + 1))
                        act.activation(QPH[:, par, :], QPF[:], ACT.Copy).then_inc(un_hi, 1)
                    elif u == 2:
                        act.activation(KNH[par][:, TC:TK], bank(0), ACT.Copy).then_inc(un_hi, 1)
                    elif u == 3:
                        act.activation(KNH[par][:, 0:TC], bank(0, TC), ACT.Copy).then_inc(un_hi, 1)
                    elif u == 4:
                        act.activation(VAH[:, 0:4, :], bank(0), ACT.Copy).then_inc(un_hi, 1)
                    else:
                        act.activation(VAH[:, 4:6, :], bank(0, TC), ACT.Copy).then_inc(un_hi, 1)

                def exps(j, q):
                    n = 16 * i + (4 * j + q)
                    act.wait_ge(s_max, n + 1)
                    act.activation(PA[:, q % 2, :], PB[:, (4 + 2 * (q % 2)) * T:(4 + 2 * (q % 2)) * T + TK], ACT.Exp, scale=MLA_SCALE,
                                   bias=NMAX[:, q % 2:q % 2 + 1], accum_out=PSUM_[:, q % 2:q % 2 + 1]).then_inc(s_exp, 1)

                def turned(j, q):
                    n = 16 * i + (4 * j + q)
                    act.wait_ge(t_mm, n + 1)
                    act.activation(PTH[:, :, q * P:(q + 1) * P], PB[:, 2 * T:2 * T + TK].rearrange("p (k n) -> p k n", n=P),
                                   ACT.Copy).then_inc(t_hi, 1)

                def rope_raw(j):
                    act.wait_ge(un_mm, (UPR - 4) * i + unit_mm_no(j, 1))
                    act.activation(QPR[:], bank(0)[0:ROPE, :], ACT.Copy).then_inc(un_raw, 1)

                def output(j):
                    act.wait_ge(o_e, 4 * i + (j + 1))
                    act.activation(UH[:, 4 * i + j, :], E[:, 1, :], ACT.Copy).then_inc(o_hi, 1)

                rope_raw(0)
                unit(0, 1)
                unit(0, 0)
                unit(0, 2)
                unit(0, 3)
                exps(0, 0)
                exps(0, 1)
                for j in range(4):
                    nxt = j < 3
                    if nxt:
                        rope_raw(j + 1)
                        unit(j + 1, 1)
                    if j:
                        output(j - 1)
                    if nxt:
                        unit(j + 1, 0)
                    turned(j, 0)
                    if nxt:
                        unit(j + 1, 2)
                    exps(j, 2)
                    if nxt:
                        unit(j + 1, 3)
                    turned(j, 1)
                    exps(j, 3)
                    unit(j, 4)
                    turned(j, 2)
                    if nxt:
                        exps(j + 1, 0)
                    unit(j, 5)
                    turned(j, 3)
                    if nxt:
                        exps(j + 1, 1)
                    split_hi(HD + 4, i, j)
                output(3)

            def square_steps(n, t0):
                with act.Fori(0, 2) as i:
                    for j in range(4):
                        c = 4 * i + j
                        act.wait_ge(norm["h"], so_far(n, "h") + c + 1)
                        act.wait_ge(norm["acc"], so_far(n, "acc") + c + 1)
                        act.activation(SQ[:, j % 2, :], HT[:, c, :], ACT.Square).then_inc(norm["sq"], 1)
                        split_hi(t0 + 4, i, j)

            def root(n, b):
                act.wait_ge(norm["ss"], so_far(n, "ss") + 1)
                act.activation(RS[:], bank(b), ACT.Sqrt, scale=1.0 / D, bias=EPST[:]).then_inc(norm["sqrt"], 1)

            square_steps(0, MO)
            root(0, 4)
            for c in range(KC):
                act.wait_ge(norm["e"], so_far(0, "e") + c + 1)
                act.activation(UH[:, c, :], E[:, c % 2, :], ACT.Identity, bias=ADAL[1][:, c:c + 1]).then_inc(norm["hi"], 1)
            act.wait_ge(s_dft, 80)
            act.activation(CDH[:], CDR[:], ACT.Copy).then_inc(df_hi, 1)
            act.activation(DFH[:], DFR[:], ACT.Copy).then_inc(df_hi, 1)
            with act.Fori(0, 2) as i:
                for j in range(4):
                    act.wait_ge(tile_done, tile_no(FG + 1, i, j))
                    act.activation(SG[:, 4 * i + j, :], bank(j), ACT.Silu).then_inc(sg1, 1)
                    split_hi(FG + 4, i, j)
            with act.Fori(0, 2) as i:
                def z_in(j):
                    act.wait_ge(tile_done, tile_no(FZ + 1, i, j))
                    if j >= 2:
                        act.wait_ge(z_fold, 4 * i + (j - 1))
                    act.activation(ZR[:, j % 2, :], bank(j), ACT.Copy).then_inc(z_raw, 1)
                    split_hi(FZ + 4, i, j)
                    act.wait_ge(z_fold, 4 * i + (j + 1))
                    act.activation(ZH[:, j % 2, :], ZF[:, j % 2, :], ACT.Copy).then_inc(z_hi, 1)

                def a_in(j):
                    act.wait_ge(d_mm, 4 * i + (j + 1))
                    act.activation(AH[:, j % 2, :], PB[:, 4 * T:6 * T], ACT.Copy).then_inc(d_hi, 1)

                def y_in(j):
                    act.wait_ge(f_e, 4 * i + (j + 1))
                    act.activation(YH[:, 4 * i + j, :], E[:, j % 2, :], ACT.Copy).then_inc(f_hi, 1)

                z_in(0)
                z_in(1)
                a_in(0)
                z_in(2)
                a_in(1)
                y_in(0)
                z_in(3)
                a_in(2)
                y_in(1)
                a_in(3)
                y_in(2)
                y_in(3)
            square_steps(1, FO)

            root(1, 4)
            for c in range(KC):
                act.wait_ge(norm["h"], so_far(2, "h") + c + 1)
                act.wait_ge(norm["acc"], so_far(2, "acc") + c + 1)
                act.activation(SQ[:, c % 2, :], HT[:, c, :], ACT.Square).then_inc(norm["sq"], 1)
            root(2, 5)

            def u_hi(n):
                for c in range(KC):
                    act.wait_ge(norm["e"], so_far(n, "e") + c + 1)
                    act.activation(UH[:, c, :], E[:, c % 2, :], ACT.Copy).then_inc(norm["hi"], 1)

            u_hi(2)
            for m in range(TT):
                act.wait_ge(tile_done, MV + m + 1)
                act.activation(VH[:, m, :], bank(m), ACT.Copy).then_inc(v_hi, 1)
            for j in range(4):
                split_hi(MQ, None, j)
            with act.Fori(0, 2) as i:
                def gate(j, b):
                    act.wait_ge(tile_done, tile_no(MQ + 5, i, j, 8))
                    act.activation(MX[:, 4 * i + j, :], bank(b), ACT.Copy).then_inc(gm_s, 1)
                    split_hi(MQ + 8, i, j, 8)

                act.wait_ge(o_lo, 4 * i + HEADS)
                for j in range(4):
                    act.wait_ge(tile_done, tile_no(MQ + 1, i, j, 8))
                    if j >= 2:
                        act.wait_ge(q_ss, 4 * i + (j - 1))
                    act.activation(SQ[:, j % 2, :], bank(j), ACT.Square).then_inc(q_sq, 1)
                    split_hi(MQ + 4, i, j, 8)
                act.wait_ge(q_ss, 4 * i + 4)
                act.activation(RROW[:], bank(4), ACT.Sqrt, scale=1.0 / MD, bias=EPST[:]).then_inc(q_rt, 1)
                gate(0, 6)
                for j in range(4):
                    act.wait_ge(q_e, 4 * i + (j + 1))
                    act.activation(QKH[:, j, :], E[:, j % 2, :], ACT.Copy).then_inc(q_hi, 1)
                gate(1, 7)

                def exps(m, q):
                    act.wait_ge(s_max, 16 * i + (M0 + 4 * m + q + 1))
                    x, w = (4 * m + q) % 3, (q + 1) * P
                    act.activation(MP[:, x, 0:w], MP[:, x, 0:w], ACT.Exp, bias=MSTAT[:, x:x + 1],
                                   accum_out=MSTAT[:, 3 + x:4 + x]).then_inc(s_exp, 1)

                def turned(m, q):
                    act.wait_ge(t_mm, 16 * i + (M0 + 4 * m + q + 1))
                    act.activation(MTH[:, 0:q + 1, q * P:(q + 1) * P],
                                   bank(6 + q % 2, (q + 1) * P).rearrange("p (k n) -> p k n", n=P), ACT.Copy).then_inc(t_hi, 1)

                def output(m):
                    rows = slice(MD * (m % 2), MD * (m % 2 + 1))
                    act.wait_ge(o_mm, 4 * i + (HEADS + m + 1))
                    act.activation(YH[rows, 2 * i + m // 2, :], bank(m % 2)[rows, :], ACT.Copy).then_inc(o_hi, 1)

                exps(0, 0)
                exps(0, 1)
                for m in range(4):
                    exps(m, 2)
                    if m:
                        output(m - 1)
                    turned(m, 0)
                    exps(m, 3)
                    turned(m, 1)
                    if m < 3:
                        exps(m + 1, 0)
                    turned(m, 2)
                    if m < 3:
                        exps(m + 1, 1)
                    turned(m, 3)
                    if m % 2 == 0:
                        gate(2 + m // 2, 2 + m // 2)
                output(3)
            for c in range(KC):
                act.activation(MX[:, c, :], MX[:, c, :], ACT.Sigmoid).then_inc(gm_s, 1)
            act.wait_ge(s_low, 32)
            act.activation(LWH[:], LWR[:], ACT.Copy).then_inc(l_hi, 1)
            for j in range(4):
                act.wait_ge(tile_done, BM + j + 1)
                split_hi(GK, None, j)
                if j == 1:
                    act.wait_ge(l_mm, 1)
                    act.activation(GLO[:], bank(7)[0:RANK, :], ACT.Copy).then_inc(l_cp, 1)
            gb = ROW["gate_bias"]
            for h in range(GH):
                act.wait_ge(l_min, h + 1)
                act.activation(BT[:, h, :], bank(h), ACT.Abs, bias=COLS[:, gb + h:gb + h + 1]).then_inc(l_abs, 1)
            act.wait_ge(l_abs, GH)
            act.activation(BT[:], BT[:], ACT.Exp, scale=-1.0).then_inc(l_abs, 1)
            act.wait_ge(l_abs, GH + 1)
            act.activation(BT[:], BT[:], ACT.Ln, bias=1.0).then_inc(l_ln, 1)
            with act.Fori(0, 2) as i:
                for j in range(4):
                    act.wait_ge(tile_done, tile_no(GK + 1, i, j, 12))
                    act.activation(GQK[:, j, :], bank(j), ACT.Copy).then_inc(g_raw, 1)
                    split_hi(GK + 4, i, j, 12)

                def decays(hh):
                    n = 2 * i + hh
                    act.activation(EB[:], BT[:, n, :], ACT.Exp, scale=1.0 / TAU).then_inc(g_ex, 1)
                    act.activation(EN[:], BT[:, n, :], ACT.Exp, scale=-1.0 / TAU).then_inc(g_ex, 1)
                    act.activation(DEC[:, hh, :].unsqueeze(2), BT[:, n, :].rearrange("p (n c) -> p n c", c=CH)[:, :, CH - 1:CH],
                                   ACT.Exp, scale=1.0 / TAU).then_inc(g_ex, 1)

                def operands(hh):
                    n = 2 * i + hh
                    act.wait_ge(g_e, 4 * i + (2 * hh + 1))
                    act.activation(QDH[hh][:], E[:, 0, :], ACT.Copy).then_inc(g_hi, 1)
                    act.wait_ge(g_e, 4 * i + (2 * hh + 2))
                    if hh:
                        act.wait_ge(at_mm, n)
                    act.activation(KIH[:], E[:, 1, :], ACT.Copy).then_inc(g_hi, 1)
                    act.wait_ge(kd_d, n + 1)
                    act.activation(SQ[:, 0, :], SQ[:, 0, :], ACT.Exp, scale=1.0 / TAU).then_inc(kd_x, 1)

                def attention(hh):
                    n = 2 * i + hh
                    act.wait_ge(am_f, n + 1)
                    act.activation(AMH[:], AMF[:], ACT.Copy).then_inc(am_hi, 1)
                    act.wait_ge(kd_t, n + 1)
                    act.activation(KDH[:], bank(1).rearrange("p (k n) -> p k n", n=P), ACT.Copy).then_inc(kd_hi, 1)

                def states(hh):
                    act.wait_ge(st_f, 2 * i + (hh + 1))
                    act.activation(SH[:], SALL[:], ACT.Copy).then_inc(st_hi, 1)

                def squares(hh):
                    for x in range(2):
                        act.wait_ge(go_mm, 4 * i + (2 * hh + x + 1))
                        act.activation(SQ[:, x, :], bank(2 + x), ACT.Square).then_inc(go_sq, 1)

                def out_gate(j, b):
                    act.wait_ge(tile_done, tile_no(GK + 9, i, j, 12))
                    act.activation(SG[:, 4 * i + j, :], bank(b), ACT.Copy).then_inc(y_s, 1)
                    split_hi(GK + 12, i, j, 12)

                def root_silu(hh):
                    n = 2 * i + hh
                    act.wait_ge(go_ss, n + 1)
                    if hh:
                        act.wait_ge(y_e, 4 * i + 2)
                    act.activation(E[:, 0, :], bank(4 if hh else 1), ACT.Sqrt, scale=1.0 / DV, bias=EPST[:]).then_inc(go_rt, 1)
                    act.activation(SG[:, bass.ds(4 * i + 2 * hh, 2), :], SG[:, bass.ds(4 * i + 2 * hh, 2), :], ACT.Silu).then_inc(g_si, 1)

                act.wait_ge(b_done, GH)
                decays(0)
                operands(0)
                for m in range(TT):
                    act.wait_ge(tile_done, tile_no(GK + 5, i, m, 12))
                    act.activation(GVH[:, m, :], bank(4 + m), ACT.Copy).then_inc(gv_hi, 1)
                for j in range(4):
                    split_hi(GK + 8, i, j, 12)
                attention(0)
                decays(1)
                operands(1)
                out_gate(0, 2)
                states(0)
                out_gate(1, 0)
                attention(1)
                squares(0)
                out_gate(2, 0)
                root_silu(0)
                states(1)
                out_gate(3, 0)
                squares(1)
                root_silu(1)
            for c in range(KC):
                act.wait_ge(y_e, c + 1)
                act.activation(YH[:, c, :], SG[:, c, :], ACT.Copy).then_inc(y_hi, 1)
            with act.Fori(0, 2) as i:
                for j in range(4):
                    act.wait_ge(tile_done, tile_no(GG + 1, i, j))
                    act.activation(GSIG[:, 4 * i + j, :], bank(j), ACT.Sigmoid).then_inc(gg_s, 1)
                    split_hi(GG + 4, i, j)
            with act.Fori(0, 2) as i:
                for j in range(4):
                    c = 4 * i + j
                    act.wait_ge(tile_done, tile_no(BG + 1, i, j))
                    split_hi(BG + 4, i, j)
                    act.wait_ge(x_e, c + 1)
                    act.activation(UH[:, c, :], E[:, j % 2, :], ACT.Copy).then_inc(x_hi, 1)
            square_steps(3, WO)
            root(3, 4)
            u_hi(3)

            def quarter(i):
                t0 = FF + 48 * (i is None)
                at8 = lambda k: 24 + k if i is None else 8 * i + k
                for b in range(8):
                    j = b % 4
                    act.wait_ge(tile_done, tile_no(t0 + (b // 4) * 4 + 1, i, j, 16))
                    if b >= 2:
                        act.wait_ge(f_ylo, at8(b - 1))
                    act.activation(E[:, b % 2, :], bank(j), ACT.Relu).then_inc(f_r, 1)
                    split_hi(t0 + (b // 4) * 4 + 4, i, j, 16)
                    act.wait_ge(f_r, at8(b + 1))
                    act.activation(YH[:, b, :], E[:, b % 2, :], ACT.Square).then_inc(f_sq, 1)
                act.wait_ge(f_ylo, at8(8))
                for b in range(8 if i is not None else 4):
                    j = b % 4
                    act.wait_ge(tile_done, tile_no(t0 + 8 + (b // 4) * 4 + 1, i, j, 16))
                    split_hi(t0 + (b // 4) * 4 + 12, i, j, 16)

            with act.Fori(0, 3) as i:
                quarter(i)
            quarter(None)

            for m in range(8):
                act.wait_ge(out_t, m + 1)
                act.activation(OUT[:, m % 4, (m // 4) * T:(m // 4 + 1) * T], bank(m), ACT.Copy).then_inc(out_c, 1)

        @block.vector
        def _(v):
            steps = Steps(link_s)

            def link(ins):
                ins.then_inc(link_s, 1)
                steps.k += 1
                v.wait_ge(link_s, steps.now())

            v.memset(ONES[:], 1.0).then_inc(ones_set, 1)
            v.memset(EPST[:], EPS).then_inc(ones_set, 1)
            v.memset(RSC[:], 0.0).then_inc(ones_set, 1)
            v.wait_ge(cols_t, 1)
            v.tensor_copy(COLS[:, 0:NROWS], bank(7, NROWS)).then_inc(cols_done, 1)
            v.wait_ge(cols_done, 1)
            v.wait_ge(row_ss, 7)
            v.reciprocal(RSC[:, 0:6], RSC[:, 0:6]).then_inc(row_rstd, 1)
            v.wait_ge(row_rstd, 1)
            v.wait_ge(x_t, KC)
            for m in range(TT):
                v.tensor_scalar(XTOK[:, m, :], XTOK[:, m, :], RSC[:, m:m + 1], None, ALU.mult).then_inc(x_scaled, 1)
            for m in range(TC // P):
                v.tensor_scalar(CTOK[:, m, :], CTOK[:, m, :], RSC[:, TT + m:TT + m + 1], None, ALU.mult).then_inc(x_scaled, 1)
            v.wait_ge(bias_mm, 1)
            v.wait_ge(s_t5, 48)
            v.tensor_tensor(BROW[:], PB[0:MH, 4 * T:4 * T + TOEP], MROW[:], ALU.add).then_inc(bias_row, 1)
            b0 = ROW["b_ada"]
            v.wait_ge(ada_t, 4)
            mod = bank(7, 32).rearrange("p (c n) -> p c n", n=2)
            v.tensor_tensor(ADAL[0][:, 0:16], mod[:, 0:16, 0], COLS[:, b0:b0 + 16], ALU.add)
            link(v.tensor_tensor(ADAC[:], mod[:, 0:16, 1], COLS[:, b0:b0 + 16], ALU.add))
            g0 = ROW["norm_g"]
            v.scalar_tensor_tensor(MULL[0][:], ADAL[0][:, 8:16], 1.0, COLS[:, g0:g0 + 8], ALU.add, ALU.mult)
            link(v.scalar_tensor_tensor(MULC[:], ADAC[:, 8:16], 1.0, COLS[:, g0:g0 + 8], ALU.add, ALU.mult))

            for n in range(2 * KC + 1):
                if n < 2 * KC:
                    c, lat = n % KC, n < KC
                    mul, add = (MULL[0], ADAL[0]) if lat else (MULC, ADAC)
                    v.wait_ge(xn_t, n + 1)
                    if n >= 2:
                        v.wait_ge(u0_lo, n - 1)
                    v.tensor_scalar(E[:, n % 2, 0:T if lat else TC], bank(c % 4) if lat else bank(4 + c % 2, TC),
                                    mul[:, c:c + 1], add[:, c:c + 1], ALU.mult, ALU.add).then_inc(u0_e, 1)
                if n >= 1:
                    m = n - 1
                    c, lat = m % KC, m < KC
                    hi, lo = (UH, UL) if lat else (UCH, UCL)
                    v.wait_ge(u0_hi, n)
                    v.tensor_tensor(lo[:, c, :], E[:, m % 2, 0:T if lat else TC], f(hi[:, c, :]), ALU.subtract).then_inc(u0_lo, 1)
            swap = [16 + x for x in range(16)] + list(range(16))

            def rotate(out, src, tmp):
                v.tensor_tensor(out, src, COS[:], ALU.mult)
                link(v.stream_shuffle(tmp, src, swap))
                link(v.tensor_tensor(tmp, tmp, SIN[:], ALU.mult))
                return v.tensor_tensor(out, out, tmp, ALU.add)

            link(v.tensor_scalar(QGAIN[:], COLS[:, ROW["q_norm"]:ROW["q_norm"] + 1], MD ** -0.5, None, ALU.mult))

            def modulation(r):
                v.wait_ge(s_adaw[r % 2], 16 * (2 + r // 2 + 1))
                if r >= 3:
                    v.wait_ge(ada_mm, 4 + r - 2)
                acc, w = AACC[r % 3][:], AD[0] if r == 1 else AB[r % 2]
                link(v.tensor_scalar(acc, w[:, 0, :], CACT[:, 0, 0:1], None, ALU.mult))
                for k in range(1, KC):
                    ins = v.scalar_tensor_tensor(acc, w[:, k, :], CACT[:, k, 0:1], acc, ALU.mult, ALU.add)
                    if k < KC - 1:
                        link(ins)
                ins.then_inc(ada_used, 1)

            for r in range(3):
                modulation(r)

            v.wait_ge(s_rope, 32)
            v.wait_ge(tile_done, 4)
            rotate(KP[:, TC:TK], bank(3)[0:ROPE, :], E[0:ROPE, 0, :]).then_inc(a_n, 1)
            v.wait_ge(a_sqrt, 1)
            link(v.reciprocal(RQ[:], RQ[:]))
            gq, gk = ROW["g_qa"], ROW["g_kva"]
            v.scalar_tensor_tensor(CQ[:, 0, :], CQ[:, 0, :], COLS[:, gq:gq + 1], RQ[:], ALU.mult, ALU.mult)
            v.scalar_tensor_tensor(CQ[:, 1, :], CQ[:, 1, :], COLS[:, gq + 1:gq + 2], RQ[:], ALU.mult, ALU.mult).then_inc(a_n, 1)
            v.wait_ge(a_sqrt, 2)
            link(v.reciprocal(RKV[:], RKV[:]))
            v.scalar_tensor_tensor(CK[:], CK[:], COLS[:, gk:gk + 1], RKV[:], ALU.mult, ALU.mult).then_inc(a_n, 1)
            for n, (lo, hi, src) in enumerate(((KPL, KPH, KP), (CQL, CQH, CQ), (CKL, CKH, CK))):
                v.wait_ge(a_hi, n + 1)
                v.tensor_tensor(lo[:], src[:], f(hi[:]), ALU.subtract).then_inc(a_lo, 1)

            for r in range(3, 8):
                modulation(r)
            v.wait_ge(ada_mm, 12)
            mod = bank(5, 64).rearrange("p (c n) -> p c n", n=2)
            v.tensor_tensor(ADAL[0][:, 16:24], mod[:, 0:8, 0], COLS[:, b0 + 16:b0 + 24], ALU.add)
            link(v.tensor_tensor(ADAL[1][:], mod[:, 8:32, 0], COLS[:, b0 + 24:b0 + 48], ALU.add))
            link(v.scalar_tensor_tensor(MULL[1][:], ADAL[1][:, 8:16], 1.0, COLS[:, g0 + 8:g0 + 16], ALU.add, ALU.mult))

            with v.Fori(0, 2) as i:
                steps.loop(i, 4 * 10)

                def unit(j, u):
                    par = j % 2
                    v.wait_ge(un_hi, UPR * i + unit_no(j, u))
                    if u == 0:
                        v.tensor_tensor(QNL[:, par, :], bank(0), f(QNH[:, par, :]), ALU.subtract).then_inc(un_lo, 1)
                    elif u == 1:
                        v.tensor_tensor(QPL[:, par, :], QPF[:], f(QPH[:, par, :]), ALU.subtract).then_inc(un_lo, 1)
                    elif u == 2:
                        v.tensor_tensor(KNL[par][:, TC:TK], bank(0), f(KNH[par][:, TC:TK]), ALU.subtract).then_inc(un_lo, 1)
                    elif u == 3:
                        v.tensor_tensor(KNL[par][:, 0:TC], bank(0, TC), f(KNH[par][:, 0:TC]), ALU.subtract).then_inc(un_lo, 1)
                    else:
                        blocks, n = (slice(0, 4), T) if u == 4 else (slice(4, 6), TC)
                        v.tensor_tensor(VAL[:, blocks, :], bank(0, n).rearrange("p (k n) -> p k n", n=P), f(VAH[:, blocks, :]), ALU.subtract)\
                            .then_inc(un_lo, 1)

                def scale(j, q):
                    n, par = 16 * i + (4 * j + q), q % 2
                    v.wait_ge(s_exp, n + 1)
                    link(v.reciprocal(PSUM_[:, 2 + par:3 + par], PSUM_[:, par:par + 1]))
                    v.tensor_scalar(PA[:, par, :], PA[:, par, :], PSUM_[:, 2 + par:3 + par], None, ALU.mult).then_inc(s_scaled, 1)

                def turned(j, q):
                    n = 16 * i + (4 * j + q)
                    v.wait_ge(t_hi, n + 1)
                    v.tensor_tensor(PTL[:, :, q * P:(q + 1) * P], PB[:, 2 * T:2 * T + TK].rearrange("p (k n) -> p k n", n=P),
                                    f(PTH[:, :, q * P:(q + 1) * P]), ALU.subtract).then_inc(t_lo, 1)

                def top(j, q):
                    n, par = 16 * i + (4 * j + q), q % 2
                    v.wait_ge(s_mm, n + 1)
                    link(v.reduce_max(NMAX[:, 2 + par:3 + par], PB[:, (4 + 2 * par) * T:(4 + 2 * par) * T + TK], AX))
                    v.tensor_scalar(NMAX[:, par:par + 1], NMAX[:, 2 + par:3 + par], -MLA_SCALE, None, ALU.mult).then_inc(s_max, 1)

                def rope(j):
                    v.wait_ge(un_raw, 4 * i + (j + 1))
                    rotate(QPF[:], QPR[:], SQ[0:ROPE, 0, :]).then_inc(un_e, 1)

                def output(j):
                    v.wait_ge(o_mm, 4 * i + (j + 1))
                    v.tensor_tensor(E[:, 1, :], bank(1), SG[:, 4 * i + j, :], ALU.mult).then_inc(o_e, 1)

                def output_lo(j):
                    v.wait_ge(o_hi, 4 * i + (j + 1))
                    v.tensor_tensor(UL[:, 4 * i + j, :], E[:, 1, :], f(UH[:, 4 * i + j, :]), ALU.subtract).then_inc(o_lo, 1)

                rope(0)
                for u in first_units:
                    unit(0, u)
                top(0, 0)
                scale(0, 0)
                top(0, 1)
                scale(0, 1)
                for j in range(4):
                    nxt = j < 3
                    top(j, 2)
                    if nxt:
                        rope(j + 1)
                        unit(j + 1, 1)
                    if j:
                        output(j - 1)
                    if nxt:
                        unit(j + 1, 0)
                    turned(j, 0)
                    if nxt:
                        unit(j + 1, 2)
                    scale(j, 2)
                    top(j, 3)
                    if nxt:
                        unit(j + 1, 3)
                    turned(j, 1)
                    scale(j, 3)
                    if j:
                        output_lo(j - 1)
                    if nxt:
                        top(j + 1, 0)
                    unit(j, 4)
                    turned(j, 2)
                    if nxt:
                        scale(j + 1, 0)
                        top(j + 1, 1)
                    unit(j, 5)
                    turned(j, 3)
                    if nxt:
                        scale(j + 1, 1)
                output(3)
                output_lo(3)
            steps.leave(2)

            def residual(n, t0, gate):
                with v.Fori(0, 2) as i:
                    for j in range(4):
                        c = 4 * i + j
                        v.wait_ge(tile_done, tile_no(t0 + 1, i, j))
                        v.scalar_tensor_tensor(HT[:, c, :], bank(j), gate[:, bass.ds(4 * i + (16 + j), 1)], HT[:, c, :], ALU.mult, ALU.add)\
                            .then_inc(norm["h"], 1)

            def rstd(n):
                v.wait_ge(norm["sqrt"], so_far(n, "sqrt") + 1)
                v.reciprocal(RS[:], RS[:]).then_inc(norm["rstd"], 1)
                v.wait_ge(norm["rstd"], so_far(n, "rstd") + 1)

            residual(0, MO, ADAL[0])
            rstd(0)
            for c in range(KC + 1):
                if c < KC:
                    if c >= 2:
                        v.wait_ge(norm["lo"], so_far(0, "lo") + c - 1)
                    v.scalar_tensor_tensor(E[:, c % 2, :], HT[:, c, :], MULL[1][:, c:c + 1], RS[:], ALU.mult, ALU.mult).then_inc(norm["e"], 1)
                if c >= 1:
                    m = c - 1
                    v.wait_ge(norm["hi"], so_far(0, "hi") + c)
                    v.scalar_tensor_tensor(UL[:, m, :], E[:, m % 2, :], ADAL[1][:, m:m + 1], f(UH[:, m, :]), ALU.add, ALU.subtract)\
                        .then_inc(norm["lo"], 1)
            v.wait_ge(df_hi, 1)
            v.tensor_tensor(CDL[:], CDR[:], f(CDH[:]), ALU.subtract).then_inc(df_lo, 1)
            v.wait_ge(df_hi, 2)
            v.tensor_tensor(DFL[:], DFR[:], f(DFH[:]), ALU.subtract).then_inc(df_lo, 1)
            with v.Fori(0, 2) as i:
                def z_in(j):
                    v.wait_ge(z_raw, 4 * i + (j + 1))
                    if j >= 2:
                        v.wait_ge(z_lo, 4 * i + (j - 1))
                    v.tensor_tensor(ZF[:, j % 2, 0:HALF], ZR[:, j % 2, 0:HALF], ZR[:, j % 2, HALF:T], ALU.add)
                    v.tensor_tensor(ZF[:, j % 2, HALF:T], ZR[:, j % 2, 0:HALF], ZR[:, j % 2, HALF:T], ALU.subtract).then_inc(z_fold, 1)
                    v.wait_ge(z_hi, 4 * i + (j + 1))
                    v.tensor_tensor(ZL[:, j % 2, :], ZF[:, j % 2, :], f(ZH[:, j % 2, :]), ALU.subtract).then_inc(z_lo, 1)

                def a_in(j):
                    v.wait_ge(d_hi, 4 * i + (j + 1))
                    v.tensor_tensor(AL[:, j % 2, :], PB[:, 4 * T:6 * T], f(AH[:, j % 2, :]), ALU.subtract).then_inc(d_lo, 1)

                def y_in(j):
                    v.wait_ge(f_mm, 4 * i + (j + 1))
                    if j >= 2:
                        v.wait_ge(f_lo, 4 * i + (j - 1))
                    two = "p (t two) -> p two t"
                    v.tensor_tensor(E[:, j % 2, :].rearrange(two, two=2), bank(6 + j % 2).rearrange("p (two t) -> p two t", two=2),
                                    SG[:, 4 * i + j, :].rearrange(two, two=2), ALU.mult).then_inc(f_e, 1)
                    v.wait_ge(f_hi, 4 * i + (j + 1))
                    v.tensor_tensor(YL[:, 4 * i + j, :], E[:, j % 2, :], f(YH[:, 4 * i + j, :]), ALU.subtract).then_inc(f_lo, 1)

                z_in(0)
                z_in(1)
                a_in(0)
                z_in(2)
                a_in(1)
                y_in(0)
                z_in(3)
                a_in(2)
                y_in(1)
                a_in(3)
                y_in(2)
                y_in(3)
            residual(1, FO, ADAL[1])
            rstd(1)
            fg = ROW["final_g"]
            for c in range(KC):
                v.scalar_tensor_tensor(HT[:, c, :], HT[:, c, :], COLS[:, fg + c:fg + c + 1], RS[:], ALU.mult, ALU.mult).then_inc(norm["h"], 1)

            def u_split(n, gain):
                rstd(n)
                for c in range(KC + 1):
                    if c < KC:
                        if c >= 2:
                            v.wait_ge(norm["lo"], so_far(n, "lo") + c - 1)
                        v.scalar_tensor_tensor(E[:, c % 2, :], HT[:, c, :], COLS[:, gain + c:gain + c + 1], RS[:], ALU.mult, ALU.mult)\
                            .then_inc(norm["e"], 1)
                    if c >= 1:
                        m = c - 1
                        v.wait_ge(norm["hi"], so_far(n, "hi") + c)
                        v.tensor_tensor(UL[:, m, :], E[:, m % 2, :], f(UH[:, m, :]), ALU.subtract).then_inc(norm["lo"], 1)

            u_split(2, ROW["norm1"])
            for m in range(TT):
                v.wait_ge(v_hi, m + 1)
                v.tensor_tensor(VL[:, m, :], bank(m), f(VH[:, m, :]), ALU.subtract).then_inc(v_lo, 1)
            v.wait_ge(s_bias, 16)
            with v.Fori(0, 2) as i:
                steps.loop(i, 32)

                v.wait_ge(q_rt, i + 1)
                v.reciprocal(RROW[:], RROW[:]).then_inc(q_rs, 1)

                def normed(j):
                    v.wait_ge(q_sp, 4 * i + (j + 1))
                    if j >= 2:
                        v.wait_ge(q_lo, 4 * i + (j - 1))
                    v.tensor_scalar(E[:, j % 2, :], bank(j), QGAIN[:] if j < 2 else COLS[:, ROW["k_norm"]:ROW["k_norm"] + 1], None, ALU.mult)\
                        .then_inc(q_g, 1)
                    v.wait_ge(q_g, 4 * i + (j + 1))
                    v.tensor_tensor(E[:, j % 2, :], bank(5 - j % 2), E[:, j % 2, :], ALU.mult).then_inc(q_e, 1)

                def low(j):
                    v.wait_ge(q_hi, 4 * i + (j + 1))
                    v.tensor_tensor(QKL[:, j, :], E[:, j % 2, :], f(QKH[:, j, :]), ALU.subtract).then_inc(q_lo, 1)

                normed(0)
                normed(1)
                low(0)
                normed(2)
                low(1)
                normed(3)
                low(2)
                low(3)

                def top(m, q):
                    x, w = (4 * m + q) % 3, (q + 1) * P
                    v.wait_ge(s_mm, 16 * i + (M0 + 4 * m + q + 1))
                    link(v.tensor_tensor(MP[:, x, 0:w], bank(4 + q % 2, w), BIAS[:, 4 * i + m, T - w:T], ALU.add))
                    v.reduce_max(MSTAT[:, x:x + 1], MP[:, x, 0:w], AX, negate=True).then_inc(s_max, 1)

                def scale(m, q):
                    x, w = (4 * m + q) % 3, (q + 1) * P
                    v.wait_ge(s_exp, 16 * i + (M0 + 4 * m + q + 1))
                    link(v.reciprocal(NMAX[:, x:x + 1], MSTAT[:, 3 + x:4 + x]))
                    v.tensor_scalar(MP[:, x, 0:w], MP[:, x, 0:w], NMAX[:, x:x + 1], None, ALU.mult).then_inc(s_scaled, 1)

                def turned(m, q):
                    v.wait_ge(t_hi, 16 * i + (M0 + 4 * m + q + 1))
                    s = slice(q * P, (q + 1) * P)
                    v.tensor_tensor(MTL[:, 0:q + 1, s], bank(6 + q % 2, (q + 1) * P).rearrange("p (k n) -> p k n", n=P),
                                    f(MTH[:, 0:q + 1, s]), ALU.subtract).then_inc(t_lo, 1)

                def output(m):
                    rows = slice(MD * (m % 2), MD * (m % 2 + 1))
                    v.wait_ge(o_hi, 4 * i + (HEADS + m + 1))
                    v.tensor_tensor(YL[rows, 2 * i + m // 2, :], bank(m % 2)[rows, :], f(YH[rows, 2 * i + m // 2, :]), ALU.subtract)\
                        .then_inc(o_lo, 1)

                top(0, 0)
                top(0, 1)
                scale(0, 0)
                for m in range(4):
                    top(m, 2)
                    scale(m, 1)
                    if m:
                        output(m - 1)
                    turned(m, 0)
                    top(m, 3)
                    scale(m, 2)
                    turned(m, 1)
                    if m < 3:
                        top(m + 1, 0)
                    scale(m, 3)
                    turned(m, 2)
                    if m < 3:
                        top(m + 1, 1)
                        scale(m + 1, 0)
                    turned(m, 3)
                output(3)
            steps.leave(2)
            v.wait_ge(l_hi, 1)
            v.tensor_tensor(LWL[:], LWR[:], f(LWH[:]), ALU.subtract).then_inc(l_lo, 1)
            for j in range(4):
                v.wait_ge(tile_done, BM + j + 1)
                v.wait_ge(gm_s, KC + 2 * j + 2)
                v.tensor_tensor(MX[:, 2 * j, :], MX[:, 2 * j, :], bank(j), ALU.mult)
                v.tensor_tensor(MX[:, 2 * j + 1, :], MX[:, 2 * j + 1, :], bank(4 + j), ALU.mult).then_inc(bm_e, 1)
            link(v.memset(RST[:], 1.0))
            link(v.memset(RST[:].rearrange("p (n c) -> p n c", c=CH)[:, :, 0:1], 0.0))
            v.memset(AMF[:], 0.0).then_inc(on_done, 1)
            gb = ROW["gate_bias"]
            for h in range(GH):
                v.wait_ge(l_up, h + 1)
                v.tensor_scalar(MN[:, h, :], bank(h), COLS[:, gb + h:gb + h + 1], 0.0, ALU.add, ALU.min).then_inc(l_min, 1)
            v.wait_ge(l_ln, 1)
            v.wait_ge(l_min, GH)
            link(v.tensor_tensor(MN[:], MN[:], BT[:], ALU.subtract))
            for h in range(GH):
                v.tensor_tensor_scan(BT[:, h, :], RST[:], MN[:, h, :], 0.0, ALU.mult, ALU.add).then_inc(b_done, 1)
            v.wait_ge(s_mask, 16)
            with v.Fori(0, 2) as i:
                steps.loop(i, 2 * 7)

                def operands(hh):
                    n = 2 * i + hh
                    v.wait_ge(g_ex, 6 * i + (3 * hh + 1))
                    v.scalar_tensor_tensor(E[:, 0, :], GQK[:, hh, :], DK ** -0.5, EB[:], ALU.mult, ALU.mult).then_inc(g_e, 1)
                    v.wait_ge(g_ex, 6 * i + (3 * hh + 2))
                    v.tensor_tensor(E[:, 1, :], GQK[:, 2 + hh, :], EN[:], ALU.mult).then_inc(g_e, 1)
                    b3 = BT[:, n, :].rearrange("p (n c) -> p n c", c=CH)
                    v.tensor_tensor(SQ[:, 0, :].rearrange("p (n c) -> p n c", c=CH), b3[:, :, CH - 1:CH].to_broadcast([P, NCH, CH]), b3,
                                    ALU.subtract).then_inc(kd_d, 1)
                    v.wait_ge(g_hi, 4 * i + (2 * hh + 1))
                    v.tensor_tensor(QDL[hh][:], E[:, 0, :], f(QDH[hh][:]), ALU.subtract).then_inc(g_lo, 1)
                    v.wait_ge(g_hi, 4 * i + (2 * hh + 2))
                    v.tensor_tensor(KIL[:], E[:, 1, :], f(KIH[:]), ALU.subtract).then_inc(g_lo, 1)
                    v.wait_ge(kd_x, n + 1)
                    v.tensor_tensor(SQ[:, 1, :], GQK[:, 2 + hh, :], SQ[:, 0, :], ALU.mult).then_inc(kd_e, 1)

                def attention(hh):
                    n = 2 * i + hh
                    v.wait_ge(at_mm, n + 1)
                    v.tensor_copy(DUMMY[:, 0:1], EPST[:])
                    v.copy_predicated(AMF[:].rearrange("p (k n) -> p k n", n=P),
                                      CMASK[:].unsqueeze(1).to_broadcast([P, TT, P]),
                                      bank(0).rearrange("p (k n) -> p k n", n=P)).then_inc(am_f, 1)
                    v.wait_ge(am_hi, n + 1)
                    v.tensor_tensor(AML[:], AMF[:], f(AMH[:]), ALU.subtract).then_inc(am_lo, 1)
                    v.wait_ge(kd_hi, n + 1)
                    v.tensor_tensor(KDL[:], bank(1).rearrange("p (k n) -> p k n", n=P), f(KDH[:]), ALU.subtract).then_inc(kd_lo, 1)

                def states(hh):
                    n = 2 * i + hh
                    v.wait_ge(kv_mm, n + 1)
                    ins = v.tensor_copy(SALL[:, 0, :], kv_bank(0))
                    for c in range(1, NCH - 1):
                        link(ins)
                        ins = v.scalar_tensor_tensor(SALL[:, c, :], SALL[:, c - 1, :], DEC[:, hh, c:c + 1], kv_bank(c), ALU.mult, ALU.add)
                    ins.then_inc(st_f, 1)

                def states_lo(hh):
                    v.wait_ge(st_hi, 2 * i + (hh + 1))
                    v.tensor_tensor(SL[:], SALL[:], f(SH[:]), ALU.subtract).then_inc(st_lo, 1)

                def normed(hh):
                    n = 2 * i + hh
                    v.wait_ge(go_rt, n + 1)
                    link(v.reciprocal(E[:, 0, :], E[:, 0, :]))
                    og = ROW["out_norm"]
                    tmp = (E[:, 1, :], E[:, 0, :])
                    for x in range(2):
                        v.scalar_tensor_tensor(tmp[x], bank(2 + x), COLS[:, og + x:og + x + 1], E[:, 0, :], ALU.mult, ALU.mult).then_inc(on_done, 1)
                    v.wait_ge(on_done, 4 * i + (2 * hh + 3))
                    v.wait_ge(g_si, n + 1)
                    for x in range(2):
                        c = 4 * i + 2 * hh + x
                        v.tensor_tensor(SG[:, c, :], SG[:, c, :], tmp[x], ALU.mult).then_inc(y_e, 1)

                v.wait_ge(g_raw, 4 * i + 4)
                operands(0)
                for m in range(TT):
                    v.wait_ge(gv_hi, 4 * i + (m + 1))
                    v.tensor_tensor(GVL[:, m, :], bank(4 + m), f(GVH[:, m, :]), ALU.subtract).then_inc(gv_lo, 1)
                attention(0)
                operands(1)
                states(0)
                states_lo(0)
                attention(1)
                states(1)
                normed(0)
                states_lo(1)
                normed(1)
                v.wait_ge(y_e, 4 * i + 4)
            steps.leave(2)
            for c in range(KC):
                v.wait_ge(y_hi, c + 1)
                v.tensor_tensor(YL[:, c, :], SG[:, c, :], f(YH[:, c, :]), ALU.subtract).then_inc(y_lo, 1)
            with v.Fori(0, 2) as i:
                steps.loop(i, 4)
                for j in range(4):
                    c = 4 * i + j
                    v.wait_ge(tile_done, tile_no(BG + 1, i, j))
                    v.wait_ge(gg_s, c + 1)
                    link(v.tensor_tensor(E[:, j % 2, :], bank(j), GSIG[:, c, :], ALU.mult))
                    v.tensor_tensor(E[:, j % 2, :], E[:, j % 2, :], MX[:, c, :], ALU.add).then_inc(x_e, 1)
                    v.wait_ge(x_hi, c + 1)
                    v.tensor_tensor(UL[:, c, :], E[:, j % 2, :], f(UH[:, c, :]), ALU.subtract).then_inc(x_lo, 1)
            steps.leave(2)
            with v.Fori(0, 2) as i:
                for j in range(4):
                    c = 4 * i + j
                    v.wait_ge(tile_done, tile_no(WO + 1, i, j))
                    v.tensor_tensor(HT[:, c, :], bank(j), HT[:, c, :], ALU.add).then_inc(norm["h"], 1)
            u_split(3, ROW["norm2"])

            def quarter(i):
                t0 = FF + 48 * (i is None)
                at8 = lambda k: 24 + k if i is None else 8 * i + k
                for b in range(8):
                    v.wait_ge(f_r, at8(b + 1))
                    link(v.tensor_tensor(SQ[:, b % 2, :], E[:, b % 2, :], E[:, b % 2, :], ALU.mult))
                    v.wait_ge(f_sq, at8(b + 1))
                    v.tensor_tensor(YL[:, b, :], SQ[:, b % 2, :], f(YH[:, b, :]), ALU.subtract).then_inc(f_ylo, 1)
                for b in range(8):
                    v.wait_ge(tile_done, tile_no(t0 + 8 + (b // 4) * 4 + 1, i, b % 4, 16))
                    v.tensor_tensor(HT[:, b, :], bank(b % 4), HT[:, b, :], ALU.add).then_inc(f_h, 1)

            with v.Fori(0, 3) as i:
                steps.loop(i, 8)
                quarter(i)
            steps.leave(3)
            quarter(None)

        @block.tensor
        def _(pe):
            def three(out, ah, al, bh, bl, first, last):
                pe.matmul(out, ah, bh, start=first, stop=False)
                pe.matmul(out, ah, bl, start=False, stop=False)
                return pe.matmul(out, al, bh, start=False, stop=last)

            def wsl(w, j, k):
                return w[:, j, k * P:(k + 1) * P]

            def product(t, j, xh, xl, n=KC, ready=None, before=0):
                pe.wait_ge(lo_done, t + 1)
                for k in range(n):
                    if ready is not None:
                        pe.wait_ge(ready, before + (k + 1))
                    mm = three(bank(j), wsl(WH, j, k), wsl(WL, j, k), xh[:, k, :], xl[:, k, :], k == 0, k == n - 1)
                mm.then_inc(tile_done, 1)

            def linear(t0, xh, xl, ready=None, before=0):
                with pe.Fori(0, 2) as i:
                    for j in range(4):
                        product(tile_no(t0, i, j), j, xh, xl, ready=ready if j == 0 else None, before=before)

            pe.wait_ge(s_const, 48)
            pe.wait_ge(s_vec, 16 * (len(VECS) + 2))
            pe.transpose(bank(7, NROWS), VROWS[:], IDENT[0:NROWS, 0:NROWS]).then_inc(cols_t, 1)
            pe.wait_ge(s_t5, 48)
            pe.matmul(PB[0:MH, 4 * T:5 * T], T5[:], HOT[:, 0:T], start=True, stop=True)
            pe.matmul(PB[0:MH, 5 * T:5 * T + P], T5[:], HOT[:, T:TOEP], start=True, stop=True).then_inc(bias_mm, 1)
            pe.wait_ge(s_x, 16)
            for c in range(KC):
                if c >= 4:
                    pe.wait_ge(x_copied, c - 3)
                for m in range(TT):
                    mm = pe.transpose(bank(c % 4, P, m * P), XTOK[:, m, c * P:(c + 1) * P], IDENT[:])
                mm.then_inc(x_t, 1)

            def ada(q):
                if q < 4:
                    pe.wait_ge(s_adaw[q % 2], 16 * (q // 2 + 1))
                    if q >= 1:
                        pe.wait_ge(ada_row, q)
                    for k in range(KC):
                        mm = pe.matmul(bank(6)[0:2, :], CACT[:, k, :], AD[q % 2][:, k, :], start=k == 0, stop=k == KC - 1)
                    mm.then_inc(ada_mm, 1)
                if q >= 1:
                    pe.wait_ge(ada_row, q)
                    for b in range(4):
                        mm = pe.transpose(bank(7, 2, 2 * (4 * (q - 1) + b)), AROW[:, q - 1, b * P:(b + 1) * P], IDENT[0:2, 0:2])
                    mm.then_inc(ada_t, 1)

            pe.wait_ge(cact_done, 2)
            for q in range(5):
                ada(q)
            pe.wait_ge(x_scaled, 4)
            pe.wait_ge(x_copied, KC)
            for c in range(KC):
                if c >= 4:
                    pe.wait_ge(u0_e, c - 3)
                for m in range(TT):
                    mm = pe.transpose(bank(c % 4, P, m * P), XTOK[:, m, c * P:(c + 1) * P], IDENT[:])
                mm.then_inc(xn_t, 1)

            def turn_ctx(c):
                if c == 0:
                    pe.wait_ge(x_scaled, 6)
                    pe.wait_ge(bias_row, 1)
                if c >= 2:
                    pe.wait_ge(u0_e, KC + c - 1)
                for m in range(TC // P):
                    mm = pe.transpose(bank(4 + c % 2, P, m * P), CTOK[:, m, c * P:(c + 1) * P], IDENT[:])
                mm.then_inc(xn_t, 1)

            pe.wait_ge(u0_e, KC)
            for j in range(4):
                pe.wait_ge(lo_done, j + 1)
                if j == 2:
                    pe.wait_ge(u0_e, 2 * KC)
                for k in range(KC):
                    if j == 0:
                        pe.wait_ge(u0_lo, k + 1)
                    mm = three(bank(j), wsl(WH, j, k), wsl(WL, j, k), UH[:, k, :], UL[:, k, :], k == 0, k == KC - 1)
                    if j < 2 and k % 2 == 1:
                        turn_ctx(4 * j + k // 2)
                if j >= 2:
                    for k in range(KC):
                        pe.wait_ge(u0_lo, KC + k + 1)
                        mm = three(bank(2 + j, TC), wsl(WH, j, k), wsl(WL, j, k), UCH[:, k, :], UCL[:, k, :], k == 0, k == KC - 1)
                mm.then_inc(tile_done, 1)
                if j == 2:
                    for n in range(2):
                        pe.wait_ge(a_sq, n + 1)
                        pe.matmul(bank(6), ONES[:], SQ[:, n, :], start=n == 0, stop=n == 1).then_inc(a_ss, 1)
            pe.wait_ge(a_sq, 3)
            pe.matmul(bank(4, TC, TC), ONES[:], SQ[:, 1, 0:TC], start=True, stop=True).then_inc(a_ss, 1)
            pe.wait_ge(a_sq, 4)
            pe.matmul(bank(7), ONES[:], SQ[:, 0, :], start=True, stop=True).then_inc(a_ss, 1)
            pe.wait_ge(a_raw, 4)
            for r in range(8):
                product(G1 + r, r % 4, UH, UL)
                pe.wait_ge(ada_used, r + 1)
                for b in range(4):
                    mm = pe.matmul(bank(5, 2, 2 * (4 * r + b)), AACC[r % 3][:, b * P:(b + 1) * P], ONES[:, 0:2], start=True, stop=True)
                mm.then_inc(ada_mm, 1)

            pe.wait_ge(a_lo, 3)
            with pe.Fori(0, 2) as i:
                def unit(j, u):
                    if u == first_units[0]:
                        pe.wait_ge(lo_done, tile_no(HD + 1, i, j))
                    if u == 0:
                        pe.wait_ge(un_raw, 4 * i + (j + 1))
                    elif unit_no(j, u) > 1:
                        pe.wait_ge(un_lo, UPR * i + (unit_no(j, u) - 1))
                    wq = lambda w, k, o: w[:, j, 192 * k + o:192 * k + o + P]
                    wk = lambda w, o: w[:, j, 2 * 192 + o:2 * 192 + o + P]
                    if u < 2:
                        for k in range(2):
                            mm = three(bank(0), wq(WH, k, NOPE * u), wq(WL, k, NOPE * u), CQH[:, k, :], CQL[:, k, :], k == 0, k == 1)
                    elif u == 2:
                        mm = three(bank(0), wk(WH, 0), wk(WL, 0), CKH[:, TC:TK], CKL[:, TC:TK], True, True)
                    elif u == 3:
                        mm = three(bank(0, TC), wk(WH, 0), wk(WL, 0), CKH[:, 0:TC], CKL[:, 0:TC], True, True)
                    else:
                        first = 4 * (u - 4)
                        for m in range(first, min(first + 4, TK // P)):
                            s = slice(m * P, (m + 1) * P)
                            mm = three(bank(0, P, (m - first) * P), CKH[:, s], CKL[:, s], wk(WH, P), wk(WL, P), True, True)
                    mm.then_inc(tile_done if u == 5 else un_mm, 1)

                def scores(j, q):
                    n, par = 16 * i + (4 * j + q), q % 2
                    if q == 0:
                        pe.wait_ge(un_lo, UPR * i + unit_no(j, 3))
                    if j or q >= 2:
                        pe.wait_ge(s_exp, n - 1)
                    s = slice(q * P, (q + 1) * P)
                    for b, (k0, k1) in enumerate(((0, T), (T, TK))):
                        out = bank(4 + 2 * par + b, k1 - k0)
                        three(out, QNH[:, j % 2, s], QNL[:, j % 2, s], KNH[j % 2][:, k0:k1], KNL[j % 2][:, k0:k1], True, False)
                        mm = three(out, QPH[:, j % 2, s], QPL[:, j % 2, s], KPH[:, k0:k1], KPL[:, k0:k1], False, True)
                    mm.then_inc(s_mm, 1)

                def turn(j, q):
                    n = 16 * i + (4 * j + q)
                    pe.wait_ge(s_scaled, n + 1)
                    if q >= 1:
                        pe.wait_ge(t_lo, n)
                    for k in range(TK // P):
                        mm = pe.transpose(bank(2, P, k * P), PA[:, q % 2, k * P:(k + 1) * P], IDENT[:])
                    mm.then_inc(t_mm, 1)

                def output(j):
                    pe.wait_ge(un_lo, UPR * i + unit_no(j, 5))
                    pe.wait_ge(t_lo, 16 * i + (4 * j + 4))
                    for k in range(TK // P):
                        mm = three(bank(1), VAH[:, k, :], VAL[:, k, :], PTH[:, k, :], PTL[:, k, :], k == 0, k == TK // P - 1)
                    mm.then_inc(o_mm, 1)

                for u in first_units:
                    unit(0, u)
                scores(0, 0)
                scores(0, 1)
                for j in range(4):
                    nxt = j < 3
                    scores(j, 2)
                    if nxt:
                        unit(j + 1, 1)
                    if j:
                        output(j - 1)
                    if nxt:
                        unit(j + 1, 0)
                    turn(j, 0)
                    if nxt:
                        unit(j + 1, 2)
                    scores(j, 3)
                    if nxt:
                        unit(j + 1, 3)
                    turn(j, 1)
                    if nxt:
                        scores(j + 1, 0)
                    unit(j, 4)
                    turn(j, 2)
                    if nxt:
                        scores(j + 1, 1)
                    unit(j, 5)
                    turn(j, 3)
                output(3)

            linear(MO, UH, UL, ready=o_lo)

            def sums(n, b):
                pe.wait_ge(norm["acc"], so_far(n, "acc") + KC + 2)
                pe.matmul(bank(b), ONES[:], ACC[:], start=True, stop=True).then_inc(norm["ss"], 1)

            sums(0, 4)
            linear(FG, UH, UL, ready=norm["lo"], before=so_far(0, "lo"))
            pe.wait_ge(df_lo, 2)
            with pe.Fori(0, 2) as i:
                def dims(j):
                    pe.wait_ge(z_lo, 4 * i + (j + 1))
                    if j >= 1:
                        pe.wait_ge(d_lo, 4 * i + j)
                    for q in range(4):
                        s = slice(q * P, (q + 1) * P)
                        mm = three(bank(4, 2 * GROUP, 2 * GROUP * q), ZH[:, j % 2, s], ZL[:, j % 2, s], CDH[:], CDL[:], True, True)
                    mm.then_inc(d_mm, 1)

                def toks(j):
                    pe.wait_ge(d_lo, 4 * i + (j + 1))
                    if j >= 2:
                        pe.wait_ge(f_e, 4 * i + (j - 1))
                    for odd in range(2):
                        for k in range(4):
                            q, sine = 2 * odd + k // 2, k % 2
                            s = slice(2 * GROUP * q + GROUP * sine, 2 * GROUP * q + GROUP * (sine + 1))
                            mat = 2 * (2 * odd + sine) + k // 2
                            mm = three(bank(6 + j % 2, HALF, HALF * odd), AH[:, j % 2, s], AL[:, j % 2, s],
                                       DFH[:, mat, :], DFL[:, mat, :], k == 0, k == 3)
                    mm.then_inc(f_mm, 1)

                def lin(j):
                    product(tile_no(FZ, i, j), j, UH, UL)

                lin(0)
                lin(1)
                dims(0)
                lin(2)
                dims(1)
                toks(0)
                lin(3)
                dims(2)
                toks(1)
                dims(3)
                toks(2)
                toks(3)
            linear(FO, YH, YL, ready=f_lo)

            sums(1, 4)
            sums(2, 5)

            def rows_product(t0, m, b, ready=None, before=0):
                s = slice(m * P, (m + 1) * P)
                out = bank(b).rearrange("p (a n) -> p a n", n=P)
                for k in range(KC):
                    if ready is not None:
                        pe.wait_ge(ready, before + k + 1)
                    mm = three(out, UH[:, k, s], UL[:, k, s], WH[:, :, k * P:(k + 1) * P], WL[:, :, k * P:(k + 1) * P],
                               k == 0, k == KC - 1)
                mm.then_inc(tile_done, 1)

            pe.wait_ge(lo_done, MV + 4)
            for m in range(TT):
                rows_product(MV, m, m, ready=norm["lo"] if m == 0 else None, before=so_far(2, "lo"))
            with pe.Fori(0, 2) as i:
                def ss(j):
                    pe.wait_ge(q_sq, 4 * i + (j + 1))
                    pe.matmul(bank(4), HPICK[:, 96 - 32 * j:224 - 32 * j], SQ[:, j % 2, :], start=j == 0, stop=j == 3).then_inc(q_ss, 1)

                def spread(j):
                    if j >= 2:
                        pe.wait_ge(q_e, 4 * i + (j - 1))
                    rows = slice(32 * j, 32 * (j + 1))
                    pe.matmul(bank(5 - j % 2), HSPREAD[rows, :], RROW[rows, :], start=True, stop=True).then_inc(q_sp, 1)

                def gate(j, b):
                    pe.wait_ge(lo_done, tile_no(MQ + 5, i, j, 8))
                    for k in range(KC):
                        mm = three(bank(b), wsl(WH, j, k), wsl(WL, j, k), UH[:, k, :], UL[:, k, :], k == 0, k == KC - 1)
                    mm.then_inc(tile_done, 1)

                pe.wait_ge(o_lo, 4 * i + HEADS)
                for j in range(4):
                    product(tile_no(MQ, i, j, 8), j, UH, UL)
                    if j:
                        ss(j - 1)
                ss(3)
                gate(0, 6)
                pe.wait_ge(q_rs, i + 1)
                for j in range(4):
                    spread(j)
                gate(1, 7)

                def scores(m, q):
                    n, w = 16 * i + (M0 + 4 * m + q), (q + 1) * P
                    if m == 0 and q == 0:
                        pe.wait_ge(q_lo, 4 * i + 4)
                    if m or q >= 2:
                        pe.wait_ge(s_max, n - 1)
                    rows = slice(MD * (m % 2), MD * (m % 2 + 1))
                    s = slice(q * P, (q + 1) * P)
                    three(bank(4 + q % 2, w), QKH[rows, m // 2, s], QKL[rows, m // 2, s],
                          QKH[rows, 2 + m // 2, 0:w], QKL[rows, 2 + m // 2, 0:w], True, True).then_inc(s_mm, 1)

                def turn(m, q):
                    n = 16 * i + (M0 + 4 * m + q)
                    pe.wait_ge(s_scaled, n + 1)
                    if m or q >= 2:
                        pe.wait_ge(t_lo, n - 1)
                    for k in range(q + 1):
                        mm = pe.transpose(bank(6 + q % 2, P, k * P), MP[:, (4 * m + q) % 3, k * P:(k + 1) * P], IDENT[:])
                    mm.then_inc(t_mm, 1)

                def output(m):
                    pe.wait_ge(t_lo, 16 * i + (M0 + 4 * m + 4))
                    if m == 0:
                        pe.wait_ge(vs_done, 4 * i + 4)
                    for k in range(TT):
                        mm = three(bank(m % 2, T - k * P, k * P), VSH[:, m // 2, k, :], VSL[:, m // 2, k, :],
                                   MTH[:, k, k * P:T], MTL[:, k, k * P:T], k == 0, k == TT - 1)
                    mm.then_inc(o_mm, 1)

                scores(0, 0)
                scores(0, 1)
                for m in range(4):
                    scores(m, 2)
                    if m:
                        output(m - 1)
                    turn(m, 0)
                    scores(m, 3)
                    turn(m, 1)
                    if m < 3:
                        scores(m + 1, 0)
                    turn(m, 2)
                    if m < 3:
                        scores(m + 1, 1)
                    turn(m, 3)
                    if m % 2 == 0:
                        gate(2 + m // 2, 2 + m // 2)
                output(3)
            def branch(j):
                pe.wait_ge(lo_done, BM + j + 1)
                for o in range(2):
                    for k in range(4):
                        s = slice(2 * P * k + P * o, 2 * P * k + P * (o + 1))
                        mm = three(bank(4 * o + j), WH[:, j, s], WL[:, j, s], YH[:, k, :], YL[:, k, :], k == 0, k == 3)
                mm.then_inc(tile_done, 1)

            pe.wait_ge(o_lo, HEADS + MH)
            branch(0)
            branch(1)
            pe.wait_ge(l_lo, 1)
            for k in range(KC):
                mm = three(bank(7), LWH[:, k, :], LWL[:, k, :], UH[:, k, :], UL[:, k, :], k == 0, k == KC - 1)
            mm.then_inc(l_mm, 1)
            branch(2)
            pe.wait_ge(s_low, 32)
            pe.wait_ge(l_cp, 1)
            branch(3)
            for h in range(GH):
                pe.wait_ge(bm_e, h + 1)
                pe.matmul(bank(h), GUP[:, h * DK:(h + 1) * DK], GLO[:], start=True, stop=True).then_inc(l_up, 1)
            pe.wait_ge(l_abs, GH)
            with pe.Fori(0, 2) as i:
                def attention(hh):
                    n = 2 * i + hh
                    if hh == 0:
                        pe.wait_ge(g_lo, 4 * i + 2)
                    pe.wait_ge(kd_e, n + 1)
                    for k in range(TT):
                        mm = pe.transpose(bank(1, P, k * P), SQ[:, 1, k * P:(k + 1) * P], IDENT[:])
                    mm.then_inc(kd_t, 1)
                    if hh:
                        pe.wait_ge(y_s, 4 * i + 2)
                    for k in range(TT):
                        s = slice(k * P, (k + 1) * P)
                        mm = three(bank(0, P, k * P), KIH[:, s], KIL[:, s], QDH[hh][:, s], QDL[hh][:, s], True, True)
                    mm.then_inc(at_mm, 1)

                def kv(hh):
                    pe.wait_ge(kd_lo, 2 * i + (hh + 1))
                    if hh == 0:
                        pe.wait_ge(gv_lo, 4 * i + 4)
                    for c in range(NCH - 1):
                        rows = slice(CH * (c % 2), CH * (c % 2 + 1))
                        vals = slice(hh * DV, (hh + 1) * DV)
                        mm = three(kv_bank(c), KDH[rows, c // 2, :], KDL[rows, c // 2, :],
                                   GVH[rows, c // 2, vals], GVL[rows, c // 2, vals], True, True)
                    mm.then_inc(kv_mm, 1)

                def inside(hh):
                    n = 2 * i + hh
                    pe.wait_ge(am_lo, n + 1)
                    if hh:
                        pe.wait_ge(on_done, 4 * i + 3)
                    else:
                        pe.wait_ge(y_s, 4 * i + 1)
                    for x in range(2):
                        for k in range(TT):
                            vals = slice(hh * DV + x * P, hh * DV + (x + 1) * P)
                            s = slice(k * P, (k + 1) * P)
                            three(bank(2 + x, P, k * P), GVH[:, k, vals], GVL[:, k, vals], AMH[:, s], AML[:, s], k == 0, False)

                def across(hh):
                    pe.wait_ge(st_lo, 2 * i + (hh + 1))
                    for x in range(2):
                        for c in range(1, NCH):
                            s, vals = slice(c * CH, (c + 1) * CH), slice(x * P, (x + 1) * P)
                            mm = three(bank(2 + x, CH, c * CH), SH[:, c - 1, vals], SL[:, c - 1, vals], QDH[hh][:, s], QDL[hh][:, s],
                                       False, c == NCH - 1)
                        mm.then_inc(go_mm, 1)

                def sums_out(hh):
                    for x in range(2):
                        pe.wait_ge(go_sq, 4 * i + (2 * hh + x + 1))
                        mm = pe.matmul(bank(4 if hh else 1), ONES[:], SQ[:, x, :], start=x == 0, stop=x == 1)
                    mm.then_inc(go_ss, 1)

                def out_gate(j, b):
                    pe.wait_ge(lo_done, tile_no(GK + 9, i, j, 12))
                    if j == 3:
                        pe.wait_ge(y_s, 4 * i + 3)
                    for k in range(KC):
                        mm = three(bank(b), wsl(WH, j, k), wsl(WL, j, k), UH[:, k, :], UL[:, k, :], k == 0, k == KC - 1)
                    mm.then_inc(tile_done, 1)

                for j in range(4):
                    if j == 2:
                        pe.wait_ge(on_done, 4 * i + 1)
                    product(tile_no(GK, i, j, 12), j, UH, UL)
                pe.wait_ge(lo_done, tile_no(GK + 8, i, 0, 12))
                for m in range(TT):
                    rows_product(GK + 4, m, 4 + m)
                attention(0)
                out_gate(0, 2)
                kv(0)
                inside(0)
                out_gate(1, 0)
                attention(1)
                across(0)
                kv(1)
                out_gate(2, 0)
                sums_out(0)
                out_gate(3, 0)
                inside(1)
                across(1)
                sums_out(1)
            with pe.Fori(0, 2) as i:
                for j in range(4):
                    if j == 2:
                        pe.wait_ge(on_done, 2 * GH + 1)
                    product(tile_no(GG, i, j), j, UH, UL)
            linear(BG, YH, YL, ready=y_lo)
            linear(WO, UH, UL, ready=x_lo)
            sums(3, 4)

            def quarter(i):
                t0 = FF + 48 * (i is None)
                for b in range(8):
                    product(tile_no(t0 + (b // 4) * 4, i, b % 4, 16), b % 4, UH, UL, ready=norm["lo"] if b == 0 else None, before=so_far(3, "lo"))
                for b in range(8):
                    product(tile_no(t0 + 8 + (b // 4) * 4, i, b % 4, 16), b % 4, YH, YL, ready=f_ylo if b == 0 else None,
                            before=24 if i is None else 8 * i)

            with pe.Fori(0, 3) as i:
                quarter(i)
            quarter(None)

            pe.wait_ge(f_h, 4 * KC)
            for m in range(8):
                for c in range(4):
                    mm = pe.transpose(bank(m, P, c * P), HT[:, 4 * (m // 4) + c, (m % 4) * P:(m % 4 + 1) * P], IDENT[:])
                mm.then_inc(out_t, 1)


_INPUTS = ["x", "c", "ctx", "c_ctx", "norm_g", "w_ada", "b_ada", "mla_w_in", "mla_g_qa", "mla_w_qup", "mla_g_kva",
           "mla_w_kvup", "mla_w_out", "fno_w_in", "fno_w_out", "final_g", "norm1_g_2", "w_in_2", "moba_q_norm_g_2",
           "moba_k_norm_g_2", "t5_bias_2", "gla_gate_up_2", "gla_gate_bias_2", "gla_out_norm_g_2", "w_branch_moba_2",
           "w_branch_gla_2", "w_out_2", "norm2_g_2", "w_up_2", "w_down_2"]
_VEC_INPUTS = {"c": "c", "c_ctx": "c_ctx", "norm_g": "norm_g", "b_ada": "b_ada", "final_g": "final_g", "norm1": "norm1_g_2",
               "norm2": "norm2_g_2", "g_qa": "mla_g_qa", "g_kva": "mla_g_kva", "gate_bias": "gla_gate_bias_2",
               "out_norm": "gla_out_norm_g_2", "q_norm": "moba_q_norm_g_2", "k_norm": "moba_k_norm_g_2"}


def kernel(**inputs):
    import numpy as _np
    import concourse.bacc as _bacc
    from concourse import mybir as _mybir
    from concourse.bass_utils import run_bass_kernel_spmd as _run

    nc = _bacc.Bacc("TRN2", target_bir_lowering=False, num_devices=1)
    arrays, d = {}, {}
    vec_of = {v: k for k, v in _VEC_INPUTS.items()}
    for name in _INPUTS:
        a = _np.ascontiguousarray(inputs[name])
        key = name
        if name in vec_of:
            key = vec_of[name]
            a = a.reshape(-1, MD if key in ("q_norm", "k_norm") else P)
        elif a.ndim == 3 and a.shape[0] == 1:
            a = a[0]
        arrays[f"in_{name}"] = a
        d[key] = nc.dram_tensor(f"in_{name}", a.shape, _mybir.dt.from_np(a.dtype), kind="ExternalInput").ap()
    for name, a in shape_constants().items():
        arrays[f"const_{name}"] = a
        d[name] = nc.dram_tensor(f"const_{name}", a.shape, _mybir.dt.from_np(a.dtype), kind="ExternalInput").ap()
    d["out"] = nc.dram_tensor("out", (T, D), _mybir.dt.float32, kind="ExternalOutput").ap()
    build(nc, d)
    r = _run(nc, [arrays], core_ids=[0])
    return r.results[0]["out"].reshape(1, T, D)
```

```python
import math
from contextlib import ExitStack

import numpy as np

import concourse.bass as bass
from concourse import mybir

P = 128
T = 512
TC = 256
TK = T + TC
D = 1024
KC = D // P
TT = T // P
EPS = 1e-6
NEG = -1e30

HEADS = 8
NOPE = 128
ROPE = 64
QL = 256
KVL = 128
MLA_SCALE = 1.0 / math.sqrt(NOPE + ROPE)
GRID_W = 64
GROUP = 128
HALF = T // 2
MH = 8
MD = 64
BUCKETS = 32
MAX_DIST = 128
TOEP = T + P
GH = 4
DK = 128
DV = 256
RANK = 16
TAU = 16.0
CH = 64
NCH = T // CH

A0, G1, HD, MO, FG, FZ, FO, MV, MQ, BM, GK, GG, BG, WO, FF = (
    0, 4, 12, 20, 28, 36, 44, 52, 56, 72, 76, 100, 108, 116, 124)

VECS = [("c", 8), ("c_ctx", 8), ("norm_g", 16), ("b_ada", 48), ("final_g", 8), ("norm1", 8), ("norm2", 8),
        ("g_qa", 2), ("g_kva", 1), ("gate_bias", 4), ("out_norm", 2), ("q_norm", 1), ("k_norm", 1)]
ROW = {}
for _n, _r in VECS:
    ROW[_n] = sum(r for _, r in VECS[:len(ROW)])
NROWS = sum(r for _, r in VECS)


def shape_constants():
    out = {}
    out["identity"] = np.eye(P, dtype=np.float32)
    pick = np.zeros((P, 224), np.float32)
    pick[:MD, 96], pick[MD:, 97] = 1.0, 1.0
    out["head_pick"] = pick
    spread = np.zeros((P, P), np.float32)
    spread[0::32, :MD], spread[1::32, MD:] = 1.0, 1.0
    out["head_spread"] = spread
    e, c = np.meshgrid(np.arange(P), np.arange(P), indexing="ij")
    out["chunk_causal"] = ((e // CH == c // CH) & (e <= c)).astype(np.int32)
    axis_dim = ROPE // 2
    inv = (1.0 / (np.float32(10000.0) ** (np.arange(0, axis_dim, 2, dtype=np.float32) / np.float32(axis_dim)))).astype(np.float32)
    row = np.repeat(np.arange(T // GRID_W), GRID_W).astype(np.float32)
    col = np.tile(np.arange(GRID_W), T // GRID_W).astype(np.float32)
    cos, sin = [], []
    for pos in (row, col):
        ang = (pos[None, :] * inv[:, None]).astype(np.float32).astype(np.float64)
        cos += [np.cos(ang), np.cos(ang)]
        sin += [-np.sin(ang), np.sin(ang)]
    out["rope_cos"] = np.concatenate(cos).astype(np.float32)
    out["rope_sin"] = np.concatenate(sin).astype(np.float32)
    k = np.arange(GROUP)
    ang = 2 * np.pi * ((k[:, None] * k[None, :]) % GROUP) / GROUP
    norm = 1.0 / math.sqrt(T * GROUP)
    out["dft_dim"] = np.concatenate([np.cos(ang), -np.sin(ang)], 1).astype(np.float32) * np.float32(norm)
    t, s = np.arange(HALF)[:, None], np.arange(HALF)[None, :]
    mats = []
    for odd in (0, 1):
        ang = 2 * np.pi * ((t * (2 * s + odd)) % T) / T
        mats += [np.cos(ang), np.sin(ang)]
    out["dft_tok"] = np.stack(mats).astype(np.float32)
    d = T - 1 - np.arange(TOEP)
    exact = BUCKETS // 2
    large = exact + (np.log(np.maximum(d, 1).astype(np.float32) / np.float32(exact))
                     / np.float32(math.log(MAX_DIST / exact)) * np.float32(BUCKETS - exact)).astype(np.int32)
    bucket = np.where(d < exact, np.maximum(d, 0), np.minimum(large, BUCKETS - 1))
    out["bucket_hot"] = ((np.arange(BUCKETS)[:, None] == bucket[None, :]) & (d >= 0)).astype(np.float32)
    out["mask_row"] = np.tile(np.where(d >= 0, 0.0, NEG).astype(np.float32), (MH, 1))
    return out


class Steps:

    def __init__(self, sem):
        self.sem, self.base, self.k = sem, 0, 0
        self.i = None

    def loop(self, i, per):
        self.base, self.i, self.per, self.k = self.base + self.k, i, per, 0

    def leave(self, rounds):
        assert self.k == self.per, (self.k, self.per)
        self.base, self.i, self.k = self.base + rounds * self.per, None, 0

    def now(self):
        here = self.base + self.k
        return here if self.i is None else self.i * self.per + here


def build(nc, d):
    f32, f32r, i32 = mybir.dt.float32, mybir.dt.float32r, mybir.dt.int32
    ACT = mybir.ActivationFunctionType
    ALU = mybir.AluOpType
    AX = mybir.AxisListType.X

    ctx = ExitStack()
    with ctx:
        KB = 1024
        BASE = 16512

        def at(name, kb, shape, dt=f32):
            return nc.alloc_sbuf_tensor_at(name, shape, dt, offset=BASE + int(kb * KB))

        def sem(name):
            return ctx.enter_context(nc.semaphore(name))

        HT = at("residual", 0, [P, KC, T])
        UH = at("u_hi", 16, [P, KC, T], f32r)
        UL = at("u_lo", 32, [P, KC, T], f32r)
        RAW = at("w_raw", 48, [P, 2, KC * P])
        WH = at("w_hi", 56, [P, 4, KC * P], f32r)
        WL = at("w_lo", 72, [P, 4, KC * P], f32r)
        YH = at("y_hi", 88, [P, KC, T], f32r)
        YL = at("y_lo", 104, [P, KC, T], f32r)
        SG = at("gated", 120, [P, KC, T])
        MX = at("mixed", 136, [P, KC, T])
        IDENT = at("ident", 152, [P, P])
        HSPREAD = at("head_spread_sb", 152.5, [P, P])
        ONES = at("ones", 153, [P, P])
        COLS = at("cols", 153.5, [P, P])
        ADAL = [at(f"ada_lat{n}", 154 + 0.125 * n, [P, 24]) for n in range(2)]
        ADAC = at("ada_ctx", 154.25, [P, 16])
        MULL = [at(f"mul_lat{n}", 154.375 + 0.0625 * n, [P, KC]) for n in range(2)]
        MULC = at("mul_ctx", 154.5, [P, KC])
        CACT = at("c_act", 154.5625, [P, KC, 2])
        ACC2 = at("gained_sq_sum", 204, [P, T])
        RSC = at("row_rstd", 154.6875, [P, 8])
        NMAX = at("neg_max", 154.75, [P, 4])
        PSUM_ = at("prob_sum", 154.8125, [P, 4])
        EPST = at("eps", 154.875, [P, 1])
        QGAIN = at("q_gain", 154.90625, [P, 1])
        DUMMY = at("dummy", 154.9375, [P, 2])
        HPICK = at("head_pick_sb", 155, [P, 224])
        RS = at("rstd", 156, [P, T])
        ACC = at("sq_sum", 158, [P, T])
        SQ = at("squares", 160, [P, 2, T])
        E = at("stage", 164, [P, 2, T])

        UCH = at("uc_hi", 88, [P, KC, TC], f32r)
        UCL = at("uc_lo", 96, [P, KC, TC], f32r)
        DIAG = at("rstd_diag", 160, [P, TT, P])
        XN = at("x_normed", 104, [P, KC, T])
        AROW = at("ada_rows", 88, [2, 4, T])
        XTOK = at("x_tok", 104, [P, TT, D])
        AD = [at("ada_w0", 120, [P, KC, T]), at("ada_w1", 136, [P, KC, T])]
        AB = [at("ada_back0", 104, [P, KC, T]), at("ada_back1", 88, [P, KC, T])]
        AACC = [at("ada_sum0", 156, [P, T]), at("ada_sum1", 158, [P, T]), at("ada_sum2", 204, [P, T])]
        VROWS = at("vec_rows", 168, [NROWS, P])
        JUNK = at("junk", 170, [P, D])
        CTOK = at("ctx_tok", 174, [P, TC // P, D])
        HOT = at("bucket_hot_sb", 184, [BUCKETS, TOEP])
        MROW = at("mask_row_sb", 187, [MH, TOEP])
        BROW = at("bias_row", 190, [MH, TOEP])
        T5 = at("t5", 193, [BUCKETS, MH])
        CQ = at("cq", 136, [P, 2, T])
        CK = at("ckv", 140, [P, TK])
        KP = at("kp", 143, [ROPE, TK])
        RQ = at("cq_rstd", 146, [P, T])
        RKV = at("ckv_rstd", 148, [P, TK])
        CQH, CQL = at("cq_hi", 168, [P, 2, T], f32r), at("cq_lo", 172, [P, 2, T], f32r)
        CKH, CKL = at("ckv_hi", 176, [P, TK], f32r), at("ckv_lo", 179, [P, TK], f32r)
        KPH, KPL = at("kp_hi", 182, [ROPE, TK], f32r), at("kp_lo", 185, [ROPE, TK], f32r)
        KNH = [at("kn_hi0", 188, [P, TK], f32r), at("kn_hi1", 204, [P, TK], f32r)]
        KNL = [at("kn_lo0", 191, [P, TK], f32r), at("kn_lo1", 162, [P, TK], f32r)]
        VAH, VAL = at("va_hi", 194, [P, TK // P, P], f32r), at("va_lo", 197, [P, TK // P, P], f32r)
        COS, SIN = at("cos", 200, [ROPE, T]), at("sin", 202, [ROPE, T])
        QPF, QPR = at("qp", 118, [ROPE, T]), at("qp_raw", 156, [ROPE, T])
        QNH, QNL = at("qn_hi", 136, [P, 2, T], f32r), at("qn_lo", 140, [P, 2, T], f32r)
        QPH, QPL = at("qp_hi", 144, [ROPE, 2, T], f32r), at("qp_lo", 148, [ROPE, 2, T], f32r)
        PTH, PTL = at("pt_hi", 88, [P, TK // P, T], f32r), at("pt_lo", 100, [P, TK // P, T], f32r)
        PA = at("probs", 112, [P, 2, TK])
        DFH, DFL = at("dft_tok_hi", 168, [P, 8, HALF], f32r), at("dft_tok_lo", 176, [P, 8, HALF], f32r)
        CDH, CDL = at("dft_dim_hi", 184, [P, 2 * GROUP], f32r), at("dft_dim_lo", 185, [P, 2 * GROUP], f32r)
        ZH, ZL = at("z_hi", 186, [P, 2, T], f32r), at("z_lo", 190, [P, 2, T], f32r)
        ZF = at("z_fold", 194, [P, 2, T])
        ZR = at("z_raw", 198, [P, 2, T])
        CDR = at("dft_dim_raw", 202, [P, 2 * GROUP])
        DFR = at("dft_tok_raw", 136, [P, 8, HALF])
        AH, AL = at("dim_dft_hi", 136, [P, 2, 4 * 2 * GROUP], f32r), at("dim_dft_lo", 144, [P, 2, 4 * 2 * GROUP], f32r)

        def m_slot(q):
            return slice(P * (q * (q + 1) // 2), P * ((q + 1) * (q + 2) // 2))

        BIAS = at("toeplitz_bias", 120, [P, MH, T])
        VH, VL = at("mv_hi", 168, [P, TT, T], f32r), at("mv_lo", 176, [P, TT, T], f32r)
        QKH, QKL = at("mqk_hi", 184, [P, 4, T], f32r), at("mqk_lo", 192, [P, 4, T], f32r)
        MP = at("m_probs", 200, [P, T * (TT + 1) // 2])
        MSTAT = at("m_stats", 154.6875, [P, 8])
        VSH, VSL = at("mv_pair_hi", 160, [P, 2, TT, P], f32r), at("mv_pair_lo", 156, [P, 2, TT, P], f32r)
        MTH, MTL = at("m_turned_hi", 96, [P, TT, T], f32r), at("m_turned_lo", 112, [P, TT, T], f32r)
        RROW = at("mqk_rstd", 112, [P, T])
        CMASK = at("causal_mask", 155, [P, P], i32)
        LWR = at("low_raw", 176, [P, KC, P])
        LWH, LWL = at("low_hi", 180, [P, KC, P], f32r), at("low_lo", 184, [P, KC, P], f32r)
        GLO = at("g_low", 188, [RANK, T])
        GUP = at("gate_up", 190, [RANK, T])
        MN = at("log_decay", 192, [P, GH, T])
        RST = at("chunk_starts", 202, [P, T])
        BT = at("decay_sum", 96, [P, GH, T])
        GQK = at("gqk", 168, [P, 4, T])
        SALL = at("states", 176, [P, NCH - 1, DV])
        SH, SL = at("states_hi", 183, [P, NCH - 1, DV], f32r), at("states_lo", 190, [P, NCH - 1, DV], f32r)
        KDH, KDL = at("kdec_hi", 197, [P, TT, DK], f32r), at("kdec_lo", 199, [P, TT, DK], f32r)
        AMH, AML = at("attn_hi", 201, [P, T], f32r), at("attn_lo", 203, [P, T], f32r)
        AMF = at("attn", 205, [P, T])
        EB, EN = at("exp_decay", 156, [P, T]), at("exp_growth", 158, [P, T])
        GVH, GVL = at("gv_hi", 88, [P, TT, T], f32r), at("gv_lo", 104, [P, TT, T], f32r)
        QDH = [at("qdec_hi0", 112, [P, T], f32r), at("qdec_hi1", 168, [P, T], f32r)]
        QDL = [at("qdec_lo0", 114, [P, T], f32r), at("qdec_lo1", 172, [P, T], f32r)]
        DEC = at("chunk_decay", 154.6875, [P, 2, NCH])
        GSIG = at("gate_gla_sb", 168, [P, KC, T])
        KIH, KIL = at("kinv_hi", 116, [P, T], f32r), at("kinv_lo", 118, [P, T], f32r)

        PB = ctx.enter_context(nc.psum_tensor("psum", [P, 8 * T], f32))

        def bank(b, n=T, o=0):
            return PB[:, b * T + o:b * T + o + n]

        def kv_bank(c):
            return bank(4 + 2 * (c % 2) + c // 4, DV, (c // 2) % 2 * DV)

        def f(ap):
            return ap.bitcast(f32)

        raw_full = [sem(f"raw_full{s}") for s in range(2)]
        hi_done = sem("w_hi_done")
        lo_done = sem("w_lo_done")
        tile_done = sem("tile_done")
        s_vec = sem("vec_loaded")
        s_x = sem("x_loaded")
        s_ctx = sem("ctx_loaded")
        s_const = sem("const_loaded")
        s_rope = sem("rope_loaded")
        s_t5 = sem("t5_loaded")
        s_adaw = [sem("ada_loaded0"), sem("ada_loaded1")]
        ones_set = sem("ones_set")
        cols_t = sem("cols_transposed")
        cols_done = sem("cols_done")
        cact_done = sem("c_act_done")
        ada_mm = sem("ada_multiplied")
        ada_row, ada_t, ada_used = sem("ada_rows_copied"), sem("ada_turned"), sem("ada_used")
        x_t = sem("x_transposed")
        x_copied = sem("x_copied")
        row_ss = sem("row_sums")
        x_scaled = sem("ctx_scaled")
        diag_done, rs_mm, xn_done, mod_done = sem("rstd_diag_done"), sem("rstd_spread"), sem("x_normed_done"), sem("mod0_done")
        xn_t = sem("xn_transposed")
        u0_e, u0_hi, u0_lo = sem("u0_e"), sem("u0_hi"), sem("u0_lo")
        bias_mm = sem("bias_mm")
        bias_row = sem("bias_row_done")
        bias_out = sem("bias_stored")
        link_s = sem("vector_steps")
        a_raw = sem("a0_copied")
        a_sq = sem("a0_squares")
        a_ss = sem("a0_sums")
        a_sqrt = sem("a0_sqrt")
        a_n = sem("a0_normed")
        a_hi, a_lo = sem("a0_hi"), sem("a0_lo")
        kv_raw = sem("kv_up_loaded")
        un_mm, un_raw, un_e, un_hi, un_lo = sem("unit_mm"), sem("unit_raw"), sem("unit_rope"), sem("unit_hi"), sem("unit_lo")
        s_mm, s_max, s_exp, s_scaled = sem("scores_mm"), sem("scores_max"), sem("scores_exp"), sem("probs_scaled")
        t_mm, t_hi, t_lo = sem("probs_turned"), sem("turned_hi"), sem("turned_lo")
        o_mm, o_e, o_hi, o_lo = sem("pv_mm"), sem("o_gated"), sem("o_hi"), sem("o_lo")

        norm = {k: sem(f"norm_{k}") for k in ("h", "sq", "acc", "ss", "sqrt", "rstd", "e", "hi", "lo")}

        def so_far(n, k):
            return {"acc": KC + 2, "ss": 1, "sqrt": 1, "rstd": 1}.get(k, KC) * n

        s2_acc, s2_ss, s2_mix = sem("gained_acc"), sem("gained_ss"), sem("gained_mixed")
        r1_sqrt = sem("final_sqrt")
        out_t = sem("out_transposed")
        out_c = sem("out_copied")
        out_s = sem("out_stored")
        s_dft = sem("dft_loaded")
        df_hi, df_lo = sem("dft_hi"), sem("dft_lo")
        z_raw, z_fold, z_hi, z_lo = sem("z_copied"), sem("z_folded"), sem("z_hi_done"), sem("z_lo_done")
        d_mm, d_hi, d_lo = sem("dim_dft_mm"), sem("dim_dft_hi_done"), sem("dim_dft_lo_done")
        f_mm, f_e, f_hi, f_lo = sem("tok_dft_mm"), sem("y_gated"), sem("y_hi_done"), sem("y_lo_done")

        s_bias = sem("bias_loaded")
        s_mask = sem("mask_loaded")
        v_hi, v_lo, vs_done = sem("mv_hi_done"), sem("mv_lo_done"), sem("mv_pair_done")
        q_sq, q_ss, q_rt = sem("mqk_squares"), sem("mqk_sums"), sem("mqk_sqrt")
        q_rs, q_sp = sem("mqk_rstd"), sem("mqk_rstd_spread")
        q_e, q_hi, q_lo = sem("mqk_normed"), sem("mqk_hi_done"), sem("mqk_lo_done")
        M0 = TT * HEADS
        gm_s, bm_e = sem("gate_moba"), sem("branch_moba")
        s_low = sem("low_loaded")
        l_hi, l_lo, l_mm, l_cp, l_up = sem("low_hi_done"), sem("low_lo_done"), sem("low_mm"), sem("low_copied"), sem("gate_up_mm")
        l_abs, l_min, l_ln, b_done = sem("gate_abs"), sem("gate_min"), sem("gate_log"), sem("decay_done")
        g_raw, gv_mm, gv_hi, gv_lo = sem("gqk_copied"), sem("gv_mm"), sem("gv_hi_done"), sem("gv_lo_done")
        g_ex, g_e, g_hi, g_lo = sem("exp_done"), sem("qk_decayed"), sem("qk_hi_done"), sem("qk_lo_done")
        kd_d, kd_x, kd_e, kd_t = sem("kdec_exponent"), sem("kdec_exp"), sem("kdec_done"), sem("kdec_turned")
        kd_hi, kd_lo = sem("kdec_hi_done"), sem("kdec_lo_done")
        at_mm, am_f, am_hi, am_lo = sem("attn_mm"), sem("attn_masked"), sem("attn_hi_done"), sem("attn_lo_done")
        kv_mm, st_f, st_hi, st_lo = sem("kv_mm"), sem("states_done"), sem("states_hi_done"), sem("states_lo_done")
        go_mm, go_sq, go_ss, go_rt, on_done = sem("gla_o_mm"), sem("gla_o_sq"), sem("gla_o_sums"), sem("gla_o_sqrt"), sem("gla_o_normed")
        g_si, y_s, y_e, y_hi, y_lo = sem("g_out_silu"), sem("g_out_copied"), sem("g_out_gated"), sem("gy_hi_done"), sem("gy_lo_done")
        gg_s = sem("gate_gla")
        x_e, x_hi, x_lo = sem("mixed_e"), sem("mixed_hi"), sem("mixed_lo")
        f_r, f_sq, f_ylo, f_h = sem("relu_done"), sem("relu_sq_hi"), sem("relu_sq_lo"), sem("ff_added")

        toep = nc.dram_tensor("bias_scratch", (MH, P, TOEP), f32)
        FTMP = at("ff_scaled", 176, [P, 2, T])
        OUT = at("out_rows", 88, [P, TT, D])

        block = ctx.enter_context(nc.Block())

        def raw_count(t0, i, j, per=4):
            return 16 * (t0 // 2 + j // 2 + 1) + (0 if i is None else 8 * per * i)

        def tile_no(t0, i, j, per=4):
            return t0 + j if i is None else per * i + (t0 + j)

        first_units = (1, 0, 2, 3)
        units = [(0, u) for u in first_units + (4,)]
        for j in range(4):
            units += [(j + 1, u) for u in first_units] * (j < 3) + ([(j, 4), (j, 5)] if j else [(0, 5)])
        UPR = len(units)

        def unit_bank(j, u):
            return {0: 4, 1: 0, 2: 6, 3: 7, 4: 2, 5: 1}[u] if j == 0 else {2: 1, 4: 1}.get(u, 0)

        def unit_no(j, u):
            return units.index((j, u)) + 1

        def unit_mm_no(j, u):
            return sum(1 for x in units[:unit_no(j, u)] if x[1] < 5)

        @block.sync
        def _(sp):
            def ada_weights(q):
                return d["w_ada"][q // 6, :, (q % 6) * T:(q % 6 + 1) * T].rearrange("(k p) n -> p k n", p=P)

            sp.dma_start(IDENT[:], d["identity"]).then_inc(s_const, 16)
            sp.dma_start(XTOK[:], d["x"].rearrange("(m p) n -> p m n", p=P)).then_inc(s_x, 16)
            for name, rows in VECS:
                src = d[name]
                if name in ("q_norm", "k_norm"):
                    for n in range(2):
                        sp.dma_start(VROWS[ROW[name]:ROW[name] + 1, n * MD:(n + 1) * MD], src).then_inc(s_vec, 16)
                else:
                    sp.dma_start(VROWS[ROW[name]:ROW[name] + rows, :], src).then_inc(s_vec, 16)
            for q in range(2):
                sp.dma_start(AD[q][:], ada_weights(q)).then_inc(s_adaw[q], 16)
            sp.dma_start(CTOK[:], d["ctx"].rearrange("(m p) n -> p m n", p=P)).then_inc(s_ctx, 16)
            sp.dma_start(T5[:], d["t5_bias_2"]).then_inc(s_t5, 16)
            sp.dma_start(HOT[:], d["bucket_hot"]).then_inc(s_t5, 16)
            sp.dma_start(MROW[:], d["mask_row"]).then_inc(s_t5, 16)
            sp.dma_start(COS[:], d["rope_cos"]).then_inc(s_rope, 16)
            sp.dma_start(SIN[:], d["rope_sin"]).then_inc(s_rope, 16)
            sp.dma_start(HSPREAD[:], d["head_spread"]).then_inc(s_mask, 16)
            sp.dma_start(HPICK[:], d["head_pick"]).then_inc(s_mask, 16)
            def load_tile(t0, i, j, src, k, per=4):
                if t0 or j >= 2:
                    sp.wait_ge(lo_done, tile_no(t0 - 1, i, j, per))
                sp.dma_start(RAW[:, j % 2, :].rearrange("p (k n) -> p k n", k=k), src.rearrange("(k p) n -> p k n", p=P))\
                    .then_inc(raw_full[j % 2], 16)

            def load(t0, n, w, c0):
                if n == 1:
                    for j in range(4):
                        load_tile(t0, None, j, w[:, c0 + j * P:c0 + (j + 1) * P], KC)
                else:
                    with sp.Fori(0, n) as i:
                        for j in range(4):
                            load_tile(t0, i, j, w[:, bass.ds(4 * P * i + (c0 + j * P), P)], KC)

            for q in range(2, 4):
                for j in range(2 * q - 4, 2 * q - 2):
                    load_tile(A0, None, j, d["mla_w_in"][:, j * P:(j + 1) * P], KC)
                sp.wait_ge(ada_mm, q - 1)
                sp.dma_start(AD[q % 2][:], ada_weights(q)).then_inc(s_adaw[q % 2], 16)
            sp.wait_ge(bias_row, 1)
            sp.dma_start(toep.ap(), BROW[:].unsqueeze(1).to_broadcast([MH, P, TOEP])).then_inc(bias_out, 16)
            sp.wait_ge(u0_lo, KC)
            def gate_tile(r):
                c0 = QL + KVL + ROPE + r * P
                load_tile(G1 + r - r % 4, None, r % 4, d["mla_w_in"][:, c0:c0 + P], KC)

            gate_tile(0)
            gate_tile(1)
            for r in range(6):
                if r == 2:
                    gate_tile(2)
                    gate_tile(3)
                if r >= 2:
                    sp.wait_ge(ada_used, r - 1)
                if r == 3:
                    sp.wait_ge(tile_done, 4)
                sp.dma_start((AD[0] if r == 1 else AB[r % 2])[:], ada_weights(4 + r)).then_inc(s_adaw[r % 2], 16)
                if r >= 3:
                    gate_tile(r + 1)
            gate_tile(7)

            def head_weights(i):
                for j in range(4):
                    sp.wait_ge(lo_done, tile_no(HD - 1, i, j))
                    h = 4 * i + j
                    sp.dma_start(RAW[:, j % 2, 2 * 192:2 * 192 + 256], d["mla_w_kvup"][:, bass.ds(256 * i * 4 + 256 * j, 256)])\
                        .then_inc(kv_raw, 16)
                    sp.wait_ge(kv_raw, 16 * h + 16)
                    sp.dma_start(RAW[:, j % 2, 0:2 * 192].rearrange("p (k n) -> p k n", k=2),
                                 d["mla_w_qup"][:, bass.ds(192 * i * 4 + 192 * j, 192)].rearrange("(k p) n -> p k n", p=P))\
                        .then_inc(raw_full[j % 2], 16)

            with sp.Fori(0, 2) as i:
                head_weights(i)
            load(MO, 2, d["mla_w_out"], 0)
            sp.wait_ge(o_lo, HEADS)
            for r in range(6, 8):
                sp.dma_start(AB[r % 2][:], ada_weights(4 + r)).then_inc(s_adaw[r % 2], 16)
            sp.dma_start(CDR[:], d["dft_dim"]).then_inc(s_dft, 16)
            for m in range(4):
                sp.dma_start(DFR[:, 2 * m:2 * m + 2, :], d["dft_tok"][m].rearrange("(k p) n -> p k n", p=P)).then_inc(s_dft, 16)
            load(FG, 2, d["fno_w_in"], D)
            load(FZ, 2, d["fno_w_in"], 0)
            load(FO, 2, d["fno_w_out"], 0)
            w = d["w_in_2"]
            mw, kw, vw = MH * MD, GH * DK, GH * DV
            sp.wait_ge(f_lo, KC)
            sp.wait_ge(bias_out, 16)
            sp.dma_start(BIAS[:], bass.AP(toep, P - 1, [[TOEP - 1, P], [P * TOEP, MH], [1, T]])).then_inc(s_bias, 16)
            load(MV, 1, w, 2 * mw)
            with sp.Fori(0, 2) as i:
                for j in range(4):
                    load_tile(MQ, i, j, w[:, bass.ds(2 * P * i + (mw * (j // 2) + P * (j % 2)), P)], KC, 8)
                for j in range(4):
                    load_tile(MQ + 4, i, j, w[:, bass.ds(4 * P * i + (3 * mw + 2 * kw + vw + RANK + vw + P * j), P)], KC, 8)
            for j in range(4):
                load_tile(BM, None, j, d["w_branch_moba_2"][:, 2 * P * j:2 * P * (j + 1)], 4)
            sp.wait_ge(o_lo, HEADS + MH)
            sp.dma_start(CMASK[:], d["chunk_causal"]).then_inc(s_mask, 16)
            low = 3 * mw + 2 * kw + vw
            sp.dma_start(LWR[:], w[:, low:low + P].rearrange("(k p) n -> p k n", p=P)).then_inc(s_low, 16)
            sp.dma_start(GUP[:], d["gla_gate_up_2"]).then_inc(s_low, 16)
            with sp.Fori(0, 2) as i:
                for j in range(4):
                    load_tile(GK, i, j, w[:, bass.ds(2 * P * i + (3 * mw + kw * (j // 2) + P * (j % 2)), P)], KC, 12)
                for j in range(4):
                    load_tile(GK + 4, i, j, w[:, bass.ds(2 * DV * i + (3 * mw + 2 * kw + P * j), P)], KC, 12)
                for j in range(4):
                    load_tile(GK + 8, i, j, w[:, bass.ds(2 * DV * i + (low + RANK + P * j), P)], KC, 12)
            load(GG, 2, w, low + RANK + vw + D)
            load(BG, 2, d["w_branch_gla_2"], 0)
            load(WO, 2, d["w_out_2"], 0)

            def quarter(i):
                for b in range(8):
                    c = slice(D * 3 + P * b, D * 3 + P * (b + 1)) if i is None else bass.ds(D * i + P * b, P)
                    load_tile(FF + 48 * (i is None) + (b // 4) * 4, i, b % 4, d["w_up_2"][:, c], KC, 16)
                for b in range(8):
                    r = slice(D * 3, D * 4) if i is None else bass.ds(D * i, D)
                    load_tile(FF + 48 * (i is None) + 8 + (b // 4) * 4, i, b % 4, d["w_down_2"][r, P * b:P * (b + 1)], KC, 16)

            with sp.Fori(0, 3) as i:
                quarter(i)
            quarter(None)
            sp.wait_ge(bias_out, 16)
            for m in range(2 * TT):
                sp.wait_ge(out_c, m + 1)
                half = slice((m // TT) * T, (m // TT + 1) * T)
                sp.dma_start(d["out"][(m % TT) * P:(m % TT + 1) * P, half], OUT[:, m % TT, half]).then_inc(out_s, 16)
            sp.wait_ge(out_s, 16 * 2 * TT)

        @block.gpsimd
        def _(pool):
            def split_lo(t0, i, j, per=4):
                pool.wait_ge(hi_done, tile_no(t0 + 1, i, j, per))
                pool.tensor_tensor(WL[:, j, :], RAW[:, j % 2, :], f(WH[:, j, :]), ALU.subtract).then_inc(lo_done, 1)

            def clear_sum(n):
                pool.memset(ACC[:, 0:T // 2], 0.0).then_inc(norm["acc"], 1)
                pool.memset(ACC[:, T // 2:T], 0.0).then_inc(norm["acc"], 1)
                pool.wait_ge(norm["acc"], so_far(n, "acc") + 2)

            def add_square(n, c, slot):
                pool.wait_ge(norm["sq"], so_far(n, "sq") + c + 1)
                pool.wait_ge(norm["acc"], so_far(n, "acc") + c + 2)
                pool.tensor_tensor(ACC[:], ACC[:], SQ[:, slot, :], ALU.add).then_inc(norm["acc"], 1)

            for j in range(4):
                split_lo(A0, None, j)
            for j in range(4):
                pool.wait_ge(a_raw, j + 1)
                split_lo(G1, None, j)
            with pool.Fori(0, 2) as i:
                for j in range(4):
                    split_lo(G1 + 4, i, j)
            with pool.Fori(0, 2) as i:
                for j in range(4):
                    split_lo(HD + 4, i, j)
            clear_sum(0)
            with pool.Fori(0, 2) as i:
                for j in range(4):
                    c = 4 * i + j
                    add_square(0, c, j % 2)
                    pool.wait_ge(norm["h"], so_far(0, "h") + c + 1)
                    split_lo(MO + 4, i, j)
            with pool.Fori(0, 2) as i:
                for j in range(4):
                    split_lo(FG + 4, i, j)
            with pool.Fori(0, 2) as i:
                for j in range(4):
                    split_lo(FZ + 4, i, j)
            pool.wait_ge(norm["rstd"], so_far(0, "rstd") + 1)
            pool.wait_ge(ada_mm, 12)
            clear_sum(1)
            pool.memset(ACC2[:], 0.0).then_inc(s2_acc, 1)
            with pool.Fori(0, 2) as i:
                for j in range(4):
                    c = 4 * i + j
                    add_square(1, c, j % 2)
                    pool.wait_ge(s2_acc, c + 1)
                    pool.tensor_tensor(ACC2[:], ACC2[:], E[:, j % 2, :], ALU.add).then_inc(s2_acc, 1)
                    pool.wait_ge(norm["h"], so_far(1, "h") + c + 1)
                    split_lo(FO + 4, i, j)
            for j in range(4):
                pool.wait_ge(v_lo, j + 1)
                split_lo(MQ, None, j)
            with pool.Fori(0, 2) as i:
                for j in range(4):
                    split_lo(MQ + 4, i, j, 8)
                pool.wait_ge(q_lo, 4 * i + 4)
                for n in range(2):
                    for dst, src in ((VSH, VH), (VSL, VL)):
                        pool.tensor_copy(dst[:, n, :, :], f(src[:, :, bass.ds(2 * P * i + n * P, P)])).then_inc(vs_done, 1)
                for j in range(4):
                    split_lo(MQ + 8, i, j, 8)
            for j in range(4):
                pool.wait_ge(bm_e, j + 1)
                split_lo(GK, None, j)
            with pool.Fori(0, 2) as i:
                for t0 in (GK + 4, GK + 8, GK + 12):
                    for j in range(4):
                        split_lo(t0, i, j, 12)
            with pool.Fori(0, 2) as i:
                for j in range(4):
                    split_lo(GG + 4, i, j)
            with pool.Fori(0, 2) as i:
                for j in range(4):
                    pool.wait_ge(x_e, 4 * i + (j + 1))
                    split_lo(BG + 4, i, j)
            clear_sum(2)
            with pool.Fori(0, 2) as i:
                for j in range(4):
                    c = 4 * i + j
                    add_square(2, c, j % 2)
                    pool.wait_ge(norm["h"], so_far(2, "h") + c + 1)
                    split_lo(WO + 4, i, j)

            def quarter(i):
                t0 = FF + 48 * (i is None)
                for b in range(8):
                    split_lo(t0 + 4 + (b // 4) * 4, i, b % 4, 16)
                for b in range(8 if i is not None else 4):
                    pool.wait_ge(f_h, 24 + b + 1 if i is None else 8 * i + (b + 1))
                    split_lo(t0 + 12 + (b // 4) * 4, i, b % 4, 16)

            with pool.Fori(0, 3) as i:
                quarter(i)
            quarter(None)

        @block.scalar
        def _(act):
            def split_hi(t0, i, j, per=4):
                act.wait_ge(raw_full[j % 2], raw_count(t0, i, j, per))
                act.activation(WH[:, j, :], RAW[:, j % 2, :], ACT.Copy).then_inc(hi_done, 1)

            act.wait_ge(cols_done, 1)
            for n in range(2):
                act.activation(CACT[:, :, n], COLS[:, 8 * n:8 * n + 8], ACT.Silu).then_inc(cact_done, 1)
            act.wait_ge(s_x, 16)
            for m in range(TT):
                if m >= 1:
                    act.wait_ge(row_ss, m)
                act.activation(JUNK[:], XTOK[:, m, :], ACT.Square, accum_out=RSC[:, m:m + 1]).then_inc(row_ss, 1)
            act.wait_ge(row_ss, TT)
            act.wait_ge(ones_set, 3)
            act.activation(RSC[:, 0:TT], RSC[:, 0:TT], ACT.Sqrt, scale=1.0 / D, bias=EPST[:]).then_inc(row_ss, 1)
            for c in range(KC):
                act.wait_ge(x_t, c + 1)
                act.activation(HT[:, c, :], bank(c % 4), ACT.Copy).then_inc(x_copied, 1)

            def ada_row_copy(q):
                act.wait_ge(ada_mm, q + 1)
                act.activation(AROW[:, q, :], bank(6)[0:2, :], ACT.Copy).then_inc(ada_row, 1)

            split_hi(A0, None, 0)
            split_hi(A0, None, 1)
            ada_row_copy(0)
            act.wait_ge(s_ctx, 16)
            for m in range(TC // P):
                act.wait_ge(row_ss, TT + 1 + m)
                act.activation(JUNK[:], CTOK[:, m, :], ACT.Square, accum_out=RSC[:, TT + m:TT + m + 1]).then_inc(row_ss, 1)
            act.wait_ge(row_ss, 7)
            act.activation(RSC[:, TT:6], RSC[:, TT:6], ACT.Sqrt, scale=1.0 / D, bias=EPST[:]).then_inc(row_ss, 1)
            split_hi(A0, None, 2)
            split_hi(A0, None, 3)
            for q in range(1, 4):
                ada_row_copy(q)
            act.wait_ge(mod_done, 1)
            for c in range(KC):
                act.activation(UH[:, c, :], XN[:, c, :], ACT.Identity, scale=MULL[0][:, c:c + 1], bias=ADAL[0][:, c:c + 1]).then_inc(u0_hi, 1)
            for c in range(KC):
                act.wait_ge(u0_e, KC + c + 1)
                act.activation(UCH[:, c, :], E[:, c % 2, 0:TC], ACT.Copy).then_inc(u0_hi, 1)

            for j in range(4):
                act.wait_ge(tile_done, j + 1)
                if j < 2:
                    act.activation(CQ[:, j, :], bank(j), ACT.Copy).then_inc(a_raw, 1)
                    act.activation(SQ[:, j, :], bank(j), ACT.Square).then_inc(a_sq, 1)
                elif j == 2:
                    act.wait_ge(a_ss, 2)
                    act.activation(CK[:, 0:TC], bank(4, TC), ACT.Copy)
                    act.activation(SQ[:, 1, 0:TC], bank(4, TC), ACT.Square).then_inc(a_sq, 1)
                    act.activation(SQ[:, 0, :], bank(2), ACT.Square).then_inc(a_sq, 1)
                    act.activation(CK[:, TC:TK], bank(2), ACT.Copy).then_inc(a_raw, 1)
                else:
                    act.activation(KP[:, 0:TC], bank(5, TC)[0:ROPE, :], ACT.Copy).then_inc(a_raw, 1)
                split_hi(G1, None, j)
            act.wait_ge(a_ss, 2)
            act.activation(RQ[:], bank(6), ACT.Sqrt, scale=1.0 / QL, bias=EPST[:]).then_inc(a_sqrt, 1)
            act.wait_ge(a_ss, 4)
            act.activation(RKV[:, 0:TC], bank(4, TC, TC), ACT.Sqrt, scale=1.0 / KVL, bias=EPST[:])
            act.activation(RKV[:, TC:TK], bank(7), ACT.Sqrt, scale=1.0 / KVL, bias=EPST[:]).then_inc(a_sqrt, 1)

            act.wait_ge(ada_used, 2)
            for r in range(8):
                act.wait_ge(tile_done, G1 + r + 1)
                act.activation(SG[:, r, :], bank(r % 4), ACT.Silu)
                split_hi(G1 + 4 + r - r % 4, None, r % 4)
                if r == 1:
                    act.wait_ge(a_raw, 4)
                    act.wait_ge(a_n, 1)
                    act.activation(KPH[:], KP[:], ACT.Copy).then_inc(a_hi, 1)
                elif r == 3:
                    act.wait_ge(a_n, 2)
                    act.activation(CQH[:], CQ[:], ACT.Copy).then_inc(a_hi, 1)
                elif r == 4:
                    act.wait_ge(a_n, 3)
                    act.activation(CKH[:], CK[:], ACT.Copy).then_inc(a_hi, 1)

            with act.Fori(0, 2) as i:
                def unit(j, u):
                    par = j % 2
                    if u == 5:
                        act.wait_ge(tile_done, tile_no(HD + 1, i, j))
                    elif u != 1:
                        act.wait_ge(un_mm, (UPR - 4) * i + unit_mm_no(j, u))
                    b = unit_bank(j, u)
                    if u == 0:
                        act.activation(QNH[:, par, :], bank(b), ACT.Copy).then_inc(un_hi, 1)
                    elif u == 1:
                        act.wait_ge(un_e, 4 * i + (j + 1))
                        act.activation(QPH[:, par, :], QPF[:], ACT.Copy).then_inc(un_hi, 1)
                    elif u == 2:
                        act.activation(KNH[par][:, TC:TK], bank(b), ACT.Copy).then_inc(un_hi, 1)
                    elif u == 3:
                        act.activation(KNH[par][:, 0:TC], bank(b, TC), ACT.Copy).then_inc(un_hi, 1)
                    elif u == 4:
                        act.activation(VAH[:, 0:4, :], bank(b), ACT.Copy).then_inc(un_hi, 1)
                    else:
                        act.activation(VAH[:, 4:6, :], bank(b, TC), ACT.Copy).then_inc(un_hi, 1)

                def exps(j, q):
                    n = 16 * i + (4 * j + q)
                    act.wait_ge(s_max, n + 1)
                    act.activation(PA[:, q % 2, :], PB[:, (4 + 2 * (q % 2)) * T:(4 + 2 * (q % 2)) * T + TK], ACT.Exp, scale=MLA_SCALE,
                                   bias=NMAX[:, q % 2:q % 2 + 1], accum_out=PSUM_[:, q % 2:q % 2 + 1]).then_inc(s_exp, 1)

                def turned(j, q):
                    n = 16 * i + (4 * j + q)
                    act.wait_ge(t_mm, n + 1)
                    act.activation(PTH[:, :, q * P:(q + 1) * P], PB[:, 2 * T:2 * T + TK].rearrange("p (k n) -> p k n", n=P),
                                   ACT.Copy).then_inc(t_hi, 1)

                def rope_raw(j):
                    act.wait_ge(un_mm, (UPR - 4) * i + unit_mm_no(j, 1))
                    act.activation(QPR[:], bank(0)[0:ROPE, :], ACT.Copy).then_inc(un_raw, 1)

                def output(j):
                    act.wait_ge(o_e, 4 * i + (j + 1))
                    act.activation(UH[:, 4 * i + j, :], E[:, 1, :], ACT.Copy).then_inc(o_hi, 1)

                unit(0, 1)
                unit(0, 0)
                unit(0, 2)
                unit(0, 3)
                unit(0, 4)
                exps(0, 0)
                exps(0, 1)
                for j in range(4):
                    nxt = j < 3
                    if nxt:
                        rope_raw(j + 1)
                        unit(j + 1, 1)
                    if j:
                        output(j - 1)
                    if nxt:
                        unit(j + 1, 0)
                    turned(j, 0)
                    if nxt:
                        unit(j + 1, 2)
                    exps(j, 2)
                    if nxt:
                        unit(j + 1, 3)
                    else:
                        unit(3, 4)
                    turned(j, 1)
                    exps(j, 3)
                    if nxt:
                        unit(j, 4 if j else 5)
                    else:
                        unit(3, 5)
                    turned(j, 2)
                    if nxt:
                        exps(j + 1, 0)
                        if j:
                            unit(j, 5)
                    turned(j, 3)
                    if nxt:
                        exps(j + 1, 1)
                    split_hi(HD + 4, i, j)
                output(3)

            def square_steps(n, t0):
                with act.Fori(0, 2) as i:
                    for j in range(4):
                        c = 4 * i + j
                        act.wait_ge(norm["h"], so_far(n, "h") + c + 1)
                        act.wait_ge(norm["acc"], so_far(n, "acc") + c + 1)
                        act.activation(SQ[:, j % 2, :], HT[:, c, :], ACT.Square).then_inc(norm["sq"], 1)
                        split_hi(t0 + 4, i, j)

            def root(n, b):
                act.wait_ge(norm["ss"], so_far(n, "ss") + 1)
                act.activation(RS[:], bank(b), ACT.Sqrt, scale=1.0 / D, bias=EPST[:]).then_inc(norm["sqrt"], 1)

            square_steps(0, MO)
            root(0, 4)
            for c in range(KC):
                act.wait_ge(norm["e"], so_far(0, "e") + c + 1)
                act.activation(UH[:, c, :], E[:, c % 2, :], ACT.Identity, bias=ADAL[1][:, c:c + 1]).then_inc(norm["hi"], 1)
            act.wait_ge(s_dft, 80)
            act.activation(CDH[:], CDR[:], ACT.Copy).then_inc(df_hi, 1)
            act.activation(DFH[:], DFR[:], ACT.Copy).then_inc(df_hi, 1)
            with act.Fori(0, 2) as i:
                for j in range(4):
                    act.wait_ge(tile_done, tile_no(FG + 1, i, j))
                    act.activation(SG[:, 4 * i + j, :], bank(j), ACT.Silu)
                    split_hi(FG + 4, i, j)
            with act.Fori(0, 2) as i:
                def z_in(j):
                    act.wait_ge(tile_done, tile_no(FZ + 1, i, j))
                    if j >= 2:
                        act.wait_ge(z_fold, 4 * i + (j - 1))
                    act.activation(ZR[:, j % 2, :], bank(j), ACT.Copy).then_inc(z_raw, 1)
                    split_hi(FZ + 4, i, j)
                    act.wait_ge(z_fold, 4 * i + (j + 1))
                    act.activation(ZH[:, j % 2, :], ZF[:, j % 2, :], ACT.Copy).then_inc(z_hi, 1)

                def a_in(j):
                    act.wait_ge(d_mm, 4 * i + (j + 1))
                    act.activation(AH[:, j % 2, :], PB[:, 4 * T:6 * T], ACT.Copy).then_inc(d_hi, 1)

                def y_in(j):
                    act.wait_ge(f_e, 4 * i + (j + 1))
                    act.activation(YH[:, 4 * i + j, :], E[:, j % 2, :], ACT.Copy).then_inc(f_hi, 1)

                z_in(0)
                z_in(1)
                a_in(0)
                z_in(2)
                a_in(1)
                y_in(0)
                z_in(3)
                a_in(2)
                y_in(1)
                a_in(3)
                y_in(2)
                y_in(3)
            fg = ROW["final_g"]
            with act.Fori(0, 2) as i:
                for j in range(4):
                    c = 4 * i + j
                    act.wait_ge(norm["h"], so_far(1, "h") + c + 1)
                    act.wait_ge(norm["acc"], so_far(1, "acc") + c + 1)
                    if j >= 2:
                        act.wait_ge(s2_acc, 4 * i + j)
                    else:
                        act.wait_ge(s2_acc, 4 * i + max(j, 1))
                    act.activation(E[:, j % 2, :], HT[:, c, :], ACT.Square, scale=COLS[:, bass.ds(4 * i + (fg + j), 1)])
                    act.activation(SQ[:, j % 2, :], HT[:, c, :], ACT.Square).then_inc(norm["sq"], 1)
                    split_hi(FO + 4, i, j)
            act.wait_ge(s2_mix, 1)
            act.activation(RS[:], RS[:], ACT.Sqrt, scale=1.0 / D, bias=DUMMY[:, 1:2]).then_inc(norm["sqrt"], 1)
            act.activation(SQ[:, 0, :], bank(4), ACT.Sqrt, scale=1.0 / D, bias=EPST[:]).then_inc(r1_sqrt, 1)
            for c in range(KC):
                act.wait_ge(norm["e"], so_far(1, "e") + c + 1)
                act.activation(UH[:, c, :], E[:, c % 2, :], ACT.Copy).then_inc(norm["hi"], 1)
            for m in range(TT):
                act.wait_ge(tile_done, MV + m + 1)
                act.activation(VH[:, m, :], bank(m), ACT.Copy).then_inc(v_hi, 1)
            for j in range(4):
                split_hi(MQ, None, j)
            with act.Fori(0, 2) as i:
                def gate(j, b):
                    act.wait_ge(tile_done, tile_no(MQ + 5, i, j, 8))
                    act.activation(MX[:, 4 * i + j, :], bank(b), ACT.Copy).then_inc(gm_s, 1)
                    split_hi(MQ + 8, i, j, 8)

                act.wait_ge(o_lo, 4 * i + HEADS)
                for j in range(4):
                    act.wait_ge(tile_done, tile_no(MQ + 1, i, j, 8))
                    if j >= 2:
                        act.wait_ge(q_ss, 4 * i + (j - 1))
                    act.activation(SQ[:, j % 2, :], bank(j), ACT.Square).then_inc(q_sq, 1)
                    split_hi(MQ + 4, i, j, 8)
                act.wait_ge(q_ss, 4 * i + 4)
                act.activation(RROW[:], bank(4), ACT.Sqrt, scale=1.0 / MD, bias=EPST[:]).then_inc(q_rt, 1)
                gate(0, 6)
                for j in range(4):
                    act.wait_ge(q_e, 4 * i + (j + 1))
                    act.activation(QKH[:, j, :], E[:, j % 2, :], ACT.Copy).then_inc(q_hi, 1)
                gate(1, 7)

                def exps(m, q):
                    act.wait_ge(s_max, 16 * i + (M0 + 4 * m + q + 1))
                    x, w = q, (q + 1) * P
                    act.activation(MP[:, m_slot(q)], MP[:, m_slot(q)], ACT.Exp, bias=MSTAT[:, x:x + 1],
                                   accum_out=MSTAT[:, 4 + x:5 + x]).then_inc(s_exp, 1)

                def turned(m, q):
                    act.wait_ge(t_mm, 16 * i + (M0 + 4 * m + q + 1))
                    act.activation(MTH[:, 0:q + 1, q * P:(q + 1) * P],
                                   bank(6 + q % 2, (q + 1) * P).rearrange("p (k n) -> p k n", n=P), ACT.Copy).then_inc(t_hi, 1)

                def output(m):
                    rows = slice(MD * (m % 2), MD * (m % 2 + 1))
                    act.wait_ge(o_mm, 4 * i + (HEADS + m + 1))
                    act.activation(YH[rows, 2 * i + m // 2, :], bank(m % 2)[rows, :], ACT.Copy).then_inc(o_hi, 1)

                exps(0, 0)
                exps(0, 1)
                for m in range(4):
                    exps(m, 2)
                    if m:
                        output(m - 1)
                    turned(m, 0)
                    turned(m, 1)
                    exps(m, 3)
                    if m < 3:
                        exps(m + 1, 0)
                    turned(m, 2)
                    if m < 3:
                        exps(m + 1, 1)
                    turned(m, 3)
                    if m % 2:
                        gate(2 + m // 2, 2 + m // 2)
                output(3)
            act.wait_ge(gm_s, KC)
            for c in range(KC):
                act.activation(MX[:, c, :], MX[:, c, :], ACT.Sigmoid).then_inc(gm_s, 1)
            act.wait_ge(s_low, 32)
            act.activation(LWH[:], LWR[:], ACT.Copy).then_inc(l_hi, 1)
            for j in range(4):
                act.wait_ge(tile_done, BM + j + 1)
                split_hi(GK, None, j)
                if j == 1:
                    act.wait_ge(l_mm, 1)
                    act.activation(GLO[:], bank(7)[0:RANK, :], ACT.Copy).then_inc(l_cp, 1)
            gb = ROW["gate_bias"]
            for h in range(GH):
                act.wait_ge(l_min, h + 1)
                act.activation(BT[:, h, :], bank(h), ACT.Abs, bias=COLS[:, gb + h:gb + h + 1]).then_inc(l_abs, 1)
            act.wait_ge(l_abs, GH)
            act.activation(BT[:], BT[:], ACT.Exp, scale=-1.0).then_inc(l_abs, 1)
            act.wait_ge(l_abs, GH + 1)
            act.activation(BT[:], BT[:], ACT.Ln, bias=1.0).then_inc(l_ln, 1)
            with act.Fori(0, 2) as i:
                for j in range(4):
                    act.wait_ge(tile_done, tile_no(GK + 1, i, j, 12))
                    act.activation(GQK[:, j, :], bank(j), ACT.Copy).then_inc(g_raw, 1)
                    split_hi(GK + 4, i, j, 12)

                def decays(hh):
                    n = 2 * i + hh
                    act.activation(EB[:], BT[:, n, :], ACT.Exp, scale=1.0 / TAU).then_inc(g_ex, 1)
                    act.activation(EN[:], BT[:, n, :], ACT.Exp, scale=-1.0 / TAU).then_inc(g_ex, 1)
                    act.activation(DEC[:, hh, :].unsqueeze(2), BT[:, n, :].rearrange("p (n c) -> p n c", c=CH)[:, :, CH - 1:CH],
                                   ACT.Exp, scale=1.0 / TAU).then_inc(g_ex, 1)

                def operands(hh):
                    n = 2 * i + hh
                    act.wait_ge(g_e, 4 * i + (2 * hh + 1))
                    act.activation(QDH[hh][:], E[:, 0, :], ACT.Copy).then_inc(g_hi, 1)
                    act.wait_ge(g_e, 4 * i + (2 * hh + 2))
                    if hh:
                        act.wait_ge(at_mm, n)
                    act.activation(KIH[:], E[:, 1, :], ACT.Copy).then_inc(g_hi, 1)
                    act.wait_ge(kd_d, n + 1)
                    act.activation(SQ[:, 0, :], SQ[:, 0, :], ACT.Exp, scale=1.0 / TAU).then_inc(kd_x, 1)

                def attention(hh):
                    n = 2 * i + hh
                    act.wait_ge(am_f, n + 1)
                    act.activation(AMH[:], AMF[:], ACT.Copy).then_inc(am_hi, 1)
                    act.wait_ge(kd_t, n + 1)
                    act.activation(KDH[:], bank(1).rearrange("p (k n) -> p k n", n=P), ACT.Copy).then_inc(kd_hi, 1)

                def states(hh):
                    act.wait_ge(st_f, 2 * i + (hh + 1))
                    act.activation(SH[:], SALL[:], ACT.Copy).then_inc(st_hi, 1)

                def squares(hh):
                    for x in range(2):
                        act.wait_ge(go_mm, 4 * i + (2 * hh + x + 1))
                        act.activation(SQ[:, x, :], bank(2 + x), ACT.Square).then_inc(go_sq, 1)

                def out_gate(j, b):
                    act.wait_ge(tile_done, tile_no(GK + 9, i, j, 12))
                    act.activation(SG[:, 4 * i + j, :], bank(b), ACT.Copy).then_inc(y_s, 1)
                    split_hi(GK + 12, i, j, 12)

                def root_silu(hh):
                    n = 2 * i + hh
                    act.wait_ge(go_ss, n + 1)
                    if hh:
                        act.wait_ge(y_e, 4 * i + 2)
                    act.activation(E[:, 0, :], bank(4 if hh else 1), ACT.Sqrt, scale=1.0 / DV, bias=EPST[:]).then_inc(go_rt, 1)
                    act.activation(SG[:, bass.ds(4 * i + 2 * hh, 2), :], SG[:, bass.ds(4 * i + 2 * hh, 2), :], ACT.Silu).then_inc(g_si, 1)

                act.wait_ge(b_done, GH)
                decays(0)
                operands(0)
                for hh in range(2):
                    for m in range(TT):
                        if m % 2:
                            act.wait_ge(tile_done, tile_no(GK + 4 + 2 * hh, i, m // 2 + 1, 12))
                        else:
                            act.wait_ge(gv_mm, 4 * i + (2 * hh + m // 2 + 1))
                        act.activation(GVH[:, m, hh * DV:(hh + 1) * DV], bank(4 + m, DV, DV * hh), ACT.Copy).then_inc(gv_hi, 1)
                    for j in range(2 * hh, 2 * hh + 2):
                        split_hi(GK + 8, i, j, 12)
                attention(0)
                decays(1)
                operands(1)
                out_gate(0, 2)
                states(0)
                out_gate(1, 0)
                attention(1)
                squares(0)
                out_gate(2, 0)
                root_silu(0)
                states(1)
                out_gate(3, 0)
                squares(1)
                root_silu(1)
            for c in range(KC):
                act.wait_ge(y_e, c + 1)
                act.activation(YH[:, c, :], SG[:, c, :], ACT.Copy).then_inc(y_hi, 1)
            with act.Fori(0, 2) as i:
                for j in range(4):
                    act.wait_ge(tile_done, tile_no(GG + 1, i, j))
                    act.activation(GSIG[:, 4 * i + j, :], bank(j), ACT.Sigmoid).then_inc(gg_s, 1)
                    split_hi(GG + 4, i, j)
            with act.Fori(0, 2) as i:
                for j in range(4):
                    c = 4 * i + j
                    act.wait_ge(tile_done, tile_no(BG + 1, i, j))
                    split_hi(BG + 4, i, j)
                    act.wait_ge(x_e, c + 1)
                    act.activation(UH[:, c, :], E[:, j % 2, :], ACT.Copy).then_inc(x_hi, 1)
            with act.Fori(0, 2) as i:
                for j in range(4):
                    c = 4 * i + j
                    act.wait_ge(norm["h"], so_far(2, "h") + c + 1)
                    act.wait_ge(norm["acc"], so_far(2, "acc") + c + 1)
                    act.activation(SQ[:, j % 2, :], HT[:, c, :], ACT.Square).then_inc(norm["sq"], 1)
                    act.activation(YH[:, c, :], HT[:, c, :], ACT.Copy, scale=COLS[:, bass.ds(4 * i + (ROW["norm2"] + j), 1)])\
                        .then_inc(norm["hi"], 1)
                    split_hi(WO + 4, i, j)
            root(2, 4)

            def quarter(i):
                t0 = FF + 48 * (i is None)
                at8 = lambda k: 24 + k if i is None else 8 * i + k
                for b in range(8):
                    j = b % 4
                    act.wait_ge(tile_done, tile_no(t0 + (b // 4) * 4 + 1, i, j, 16))
                    if b >= 2:
                        act.wait_ge(f_ylo, at8(b - 1))
                    act.activation(E[:, b % 2, :], bank(j), ACT.Relu).then_inc(f_r, 1)
                    split_hi(t0 + (b // 4) * 4 + 4, i, j, 16)
                    act.wait_ge(f_r, at8(b + 1))
                    act.activation(UH[:, b, :], E[:, b % 2, :], ACT.Square).then_inc(f_sq, 1)
                act.wait_ge(f_ylo, at8(8))
                for b in range(8 if i is not None else 4):
                    j = b % 4
                    act.wait_ge(tile_done, tile_no(t0 + 8 + (b // 4) * 4 + 1, i, j, 16))
                    split_hi(t0 + (b // 4) * 4 + 12, i, j, 16)

            with act.Fori(0, 3) as i:
                quarter(i)
            quarter(None)

            for m in range(8):
                act.wait_ge(out_t, m + 1)
                act.activation(OUT[:, m % 4, (m // 4) * T:(m // 4 + 1) * T], bank((m + 4) % 8), ACT.Copy).then_inc(out_c, 1)

        @block.vector
        def _(v):
            steps = Steps(link_s)

            def link(ins):
                ins.then_inc(link_s, 1)
                steps.k += 1
                v.wait_ge(link_s, steps.now())

            v.memset(ONES[:], 1.0).then_inc(ones_set, 1)
            v.memset(EPST[:], EPS).then_inc(ones_set, 1)
            v.memset(RSC[:], 0.0).then_inc(ones_set, 1)
            v.wait_ge(cols_t, 1)
            v.tensor_copy(COLS[:, 0:NROWS], bank(7, NROWS)).then_inc(cols_done, 1)
            v.wait_ge(cols_done, 1)
            v.wait_ge(row_ss, TT + 1)
            link(v.reciprocal(RSC[:, 0:TT], RSC[:, 0:TT]))
            v.wait_ge(s_const, 16)
            for m in range(TT):
                v.tensor_scalar(DIAG[:, m, :], IDENT[:], RSC[:, m:m + 1], None, ALU.mult).then_inc(diag_done, 1)
            v.wait_ge(rs_mm, 1)
            v.wait_ge(x_copied, KC)
            for c in range(KC):
                v.tensor_tensor(XN[:, c, :], HT[:, c, :], bank(3), ALU.mult).then_inc(xn_done, 1)
            v.wait_ge(row_ss, 8)
            link(v.reciprocal(RSC[:, TT:6], RSC[:, TT:6]))
            for m in range(TC // P):
                v.tensor_scalar(CTOK[:, m, :], CTOK[:, m, :], RSC[:, TT + m:TT + m + 1], None, ALU.mult).then_inc(x_scaled, 1)
            v.wait_ge(bias_mm, 1)
            v.wait_ge(s_t5, 48)
            v.tensor_tensor(BROW[:], PB[0:MH, 4 * T:4 * T + TOEP], MROW[:], ALU.add).then_inc(bias_row, 1)
            b0 = ROW["b_ada"]
            v.wait_ge(ada_t, 4)
            mod = bank(7, 32).rearrange("p (c n) -> p c n", n=2)
            v.tensor_tensor(ADAL[0][:, 0:16], mod[:, 0:16, 0], COLS[:, b0:b0 + 16], ALU.add)
            link(v.tensor_tensor(ADAC[:], mod[:, 0:16, 1], COLS[:, b0:b0 + 16], ALU.add))
            g0 = ROW["norm_g"]
            v.scalar_tensor_tensor(MULL[0][:], ADAL[0][:, 8:16], 1.0, COLS[:, g0:g0 + 8], ALU.add, ALU.mult)
            v.scalar_tensor_tensor(MULC[:], ADAC[:, 8:16], 1.0, COLS[:, g0:g0 + 8], ALU.add, ALU.mult).then_inc(mod_done, 1)
            v.wait_ge(mod_done, 1)
            v.wait_ge(xn_done, KC)

            for n in range(2 * KC + 1):
                if n < 2 * KC:
                    c, lat = n % KC, n < KC
                    mul, add = (MULL[0], ADAL[0]) if lat else (MULC, ADAC)
                    if not lat:
                        v.wait_ge(xn_t, c + 1)
                    if n >= 2:
                        v.wait_ge(u0_lo, n - 1)
                    v.tensor_scalar(E[:, n % 2, 0:T if lat else TC], XN[:, c, :] if lat else bank(4 + c % 2, TC),
                                    mul[:, c:c + 1], add[:, c:c + 1], ALU.mult, ALU.add).then_inc(u0_e, 1)
                if n >= 1:
                    m = n - 1
                    c, lat = m % KC, m < KC
                    hi, lo = (UH, UL) if lat else (UCH, UCL)
                    v.wait_ge(u0_e, n)
                    v.wait_ge(u0_hi, n)
                    v.tensor_tensor(lo[:, c, :], E[:, m % 2, 0:T if lat else TC], f(hi[:, c, :]), ALU.subtract).then_inc(u0_lo, 1)
            swap = [16 + x for x in range(16)] + list(range(16))

            def rotate(out, src, tmp):
                v.tensor_tensor(out, src, COS[:], ALU.mult)
                link(v.stream_shuffle(tmp, src, swap))
                link(v.tensor_tensor(tmp, tmp, SIN[:], ALU.mult))
                return v.tensor_tensor(out, out, tmp, ALU.add)

            link(v.tensor_scalar(QGAIN[:], COLS[:, ROW["q_norm"]:ROW["q_norm"] + 1], MD ** -0.5, None, ALU.mult))

            def modulation(r):
                v.wait_ge(s_adaw[r % 2], 16 * (2 + r // 2 + 1))
                if r >= 3:
                    v.wait_ge(ada_mm, 4 + r - 2)
                acc, w = AACC[r % 3][:], AD[0] if r == 1 else AB[r % 2]
                link(v.tensor_scalar(acc, w[:, 0, :], CACT[:, 0, 0:1], None, ALU.mult))
                for k in range(1, KC):
                    ins = v.scalar_tensor_tensor(acc, w[:, k, :], CACT[:, k, 0:1], acc, ALU.mult, ALU.add)
                    if k < KC - 1:
                        link(ins)
                ins.then_inc(ada_used, 1)

            for r in range(3):
                modulation(r)

            v.wait_ge(s_rope, 32)
            v.wait_ge(tile_done, 4)
            rotate(KP[:, TC:TK], bank(3)[0:ROPE, :], E[0:ROPE, 0, :]).then_inc(a_n, 1)
            gq, gk = ROW["g_qa"], ROW["g_kva"]
            modulation(3)
            v.wait_ge(a_sqrt, 1)
            link(v.reciprocal(RQ[:], RQ[:]))
            v.scalar_tensor_tensor(CQ[:, 0, :], CQ[:, 0, :], COLS[:, gq:gq + 1], RQ[:], ALU.mult, ALU.mult)
            v.scalar_tensor_tensor(CQ[:, 1, :], CQ[:, 1, :], COLS[:, gq + 1:gq + 2], RQ[:], ALU.mult, ALU.mult).then_inc(a_n, 1)
            modulation(4)
            v.wait_ge(a_sqrt, 2)
            link(v.reciprocal(RKV[:], RKV[:]))
            v.scalar_tensor_tensor(CK[:], CK[:], COLS[:, gk:gk + 1], RKV[:], ALU.mult, ALU.mult).then_inc(a_n, 1)
            modulation(5)
            for n, (lo, hi, src) in enumerate(((KPL, KPH, KP), (CQL, CQH, CQ), (CKL, CKH, CK))):
                v.wait_ge(a_hi, n + 1)
                v.tensor_tensor(lo[:], src[:], f(hi[:]), ALU.subtract).then_inc(a_lo, 1)

            v.wait_ge(ada_mm, 10)
            mod = bank(5, 64).rearrange("p (c n) -> p c n", n=2)
            v.tensor_tensor(ADAL[0][:, 16:24], mod[:, 0:8, 0], COLS[:, b0 + 16:b0 + 24], ALU.add)
            link(v.tensor_tensor(ADAL[1][:, 0:16], mod[:, 8:24, 0], COLS[:, b0 + 24:b0 + 40], ALU.add))
            link(v.scalar_tensor_tensor(MULL[1][:], ADAL[1][:, 8:16], 1.0, COLS[:, g0 + 8:g0 + 16], ALU.add, ALU.mult))

            with v.Fori(0, 2) as i:
                steps.loop(i, 4 * 10)

                def unit(j, u):
                    par = j % 2
                    v.wait_ge(un_hi, UPR * i + unit_no(j, u))
                    b = unit_bank(j, u)
                    if u == 0:
                        v.tensor_tensor(QNL[:, par, :], bank(b), f(QNH[:, par, :]), ALU.subtract).then_inc(un_lo, 1)
                    elif u == 1:
                        v.tensor_tensor(QPL[:, par, :], QPF[:], f(QPH[:, par, :]), ALU.subtract).then_inc(un_lo, 1)
                    elif u == 2:
                        v.tensor_tensor(KNL[par][:, TC:TK], bank(b), f(KNH[par][:, TC:TK]), ALU.subtract).then_inc(un_lo, 1)
                    elif u == 3:
                        v.tensor_tensor(KNL[par][:, 0:TC], bank(b, TC), f(KNH[par][:, 0:TC]), ALU.subtract).then_inc(un_lo, 1)
                    else:
                        blocks, n = (slice(0, 4), T) if u == 4 else (slice(4, 6), TC)
                        v.tensor_tensor(VAL[:, blocks, :], bank(b, n).rearrange("p (k n) -> p k n", n=P), f(VAH[:, blocks, :]), ALU.subtract)\
                            .then_inc(un_lo, 1)

                def scale(j, q):
                    n, par = 16 * i + (4 * j + q), q % 2
                    v.wait_ge(s_exp, n + 1)
                    link(v.reciprocal(PSUM_[:, 2 + par:3 + par], PSUM_[:, par:par + 1]))
                    v.tensor_scalar(PA[:, par, :], PA[:, par, :], PSUM_[:, 2 + par:3 + par], None, ALU.mult).then_inc(s_scaled, 1)

                def turned(j, q):
                    n = 16 * i + (4 * j + q)
                    v.wait_ge(t_hi, n + 1)
                    v.tensor_tensor(PTL[:, :, q * P:(q + 1) * P], PB[:, 2 * T:2 * T + TK].rearrange("p (k n) -> p k n", n=P),
                                    f(PTH[:, :, q * P:(q + 1) * P]), ALU.subtract).then_inc(t_lo, 1)

                def top(j, q):
                    n, par = 16 * i + (4 * j + q), q % 2
                    v.wait_ge(s_mm, n + 1)
                    link(v.reduce_max(NMAX[:, 2 + par:3 + par], PB[:, (4 + 2 * par) * T:(4 + 2 * par) * T + TK], AX))
                    v.tensor_scalar(NMAX[:, par:par + 1], NMAX[:, 2 + par:3 + par], -MLA_SCALE, None, ALU.mult).then_inc(s_max, 1)

                def rope(j):
                    if j:
                        v.wait_ge(un_raw, 3 * i + j)
                    else:
                        v.wait_ge(un_mm, (UPR - 4) * i + unit_mm_no(0, 1))
                    rotate(QPF[:], QPR[:] if j else bank(unit_bank(0, 1))[0:ROPE, :], SQ[0:ROPE, 0, :]).then_inc(un_e, 1)

                def output(j):
                    v.wait_ge(o_mm, 4 * i + (j + 1))
                    v.tensor_tensor(E[:, 1, :], bank(1), SG[:, 4 * i + j, :], ALU.mult).then_inc(o_e, 1)

                def output_lo(j):
                    v.wait_ge(o_hi, 4 * i + (j + 1))
                    v.tensor_tensor(UL[:, 4 * i + j, :], E[:, 1, :], f(UH[:, 4 * i + j, :]), ALU.subtract).then_inc(o_lo, 1)

                rope(0)
                for u in first_units:
                    unit(0, u)
                top(0, 0)
                unit(0, 4)
                scale(0, 0)
                top(0, 1)
                scale(0, 1)
                for j in range(4):
                    nxt = j < 3
                    top(j, 2)
                    if nxt:
                        rope(j + 1)
                        unit(j + 1, 1)
                    if j:
                        output(j - 1)
                    if nxt:
                        unit(j + 1, 0)
                    turned(j, 0)
                    if nxt:
                        unit(j + 1, 2)
                    scale(j, 2)
                    top(j, 3)
                    if nxt:
                        unit(j + 1, 3)
                    else:
                        unit(3, 4)
                    turned(j, 1)
                    scale(j, 3)
                    if not nxt:
                        unit(3, 5)
                    if j:
                        output_lo(j - 1)
                    if nxt:
                        unit(j, 4 if j else 5)
                        top(j + 1, 0)
                    turned(j, 2)
                    if nxt:
                        scale(j + 1, 0)
                        top(j + 1, 1)
                        if j:
                            unit(j, 5)
                    turned(j, 3)
                    if nxt:
                        scale(j + 1, 1)
                output(3)
                output_lo(3)
            steps.leave(2)

            def residual(n, t0, gate):
                with v.Fori(0, 2) as i:
                    for j in range(4):
                        c = 4 * i + j
                        v.wait_ge(tile_done, tile_no(t0 + 1, i, j))
                        v.scalar_tensor_tensor(HT[:, c, :], bank(j), gate[:, bass.ds(4 * i + (16 + j), 1)], HT[:, c, :], ALU.mult, ALU.add)\
                            .then_inc(norm["h"], 1)

            def rstd(n):
                v.wait_ge(norm["sqrt"], so_far(n, "sqrt") + 1)
                v.reciprocal(RS[:], RS[:]).then_inc(norm["rstd"], 1)
                v.wait_ge(norm["rstd"], so_far(n, "rstd") + 1)

            residual(0, MO, ADAL[0])
            rstd(0)
            for c in range(KC + 1):
                if c < KC:
                    if c >= 2:
                        v.wait_ge(norm["lo"], so_far(0, "lo") + c - 1)
                    v.scalar_tensor_tensor(E[:, c % 2, :], HT[:, c, :], MULL[1][:, c:c + 1], RS[:], ALU.mult, ALU.mult).then_inc(norm["e"], 1)
                if c >= 1:
                    m = c - 1
                    v.wait_ge(norm["hi"], so_far(0, "hi") + c)
                    v.scalar_tensor_tensor(UL[:, m, :], E[:, m % 2, :], ADAL[1][:, m:m + 1], f(UH[:, m, :]), ALU.add, ALU.subtract)\
                        .then_inc(norm["lo"], 1)
            v.wait_ge(norm["lo"], KC)
            for r in range(6, 8):
                modulation(r)
            v.wait_ge(df_hi, 1)
            v.tensor_tensor(CDL[:], CDR[:], f(CDH[:]), ALU.subtract).then_inc(df_lo, 1)
            v.wait_ge(df_hi, 2)
            v.tensor_tensor(DFL[:], DFR[:], f(DFH[:]), ALU.subtract).then_inc(df_lo, 1)
            v.wait_ge(ada_mm, 12)
            link(v.tensor_tensor(ADAL[1][:, 16:24], mod[:, 24:32, 0], COLS[:, b0 + 40:b0 + 48], ALU.add))
            with v.Fori(0, 2) as i:
                def z_in(j):
                    v.wait_ge(z_raw, 4 * i + (j + 1))
                    if j >= 2:
                        v.wait_ge(z_lo, 4 * i + (j - 1))
                    v.tensor_tensor(ZF[:, j % 2, 0:HALF], ZR[:, j % 2, 0:HALF], ZR[:, j % 2, HALF:T], ALU.add)
                    v.tensor_tensor(ZF[:, j % 2, HALF:T], ZR[:, j % 2, 0:HALF], ZR[:, j % 2, HALF:T], ALU.subtract).then_inc(z_fold, 1)
                    v.wait_ge(z_hi, 4 * i + (j + 1))
                    v.tensor_tensor(ZL[:, j % 2, :], ZF[:, j % 2, :], f(ZH[:, j % 2, :]), ALU.subtract).then_inc(z_lo, 1)

                def a_in(j):
                    v.wait_ge(d_hi, 4 * i + (j + 1))
                    v.tensor_tensor(AL[:, j % 2, :], PB[:, 4 * T:6 * T], f(AH[:, j % 2, :]), ALU.subtract).then_inc(d_lo, 1)

                def y_in(j):
                    v.wait_ge(f_mm, 4 * i + (j + 1))
                    if j >= 2:
                        v.wait_ge(f_lo, 4 * i + (j - 1))
                    two = "p (t two) -> p two t"
                    v.tensor_tensor(E[:, j % 2, :].rearrange(two, two=2), bank(6 + j % 2).rearrange("p (two t) -> p two t", two=2),
                                    SG[:, 4 * i + j, :].rearrange(two, two=2), ALU.mult).then_inc(f_e, 1)
                    v.wait_ge(f_hi, 4 * i + (j + 1))
                    v.tensor_tensor(YL[:, 4 * i + j, :], E[:, j % 2, :], f(YH[:, 4 * i + j, :]), ALU.subtract).then_inc(f_lo, 1)

                z_in(0)
                z_in(1)
                a_in(0)
                z_in(2)
                a_in(1)
                y_in(0)
                z_in(3)
                a_in(2)
                y_in(1)
                a_in(3)
                y_in(2)
                y_in(3)
            residual(1, FO, ADAL[1])
            fg, g1 = ROW["final_g"], ROW["norm1"]
            link(v.tensor_tensor(MULC[:], COLS[:, fg:fg + 8], COLS[:, g1:g1 + 8], ALU.mult))
            v.memset(DUMMY[:, 1:2], EPS * EPS)
            v.wait_ge(norm["ss"], so_far(1, "ss") + 1)
            v.wait_ge(s2_ss, 1)
            link(v.tensor_copy(RS[:], bank(4)))
            v.scalar_tensor_tensor(RS[:], RS[:], EPS, bank(5), ALU.mult, ALU.add).then_inc(s2_mix, 1)
            rstd(1)
            for c in range(KC + 1):
                if c < KC:
                    if c >= 2:
                        v.wait_ge(norm["lo"], so_far(1, "lo") + c - 1)
                    v.scalar_tensor_tensor(E[:, c % 2, :], HT[:, c, :], MULC[:, c:c + 1], RS[:], ALU.mult, ALU.mult).then_inc(norm["e"], 1)
                if c >= 1:
                    m = c - 1
                    v.wait_ge(norm["hi"], so_far(1, "hi") + c)
                    v.tensor_tensor(UL[:, m, :], E[:, m % 2, :], f(UH[:, m, :]), ALU.subtract).then_inc(norm["lo"], 1)
            v.wait_ge(norm["lo"], so_far(1, "lo") + KC)
            v.wait_ge(r1_sqrt, 1)
            link(v.reciprocal(SQ[:, 0, :], SQ[:, 0, :]))
            for c in range(KC):
                v.scalar_tensor_tensor(HT[:, c, :], HT[:, c, :], COLS[:, fg + c:fg + c + 1], SQ[:, 0, :], ALU.mult, ALU.mult)
            for m in range(TT):
                v.wait_ge(v_hi, m + 1)
                v.tensor_tensor(VL[:, m, :], bank(m), f(VH[:, m, :]), ALU.subtract).then_inc(v_lo, 1)
            v.wait_ge(s_bias, 16)
            with v.Fori(0, 2) as i:
                steps.loop(i, 36)

                v.wait_ge(q_rt, i + 1)
                v.reciprocal(RROW[:], RROW[:]).then_inc(q_rs, 1)

                def normed(j):
                    v.wait_ge(q_sp, 4 * i + (j + 1))
                    if j >= 2:
                        v.wait_ge(q_lo, 4 * i + (j - 1))
                    link(v.tensor_scalar(E[:, j % 2, :], bank(j), QGAIN[:] if j < 2 else COLS[:, ROW["k_norm"]:ROW["k_norm"] + 1], None,
                                         ALU.mult))
                    v.tensor_tensor(E[:, j % 2, :], bank(5 - j % 2), E[:, j % 2, :], ALU.mult).then_inc(q_e, 1)

                def low(j):
                    v.wait_ge(q_hi, 4 * i + (j + 1))
                    v.tensor_tensor(QKL[:, j, :], E[:, j % 2, :], f(QKH[:, j, :]), ALU.subtract).then_inc(q_lo, 1)

                normed(0)
                normed(1)
                low(0)
                normed(2)
                low(1)
                normed(3)
                low(2)
                low(3)

                def top(m, q):
                    x, w = q, (q + 1) * P
                    v.wait_ge(s_mm, 16 * i + (M0 + 4 * m + q + 1))
                    link(v.tensor_tensor(MP[:, m_slot(q)], bank(4 + q % 2, w), BIAS[:, 4 * i + m, T - w:T], ALU.add))
                    v.reduce_max(MSTAT[:, x:x + 1], MP[:, m_slot(q)], AX, negate=True).then_inc(s_max, 1)

                def scale(m, q):
                    x, w = q, (q + 1) * P
                    v.wait_ge(s_exp, 16 * i + (M0 + 4 * m + q + 1))
                    link(v.reciprocal(NMAX[:, x:x + 1], MSTAT[:, 4 + x:5 + x]))
                    v.tensor_scalar(MP[:, m_slot(q)], MP[:, m_slot(q)], NMAX[:, x:x + 1], None, ALU.mult).then_inc(s_scaled, 1)

                def turned(m, q):
                    v.wait_ge(t_hi, 16 * i + (M0 + 4 * m + q + 1))
                    s = slice(q * P, (q + 1) * P)
                    v.tensor_tensor(MTL[:, 0:q + 1, s], bank(6 + q % 2, (q + 1) * P).rearrange("p (k n) -> p k n", n=P),
                                    f(MTH[:, 0:q + 1, s]), ALU.subtract).then_inc(t_lo, 1)

                def output(m):
                    rows = slice(MD * (m % 2), MD * (m % 2 + 1))
                    v.wait_ge(o_hi, 4 * i + (HEADS + m + 1))
                    v.tensor_tensor(YL[rows, 2 * i + m // 2, :], bank(m % 2)[rows, :], f(YH[rows, 2 * i + m // 2, :]), ALU.subtract)\
                        .then_inc(o_lo, 1)

                top(0, 0)
                top(0, 1)
                scale(0, 0)
                for m in range(4):
                    top(m, 2)
                    scale(m, 1)
                    top(m, 3)
                    turned(m, 0)
                    scale(m, 2)
                    turned(m, 1)
                    if m:
                        output(m - 1)
                    if m < 3:
                        top(m + 1, 0)
                    scale(m, 3)
                    turned(m, 2)
                    if m < 3:
                        top(m + 1, 1)
                        scale(m + 1, 0)
                    turned(m, 3)
                output(3)
            steps.leave(2)
            v.wait_ge(l_hi, 1)
            v.tensor_tensor(LWL[:], LWR[:], f(LWH[:]), ALU.subtract).then_inc(l_lo, 1)
            for j in range(4):
                v.wait_ge(tile_done, BM + j + 1)
                v.wait_ge(gm_s, KC + 2 * j + 2)
                v.tensor_tensor(MX[:, 2 * j, :], MX[:, 2 * j, :], bank(j), ALU.mult)
                v.tensor_tensor(MX[:, 2 * j + 1, :], MX[:, 2 * j + 1, :], bank(4 + j), ALU.mult).then_inc(bm_e, 1)
            link(v.memset(RST[:], 1.0))
            link(v.memset(RST[:].rearrange("p (n c) -> p n c", c=CH)[:, :, 0:1], 0.0))
            v.memset(AMF[:], 0.0).then_inc(on_done, 1)
            gb = ROW["gate_bias"]
            for h in range(GH):
                v.wait_ge(l_up, h + 1)
                v.tensor_scalar(MN[:, h, :], bank(h), COLS[:, gb + h:gb + h + 1], 0.0, ALU.add, ALU.min).then_inc(l_min, 1)
            v.wait_ge(l_ln, 1)
            v.wait_ge(l_min, GH)
            link(v.tensor_tensor(MN[:], MN[:], BT[:], ALU.subtract))
            for h in range(GH):
                v.tensor_tensor_scan(BT[:, h, :], RST[:], MN[:, h, :], 0.0, ALU.mult, ALU.add).then_inc(b_done, 1)
            v.wait_ge(s_mask, 48)
            with v.Fori(0, 2) as i:
                steps.loop(i, 2 * 7)

                def operands(hh):
                    n = 2 * i + hh
                    v.wait_ge(g_ex, 6 * i + (3 * hh + 1))
                    v.scalar_tensor_tensor(E[:, 0, :], GQK[:, hh, :], DK ** -0.5, EB[:], ALU.mult, ALU.mult).then_inc(g_e, 1)
                    v.wait_ge(g_ex, 6 * i + (3 * hh + 2))
                    v.tensor_tensor(E[:, 1, :], GQK[:, 2 + hh, :], EN[:], ALU.mult).then_inc(g_e, 1)
                    b3 = BT[:, n, :].rearrange("p (n c) -> p n c", c=CH)
                    v.tensor_tensor(SQ[:, 0, :].rearrange("p (n c) -> p n c", c=CH), b3[:, :, CH - 1:CH].to_broadcast([P, NCH, CH]), b3,
                                    ALU.subtract).then_inc(kd_d, 1)
                    v.wait_ge(g_hi, 4 * i + (2 * hh + 1))
                    v.tensor_tensor(QDL[hh][:], E[:, 0, :], f(QDH[hh][:]), ALU.subtract).then_inc(g_lo, 1)
                    v.wait_ge(g_hi, 4 * i + (2 * hh + 2))
                    v.tensor_tensor(KIL[:], E[:, 1, :], f(KIH[:]), ALU.subtract).then_inc(g_lo, 1)
                    v.wait_ge(kd_x, n + 1)
                    v.tensor_tensor(SQ[:, 1, :], GQK[:, 2 + hh, :], SQ[:, 0, :], ALU.mult).then_inc(kd_e, 1)

                def attention(hh):
                    n = 2 * i + hh
                    v.wait_ge(at_mm, n + 1)
                    v.tensor_copy(DUMMY[:, 0:1], EPST[:])
                    v.copy_predicated(AMF[:].rearrange("p (k n) -> p k n", n=P),
                                      CMASK[:].unsqueeze(1).to_broadcast([P, TT, P]),
                                      bank(0).rearrange("p (k n) -> p k n", n=P)).then_inc(am_f, 1)
                    v.wait_ge(am_hi, n + 1)
                    v.tensor_tensor(AML[:], AMF[:], f(AMH[:]), ALU.subtract).then_inc(am_lo, 1)
                    v.wait_ge(kd_hi, n + 1)
                    v.tensor_tensor(KDL[:], bank(1).rearrange("p (k n) -> p k n", n=P), f(KDH[:]), ALU.subtract).then_inc(kd_lo, 1)

                def states(hh):
                    n = 2 * i + hh
                    v.wait_ge(kv_mm, n + 1)
                    ins = v.tensor_copy(SALL[:, 0, :], kv_bank(0))
                    for c in range(1, NCH - 1):
                        link(ins)
                        ins = v.scalar_tensor_tensor(SALL[:, c, :], SALL[:, c - 1, :], DEC[:, hh, c:c + 1], kv_bank(c), ALU.mult, ALU.add)
                    ins.then_inc(st_f, 1)

                def states_lo(hh):
                    v.wait_ge(st_hi, 2 * i + (hh + 1))
                    v.tensor_tensor(SL[:], SALL[:], f(SH[:]), ALU.subtract).then_inc(st_lo, 1)

                def normed(hh):
                    n = 2 * i + hh
                    v.wait_ge(go_rt, n + 1)
                    link(v.reciprocal(E[:, 0, :], E[:, 0, :]))
                    og = ROW["out_norm"]
                    tmp = (E[:, 1, :], E[:, 0, :])
                    for x in range(2):
                        v.scalar_tensor_tensor(tmp[x], bank(2 + x), COLS[:, og + x:og + x + 1], E[:, 0, :], ALU.mult, ALU.mult).then_inc(on_done, 1)
                    v.wait_ge(on_done, 4 * i + (2 * hh + 3))
                    v.wait_ge(g_si, n + 1)
                    for x in range(2):
                        c = 4 * i + 2 * hh + x
                        v.tensor_tensor(SG[:, c, :], SG[:, c, :], tmp[x], ALU.mult).then_inc(y_e, 1)

                v.wait_ge(g_raw, 4 * i + 4)
                operands(0)
                for hh in range(2):
                    for m in range(TT):
                        v.wait_ge(gv_hi, 8 * i + (4 * hh + m + 1))
                        vals = slice(hh * DV, (hh + 1) * DV)
                        v.tensor_tensor(GVL[:, m, vals], bank(4 + m, DV, DV * hh), f(GVH[:, m, vals]), ALU.subtract).then_inc(gv_lo, 1)
                attention(0)
                operands(1)
                states(0)
                states_lo(0)
                attention(1)
                states(1)
                normed(0)
                states_lo(1)
                normed(1)
                v.wait_ge(y_e, 4 * i + 4)
            steps.leave(2)
            for c in range(KC):
                v.wait_ge(y_hi, c + 1)
                v.tensor_tensor(YL[:, c, :], SG[:, c, :], f(YH[:, c, :]), ALU.subtract).then_inc(y_lo, 1)
            with v.Fori(0, 2) as i:
                steps.loop(i, 4)
                for j in range(4):
                    c = 4 * i + j
                    v.wait_ge(tile_done, tile_no(BG + 1, i, j))
                    v.wait_ge(gg_s, c + 1)
                    link(v.tensor_tensor(E[:, j % 2, :], bank(j), GSIG[:, c, :], ALU.mult))
                    v.tensor_tensor(E[:, j % 2, :], E[:, j % 2, :], MX[:, c, :], ALU.add).then_inc(x_e, 1)
                    v.wait_ge(x_hi, c + 1)
                    v.tensor_tensor(UL[:, c, :], E[:, j % 2, :], f(UH[:, c, :]), ALU.subtract).then_inc(x_lo, 1)
            steps.leave(2)
            with v.Fori(0, 2) as i:
                for j in range(4):
                    c = 4 * i + j
                    v.wait_ge(tile_done, tile_no(WO + 1, i, j))
                    v.tensor_tensor(HT[:, c, :], bank(j), HT[:, c, :], ALU.add).then_inc(norm["h"], 1)
                    v.wait_ge(norm["hi"], so_far(2, "hi") + c + 1)
                    v.scalar_tensor_tensor(YL[:, c, :], HT[:, c, :], COLS[:, bass.ds(4 * i + (ROW["norm2"] + j), 1)], f(YH[:, c, :]),
                                           ALU.mult, ALU.subtract).then_inc(norm["lo"], 1)
            rstd(2)
            link(v.tensor_tensor(RS[:], RS[:], RS[:], ALU.mult))

            def quarter(i):
                t0 = FF + 48 * (i is None)
                at8 = lambda k: 24 + k if i is None else 8 * i + k
                for b in range(8):
                    v.wait_ge(f_r, at8(b + 1))
                    link(v.tensor_tensor(SQ[:, b % 2, :], E[:, b % 2, :], E[:, b % 2, :], ALU.mult))
                    v.wait_ge(f_sq, at8(b + 1))
                    v.tensor_tensor(UL[:, b, :], SQ[:, b % 2, :], f(UH[:, b, :]), ALU.subtract).then_inc(f_ylo, 1)
                for b in range(8):
                    v.wait_ge(tile_done, tile_no(t0 + 8 + (b // 4) * 4 + 1, i, b % 4, 16))
                    link(v.tensor_tensor(FTMP[:, b % 2, :], bank(b % 4), RS[:], ALU.mult))
                    v.tensor_tensor(HT[:, b, :], FTMP[:, b % 2, :], HT[:, b, :], ALU.add).then_inc(f_h, 1)
                    if b == 7:
                        v.wait_ge(f_h, at8(8))

            with v.Fori(0, 3) as i:
                steps.loop(i, 16)
                quarter(i)
            steps.leave(3)
            quarter(None)

        @block.tensor
        def _(pe):
            def three(out, ah, al, bh, bl, first, last):
                pe.matmul(out, ah, bh, start=first, stop=False)
                pe.matmul(out, ah, bl, start=False, stop=False)
                return pe.matmul(out, al, bh, start=False, stop=last)

            def wsl(w, j, k):
                return w[:, j, k * P:(k + 1) * P]

            def product(t, j, xh, xl, n=KC, ready=None, before=0):
                pe.wait_ge(lo_done, t + 1)
                for k in range(n):
                    if ready is not None:
                        pe.wait_ge(ready, before + (k + 1))
                    mm = three(bank(j), wsl(WH, j, k), wsl(WL, j, k), xh[:, k, :], xl[:, k, :], k == 0, k == n - 1)
                mm.then_inc(tile_done, 1)

            def linear(t0, xh, xl, ready=None, before=0):
                with pe.Fori(0, 2) as i:
                    for j in range(4):
                        product(tile_no(t0, i, j), j, xh, xl, ready=ready if j == 0 else None, before=before)

            pe.wait_ge(s_const, 16)
            pe.wait_ge(s_vec, 16 * (len(VECS) + 2))
            pe.transpose(bank(7, NROWS), VROWS[:], IDENT[0:NROWS, 0:NROWS]).then_inc(cols_t, 1)
            pe.wait_ge(s_x, 16)
            for c in range(KC):
                if c >= 4:
                    pe.wait_ge(x_copied, c - 3)
                for m in range(TT):
                    mm = pe.transpose(bank(c % 4, P, m * P), XTOK[:, m, c * P:(c + 1) * P], IDENT[:])
                mm.then_inc(x_t, 1)

            def ada(q):
                if q < 4:
                    pe.wait_ge(s_adaw[q % 2], 16 * (q // 2 + 1))
                    if q >= 1:
                        pe.wait_ge(ada_row, q)
                    for k in range(KC):
                        mm = pe.matmul(bank(6)[0:2, :], CACT[:, k, :], AD[q % 2][:, k, :], start=k == 0, stop=k == KC - 1)
                    mm.then_inc(ada_mm, 1)
                if q >= 1:
                    pe.wait_ge(ada_row, q)
                    for b in range(4):
                        mm = pe.transpose(bank(7, 2, 2 * (4 * (q - 1) + b)), AROW[:, q - 1, b * P:(b + 1) * P], IDENT[0:2, 0:2])
                    mm.then_inc(ada_t, 1)

            pe.wait_ge(cact_done, 2)
            ada(0)
            pe.wait_ge(diag_done, TT)
            pe.wait_ge(x_copied, KC)
            for m in range(TT):
                mm = pe.matmul(bank(3, P, m * P), ONES[:], DIAG[:, m, :], start=True, stop=True)
            mm.then_inc(rs_mm, 1)
            ada(1)
            pe.wait_ge(s_t5, 48)
            pe.matmul(PB[0:MH, 4 * T:5 * T], T5[:], HOT[:, 0:T], start=True, stop=True)
            pe.matmul(PB[0:MH, 5 * T:5 * T + P], T5[:], HOT[:, T:TOEP], start=True, stop=True).then_inc(bias_mm, 1)
            for q in range(2, 5):
                ada(q)

            def turn_ctx(c):
                if c == 0:
                    pe.wait_ge(x_scaled, 2)
                    pe.wait_ge(bias_row, 1)
                if c >= 2:
                    pe.wait_ge(u0_e, KC + c - 1)
                for m in range(TC // P):
                    mm = pe.transpose(bank(4 + c % 2, P, m * P), CTOK[:, m, c * P:(c + 1) * P], IDENT[:])
                mm.then_inc(xn_t, 1)

            pe.wait_ge(xn_done, KC)
            for j in range(4):
                pe.wait_ge(lo_done, j + 1)
                if j == 2:
                    pe.wait_ge(u0_e, 2 * KC)
                for k in range(KC):
                    if j == 0:
                        pe.wait_ge(u0_lo, k + 1)
                    mm = three(bank(j), wsl(WH, j, k), wsl(WL, j, k), UH[:, k, :], UL[:, k, :], k == 0, k == KC - 1)
                    if j < 2 and k % 2 == 1:
                        turn_ctx(4 * j + k // 2)
                if j >= 2:
                    for k in range(KC):
                        pe.wait_ge(u0_lo, KC + k + 1)
                        mm = three(bank(2 + j, TC), wsl(WH, j, k), wsl(WL, j, k), UCH[:, k, :], UCL[:, k, :], k == 0, k == KC - 1)
                mm.then_inc(tile_done, 1)
                if j == 2:
                    for n in range(2):
                        pe.wait_ge(a_sq, n + 1)
                        pe.matmul(bank(6), ONES[:], SQ[:, n, :], start=n == 0, stop=n == 1).then_inc(a_ss, 1)
            pe.wait_ge(a_sq, 3)
            pe.matmul(bank(4, TC, TC), ONES[:], SQ[:, 1, 0:TC], start=True, stop=True).then_inc(a_ss, 1)
            pe.wait_ge(a_sq, 4)
            pe.matmul(bank(7), ONES[:], SQ[:, 0, :], start=True, stop=True).then_inc(a_ss, 1)
            def modulation(r):
                pe.wait_ge(ada_used, r + 1)
                for b in range(4):
                    mm = pe.matmul(bank(5, 2, 2 * (4 * r + b)), AACC[r % 3][:, b * P:(b + 1) * P], ONES[:, 0:2], start=True, stop=True)
                mm.then_inc(ada_mm, 1)

            pe.wait_ge(a_raw, 4)
            for r in range(8):
                if r == 3:
                    pe.wait_ge(a_n, 1)
                product(G1 + r, r % 4, UH, UL)
                for x in {1: (0, 1), 2: (2,), 4: (3,), 6: (4,), 7: (5,)}.get(r, ()):
                    modulation(x)

            pe.wait_ge(a_lo, 3)
            with pe.Fori(0, 2) as i:
                def unit(j, u):
                    if u == first_units[0]:
                        pe.wait_ge(lo_done, tile_no(HD + 1, i, j))
                    b = unit_bank(j, u)
                    if j and u == 0:
                        pe.wait_ge(un_raw, 3 * i + j)
                    elif (u == 2 and j >= 2) or (u == 4 and j == 3):
                        pe.wait_ge(o_e, 4 * i + (j if u == 4 else j - 1))
                    elif u == 4 and j == 0:
                        pe.wait_ge(lo_done, tile_no(HD + 3, i, 0))
                    elif u >= 4 or (j and u == 3) or (u == 1 and j >= 2):
                        before = {1: (j - 2, 5), 3: (j, 0), 4: (j + 1, 2), 5: (1, 2) if j == 0 else (j + 1, 3) if j < 3 else (2, 5)}[u]
                        pe.wait_ge(un_lo, UPR * i + unit_no(*before))
                    wq = lambda w, k, o: w[:, j, 192 * k + o:192 * k + o + P]
                    wk = lambda w, o: w[:, j, 2 * 192 + o:2 * 192 + o + P]
                    if u < 2:
                        for k in range(2):
                            mm = three(bank(b), wq(WH, k, NOPE * u), wq(WL, k, NOPE * u), CQH[:, k, :], CQL[:, k, :], k == 0, k == 1)
                    elif u == 2:
                        mm = three(bank(b), wk(WH, 0), wk(WL, 0), CKH[:, TC:TK], CKL[:, TC:TK], True, True)
                    elif u == 3:
                        mm = three(bank(b, TC), wk(WH, 0), wk(WL, 0), CKH[:, 0:TC], CKL[:, 0:TC], True, True)
                    else:
                        first = 4 * (u - 4)
                        for m in range(first, min(first + 4, TK // P)):
                            s = slice(m * P, (m + 1) * P)
                            mm = three(bank(b, P, (m - first) * P), CKH[:, s], CKL[:, s], wk(WH, P), wk(WL, P), True, True)
                    mm.then_inc(tile_done if u == 5 else un_mm, 1)

                def scores(j, q):
                    n, par = 16 * i + (4 * j + q), q % 2
                    if q == 0:
                        pe.wait_ge(un_lo, UPR * i + unit_no(j, 3))
                    if j or q >= 2:
                        pe.wait_ge(s_exp, n - 1)
                    s = slice(q * P, (q + 1) * P)
                    for b, (k0, k1) in enumerate(((0, T), (T, TK))):
                        out = bank(4 + 2 * par + b, k1 - k0)
                        three(out, QNH[:, j % 2, s], QNL[:, j % 2, s], KNH[j % 2][:, k0:k1], KNL[j % 2][:, k0:k1], True, False)
                        mm = three(out, QPH[:, j % 2, s], QPL[:, j % 2, s], KPH[:, k0:k1], KPL[:, k0:k1], False, True)
                    mm.then_inc(s_mm, 1)

                def turn(j, q):
                    n = 16 * i + (4 * j + q)
                    pe.wait_ge(s_scaled, n + 1)
                    if q >= 1:
                        pe.wait_ge(t_lo, n)
                    for k in range(TK // P):
                        mm = pe.transpose(bank(2, P, k * P), PA[:, q % 2, k * P:(k + 1) * P], IDENT[:])
                    mm.then_inc(t_mm, 1)

                def output(j, q0=0, q1=4):
                    if q0 == 0:
                        pe.wait_ge(un_lo, UPR * i + unit_no(j, 5))
                    pe.wait_ge(t_lo, 16 * i + (4 * j + q1))
                    s = slice(q0 * P, q1 * P)
                    for k in range(TK // P):
                        mm = three(bank(1, (q1 - q0) * P, q0 * P), VAH[:, k, :], VAL[:, k, :], PTH[:, k, s], PTL[:, k, s],
                                   k == 0, k == TK // P - 1)
                    if q1 == 4:
                        mm.then_inc(o_mm, 1)

                for u in first_units + (4,):
                    unit(0, u)
                scores(0, 0)
                scores(0, 1)
                for j in range(4):
                    nxt = j < 3
                    scores(j, 2)
                    if nxt:
                        unit(j + 1, 1)
                    if j:
                        output(j - 1)
                    if nxt:
                        unit(j + 1, 0)
                    turn(j, 0)
                    if nxt:
                        unit(j + 1, 2)
                    scores(j, 3)
                    if nxt:
                        unit(j + 1, 3)
                    else:
                        unit(3, 4)
                    turn(j, 1)
                    if nxt:
                        unit(j, 4 if j else 5)
                        scores(j + 1, 0)
                    else:
                        unit(3, 5)
                    turn(j, 2)
                    if nxt:
                        scores(j + 1, 1)
                        if j:
                            unit(j, 5)
                    else:
                        output(3, 0, 2)
                    turn(j, 3)
                output(3, 2, 3)
                output(3, 3, 4)

            linear(MO, UH, UL, ready=o_lo)

            def sums(n, b):
                pe.wait_ge(norm["acc"], so_far(n, "acc") + KC + 2)
                pe.matmul(bank(b), ONES[:], ACC[:], start=True, stop=True).then_inc(norm["ss"], 1)

            sums(0, 4)
            linear(FG, UH, UL, ready=norm["lo"], before=so_far(0, "lo"))
            for r in range(6, 8):
                modulation(r)
            pe.wait_ge(s_mask, 32)
            pe.wait_ge(df_lo, 2)
            with pe.Fori(0, 2) as i:
                def dims(j):
                    pe.wait_ge(z_lo, 4 * i + (j + 1))
                    if j >= 1:
                        pe.wait_ge(d_lo, 4 * i + j)
                    for q in range(4):
                        s = slice(q * P, (q + 1) * P)
                        mm = three(bank(4, 2 * GROUP, 2 * GROUP * q), ZH[:, j % 2, s], ZL[:, j % 2, s], CDH[:], CDL[:], True, True)
                    mm.then_inc(d_mm, 1)

                def toks(j):
                    pe.wait_ge(d_lo, 4 * i + (j + 1))
                    if j >= 2:
                        pe.wait_ge(f_e, 4 * i + (j - 1))
                    for odd in range(2):
                        for k in range(4):
                            q, sine = 2 * odd + k // 2, k % 2
                            s = slice(2 * GROUP * q + GROUP * sine, 2 * GROUP * q + GROUP * (sine + 1))
                            mat = 2 * (2 * odd + sine) + k // 2
                            mm = three(bank(6 + j % 2, HALF, HALF * odd), AH[:, j % 2, s], AL[:, j % 2, s],
                                       DFH[:, mat, :], DFL[:, mat, :], k == 0, k == 3)
                    mm.then_inc(f_mm, 1)

                def lin(j):
                    product(tile_no(FZ, i, j), j, UH, UL)

                lin(0)
                lin(1)
                dims(0)
                lin(2)
                dims(1)
                toks(0)
                lin(3)
                dims(2)
                toks(1)
                dims(3)
                toks(2)
                toks(3)
            linear(FO, YH, YL, ready=f_lo)

            sums(1, 4)
            pe.wait_ge(s2_acc, KC + 1)
            pe.matmul(bank(5), ONES[:], ACC2[:], start=True, stop=True).then_inc(s2_ss, 1)

            def rows_product(t0, m, b, ready=None, before=0):
                s = slice(m * P, (m + 1) * P)
                out = bank(b).rearrange("p (a n) -> p a n", n=P)
                for k in range(KC):
                    if ready is not None:
                        pe.wait_ge(ready, before + k + 1)
                    mm = three(out, UH[:, k, s], UL[:, k, s], WH[:, :, k * P:(k + 1) * P], WL[:, :, k * P:(k + 1) * P],
                               k == 0, k == KC - 1)
                mm.then_inc(tile_done, 1)

            pe.wait_ge(lo_done, MV + 4)
            for m in range(TT):
                rows_product(MV, m, m, ready=norm["lo"] if m == 0 else None, before=so_far(1, "lo"))
            with pe.Fori(0, 2) as i:
                def ss(j):
                    pe.wait_ge(q_sq, 4 * i + (j + 1))
                    pe.matmul(bank(4), HPICK[:, 96 - 32 * j:224 - 32 * j], SQ[:, j % 2, :], start=j == 0, stop=j == 3).then_inc(q_ss, 1)

                def spread(j):
                    if j >= 2:
                        pe.wait_ge(q_e, 4 * i + (j - 1))
                    rows = slice(32 * j, 32 * (j + 1))
                    pe.matmul(bank(5 - j % 2), HSPREAD[rows, :], RROW[rows, :], start=True, stop=True).then_inc(q_sp, 1)

                def gate(j, b, k0=0, k1=KC):
                    if k0 == 0:
                        pe.wait_ge(lo_done, tile_no(MQ + 5, i, j, 8))
                    for k in range(k0, k1):
                        mm = three(bank(b), wsl(WH, j, k), wsl(WL, j, k), UH[:, k, :], UL[:, k, :], k == 0, k == KC - 1)
                    if k1 == KC:
                        mm.then_inc(tile_done, 1)

                pe.wait_ge(o_lo, 4 * i + HEADS)
                for j in range(4):
                    product(tile_no(MQ, i, j, 8), j, UH, UL)
                    if j:
                        ss(j - 1)
                ss(3)
                gate(0, 6)
                pe.wait_ge(q_rs, i + 1)
                for j in range(4):
                    spread(j)
                gate(1, 7)

                def scores(m, q):
                    n, w = 16 * i + (M0 + 4 * m + q), (q + 1) * P
                    if m == 0 and q == 0:
                        pe.wait_ge(q_lo, 4 * i + 4)
                    if m or q >= 2:
                        pe.wait_ge(s_max, n - 1)
                    rows = slice(MD * (m % 2), MD * (m % 2 + 1))
                    s = slice(q * P, (q + 1) * P)
                    three(bank(4 + q % 2, w), QKH[rows, m // 2, s], QKL[rows, m // 2, s],
                          QKH[rows, 2 + m // 2, 0:w], QKL[rows, 2 + m // 2, 0:w], True, True).then_inc(s_mm, 1)

                def turn(m, q):
                    n = 16 * i + (M0 + 4 * m + q)
                    pe.wait_ge(s_scaled, n + 1)
                    if m or q >= 2:
                        pe.wait_ge(t_lo, n - 1)
                    for k in range(q + 1):
                        mm = pe.transpose(bank(6 + q % 2, P, k * P), MP[:, m_slot(q)][:, k * P:(k + 1) * P], IDENT[:])
                    mm.then_inc(t_mm, 1)

                def output(m):
                    pe.wait_ge(t_lo, 16 * i + (M0 + 4 * m + 4))
                    if m == 0:
                        pe.wait_ge(vs_done, 4 * i + 4)
                    for k in range(TT):
                        mm = three(bank(m % 2, T - k * P, k * P), VSH[:, m // 2, k, :], VSL[:, m // 2, k, :],
                                   MTH[:, k, k * P:T], MTL[:, k, k * P:T], k == 0, k == TT - 1)
                    mm.then_inc(o_mm, 1)

                scores(0, 0)
                scores(0, 1)
                for m in range(4):
                    scores(m, 2)
                    scores(m, 3)
                    if m:
                        output(m - 1)
                    turn(m, 0)
                    turn(m, 1)
                    if m < 3:
                        scores(m + 1, 0)
                    gate(2 + m // 2, 2 + m // 2, (m % 2) * KC // 2, (m % 2 + 1) * KC // 2)
                    turn(m, 2)
                    if m < 3:
                        scores(m + 1, 1)
                    turn(m, 3)
                output(3)
            def branch(j):
                pe.wait_ge(lo_done, BM + j + 1)
                for o in range(2):
                    for k in range(4):
                        s = slice(2 * P * k + P * o, 2 * P * k + P * (o + 1))
                        mm = three(bank(4 * o + j), WH[:, j, s], WL[:, j, s], YH[:, k, :], YL[:, k, :], k == 0, k == 3)
                mm.then_inc(tile_done, 1)

            pe.wait_ge(o_lo, HEADS + MH)
            branch(0)
            branch(1)
            pe.wait_ge(l_lo, 1)
            for k in range(KC):
                mm = three(bank(7), LWH[:, k, :], LWL[:, k, :], UH[:, k, :], UL[:, k, :], k == 0, k == KC - 1)
            mm.then_inc(l_mm, 1)
            branch(2)
            pe.wait_ge(s_low, 32)
            pe.wait_ge(l_cp, 1)
            branch(3)
            for h in range(GH):
                pe.wait_ge(bm_e, h + 1)
                pe.matmul(bank(h), GUP[:, h * DK:(h + 1) * DK], GLO[:], start=True, stop=True).then_inc(l_up, 1)
            pe.wait_ge(l_abs, GH)
            with pe.Fori(0, 2) as i:
                def attention(hh):
                    n = 2 * i + hh
                    if hh == 0:
                        pe.wait_ge(g_lo, 4 * i + 2)
                    pe.wait_ge(kd_e, n + 1)
                    for k in range(TT):
                        mm = pe.transpose(bank(1, P, k * P), SQ[:, 1, k * P:(k + 1) * P], IDENT[:])
                    mm.then_inc(kd_t, 1)
                    if hh:
                        pe.wait_ge(y_s, 4 * i + 2)
                    for k in range(TT):
                        s = slice(k * P, (k + 1) * P)
                        mm = three(bank(0, P, k * P), KIH[:, s], KIL[:, s], QDH[hh][:, s], QDL[hh][:, s], True, True)
                    mm.then_inc(at_mm, 1)

                def kv(hh):
                    pe.wait_ge(kd_lo, 2 * i + (hh + 1))
                    if hh == 0:
                        pe.wait_ge(gv_lo, 8 * i + 8)
                    for c in range(NCH - 1):
                        rows = slice(CH * (c % 2), CH * (c % 2 + 1))
                        vals = slice(hh * DV, (hh + 1) * DV)
                        mm = three(kv_bank(c), KDH[rows, c // 2, :], KDL[rows, c // 2, :],
                                   GVH[rows, c // 2, vals], GVL[rows, c // 2, vals], True, True)
                    mm.then_inc(kv_mm, 1)

                def inside(hh):
                    n = 2 * i + hh
                    pe.wait_ge(am_lo, n + 1)
                    if hh:
                        pe.wait_ge(on_done, 4 * i + 3)
                    else:
                        pe.wait_ge(y_s, 4 * i + 1)
                    for x in range(2):
                        for k in range(TT):
                            vals = slice(hh * DV + x * P, hh * DV + (x + 1) * P)
                            s = slice(k * P, (k + 1) * P)
                            three(bank(2 + x, P, k * P), GVH[:, k, vals], GVL[:, k, vals], AMH[:, s], AML[:, s], k == 0, False)

                def across(hh):
                    pe.wait_ge(st_lo, 2 * i + (hh + 1))
                    for x in range(2):
                        for c in range(1, NCH):
                            s, vals = slice(c * CH, (c + 1) * CH), slice(x * P, (x + 1) * P)
                            mm = three(bank(2 + x, CH, c * CH), SH[:, c - 1, vals], SL[:, c - 1, vals], QDH[hh][:, s], QDL[hh][:, s],
                                       False, c == NCH - 1)
                        mm.then_inc(go_mm, 1)

                def sums_out(hh):
                    for x in range(2):
                        pe.wait_ge(go_sq, 4 * i + (2 * hh + x + 1))
                        mm = pe.matmul(bank(4 if hh else 1), ONES[:], SQ[:, x, :], start=x == 0, stop=x == 1)
                    mm.then_inc(go_ss, 1)

                def out_gate(j, b):
                    pe.wait_ge(lo_done, tile_no(GK + 9, i, j, 12))
                    if j == 3:
                        pe.wait_ge(y_s, 4 * i + 3)
                    for k in range(KC):
                        mm = three(bank(b), wsl(WH, j, k), wsl(WL, j, k), UH[:, k, :], UL[:, k, :], k == 0, k == KC - 1)
                    mm.then_inc(tile_done, 1)

                for j in range(4):
                    if j == 2:
                        pe.wait_ge(on_done, 4 * i + 1)
                    product(tile_no(GK, i, j, 12), j, UH, UL)
                for hh in range(2):
                    pe.wait_ge(lo_done, tile_no(GK + 6 + 2 * hh, i, 0, 12))
                    for m in range(TT):
                        if hh:
                            pe.wait_ge(gv_lo, 8 * i + (m + 1))
                        s, tiles = slice(m * P, (m + 1) * P), slice(2 * hh, 2 * hh + 2)
                        out = bank(4 + m, DV, DV * hh).rearrange("p (a n) -> p a n", n=P)
                        for k in range(KC):
                            mm = three(out, UH[:, k, s], UL[:, k, s], WH[:, tiles, k * P:(k + 1) * P], WL[:, tiles, k * P:(k + 1) * P],
                                       k == 0, k == KC - 1)
                        mm.then_inc(tile_done if m % 2 else gv_mm, 1)
                attention(0)
                out_gate(0, 2)
                kv(0)
                inside(0)
                out_gate(1, 0)
                attention(1)
                across(0)
                kv(1)
                out_gate(2, 0)
                sums_out(0)
                out_gate(3, 0)
                inside(1)
                across(1)
                sums_out(1)
            with pe.Fori(0, 2) as i:
                for j in range(4):
                    if j == 2:
                        pe.wait_ge(on_done, 2 * GH + 1)
                    product(tile_no(GG, i, j), j, UH, UL)
            linear(BG, YH, YL, ready=y_lo)
            linear(WO, UH, UL, ready=x_lo)

            for b in range(2):
                product(FF + b, b, YH, YL, ready=norm["lo"] if b == 0 else None, before=so_far(2, "lo"))
            sums(2, 4)

            def result(half):
                pe.wait_ge(f_h, 3 * KC + 4 * (half + 1))
                for m in range(TT):
                    for c in range(4):
                        mm = pe.transpose(bank(4 * (1 - half) + m, P, c * P), HT[:, 4 * half + c, m * P:(m + 1) * P], IDENT[:])
                    mm.then_inc(out_t, 1)

            def quarter(i):
                t0 = FF + 48 * (i is None)
                for b in range(2, 8):
                    product(tile_no(t0 + (b // 4) * 4, i, b % 4, 16), b % 4, YH, YL)
                for b in range(8):
                    product(tile_no(t0 + 8 + (b // 4) * 4, i, b % 4, 16), b % 4, UH, UL, ready=f_ylo if b == 0 else None,
                            before=24 if i is None else 8 * i)
                    if i is None and b == 5:
                        result(0)
                if i is not None:
                    for b in range(2):
                        product(tile_no(t0 + 16, i, b, 16), b, YH, YL)

            with pe.Fori(0, 3) as i:
                quarter(i)
            quarter(None)

            result(1)


_INPUTS = ["x", "c", "ctx", "c_ctx", "norm_g", "w_ada", "b_ada", "mla_w_in", "mla_g_qa", "mla_w_qup", "mla_g_kva",
           "mla_w_kvup", "mla_w_out", "fno_w_in", "fno_w_out", "final_g", "norm1_g_2", "w_in_2", "moba_q_norm_g_2",
           "moba_k_norm_g_2", "t5_bias_2", "gla_gate_up_2", "gla_gate_bias_2", "gla_out_norm_g_2", "w_branch_moba_2",
           "w_branch_gla_2", "w_out_2", "norm2_g_2", "w_up_2", "w_down_2"]
_VEC_INPUTS = {"c": "c", "c_ctx": "c_ctx", "norm_g": "norm_g", "b_ada": "b_ada", "final_g": "final_g", "norm1": "norm1_g_2",
               "norm2": "norm2_g_2", "g_qa": "mla_g_qa", "g_kva": "mla_g_kva", "gate_bias": "gla_gate_bias_2",
               "out_norm": "gla_out_norm_g_2", "q_norm": "moba_q_norm_g_2", "k_norm": "moba_k_norm_g_2"}


def kernel(**inputs):
    import numpy as _np
    import concourse.bacc as _bacc
    from concourse import mybir as _mybir
    from concourse.bass_utils import run_bass_kernel_spmd as _run

    nc = _bacc.Bacc("TRN2", target_bir_lowering=False, num_devices=1)
    arrays, d = {}, {}
    vec_of = {v: k for k, v in _VEC_INPUTS.items()}
    for name in _INPUTS:
        a = _np.ascontiguousarray(inputs[name])
        key = name
        if name in vec_of:
            key = vec_of[name]
            a = a.reshape(-1, MD if key in ("q_norm", "k_norm") else P)
        elif a.ndim == 3 and a.shape[0] == 1:
            a = a[0]
        arrays[f"in_{name}"] = a
        d[key] = nc.dram_tensor(f"in_{name}", a.shape, _mybir.dt.from_np(a.dtype), kind="ExternalInput").ap()
    for name, a in shape_constants().items():
        arrays[f"const_{name}"] = a
        d[name] = nc.dram_tensor(f"const_{name}", a.shape, _mybir.dt.from_np(a.dtype), kind="ExternalInput").ap()
    d["out"] = nc.dram_tensor("out", (T, D), _mybir.dt.float32, kind="ExternalOutput").ap()
    build(nc, d)
    r = _run(nc, [arrays], core_ids=[0])
    return r.results[0]["out"].reshape(1, T, D)
```
